# Optimizing a Trainium2 kernel written in Bass

```python
import math
import jax, jax.numpy as jnp
from jax import lax
import numpy as np
import jax
import jax.numpy as jnp

D_MODEL = 1024
BATCH = 1
SEQ = 512
DEPTH = 2

GRID_W = 64
CTX_LEN = 256
N_EVEN = (DEPTH + 1) // 2
N_ODD = DEPTH // 2
RNN_WIDTH = D_MODEL // 2
LRU_HEADS = 8
LRU_HEAD_DIM = RNN_WIDTH // LRU_HEADS
LRU_CONV = 4
LRU_C = 8.0
LRU_A_MIN = 0.9
LRU_A_MAX = 0.999
HYENA_WIDTH = D_MODEL // 2
HYENA_ORDER = 2
HYENA_SHORT_CONV = 3
FILTER_EMB = 33
FILTER_HIDDEN = 64
HYENA_DECAY_TARGET = 1e-2
HYENA_FAST_PCT = 0.3
HYENA_SLOW_PCT = 1.5
HYENA_SHIFT = 0.05
IN_WIDTH = 2 * RNN_WIDTH + (HYENA_ORDER + 1) * HYENA_WIDTH
CONF_KERNEL = 31
N_EXPERTS = 16
EC_CAPACITY = 2
EXPERT_FF = 1024
N_MOD = 6
EPS = 1e-6


def _rmsnorm(x, g):
    xf = x.astype(jnp.float32)
    y = xf * lax.rsqrt(jnp.mean(xf * xf, axis=-1, keepdims=True) + EPS)
    return (y * g.astype(jnp.float32)).astype(x.dtype)

def _layernorm(x, g, b):
    xf = x.astype(jnp.float32)
    mu = jnp.mean(xf, axis=-1, keepdims=True)
    var = jnp.mean(jnp.square(xf - mu), axis=-1, keepdims=True)
    y = (xf - mu) * lax.rsqrt(var + EPS) * g.astype(jnp.float32) + b.astype(jnp.float32)
    return y.astype(x.dtype)

def _adaln(cvec, w_mod, b_mod, n_chunks):
    m = jax.nn.silu(cvec) @ w_mod[:, :n_chunks * D_MODEL] + b_mod[:n_chunks * D_MODEL]
    return [m[:, None, j * D_MODEL:(j + 1) * D_MODEL] for j in range(n_chunks)]

def _modulate(h, shift, scale):
    return h * (1 + scale) + shift

def _dwconv1d(x, w, b):
    k = w.shape[0]
    y = lax.conv_general_dilated(x, w[:, None, :], window_strides=(1,),
                                 padding=[((k - 1) // 2, k // 2)],
                                 dimension_numbers=('NWC', 'WIO', 'NWC'),
                                 feature_group_count=x.shape[-1])
    return y + b

def _dwconv_vertical(x, w, b, rows):
    bsz, n, ch = x.shape
    k = w.shape[0]
    grid = x.reshape(bsz, rows, GRID_W, ch)
    y = lax.conv_general_dilated(grid, w[:, None, None, :], window_strides=(1, 1),
                                 padding=[((k - 1) // 2, k // 2), (0, 0)],
                                 dimension_numbers=('NHWC', 'HWIO', 'NHWC'),
                                 feature_group_count=ch)
    return y.reshape(bsz, n, ch) + b

def _lin_combine(left, right):
    a_l, b_l = left
    a_r, b_r = right
    return a_l * a_r, a_r * b_l + b_r

def _rglru(xa_raw, p, h0):
    f32 = jnp.float32
    xa = _dwconv1d(xa_raw, p['conv_a_w'], p['conv_a_b'])
    bsz, n, _ = xa.shape
    xh = xa.reshape(bsz, n, LRU_HEADS, LRU_HEAD_DIM)

    def gate(w, b):
        z = jnp.einsum('bnhi,khij->kbnhj', xh, w).reshape(2, bsz, n, RNN_WIDTH)
        return jax.nn.sigmoid((z + b[:, None, None, :]).astype(f32))

    r = gate(p['lru_wr'], p['lru_br'])
    i = gate(p['lru_wi'], p['lru_bi'])
    log_a = -LRU_C * r * jax.nn.softplus(-p['lru_lam'].astype(f32))[:, None, None, :]
    a = jnp.exp(log_a)
    u = jnp.sqrt(-jnp.expm1(2.0 * log_a)) * i * xa.astype(f32)[None]
    a = jnp.stack([a[0], jnp.flip(a[1], axis=1)])
    u = jnp.stack([u[0], jnp.flip(u[1], axis=1)])
    a_cum, h = lax.associative_scan(_lin_combine, (a, u), axis=2)
    h = h + a_cum * h0[:, :, None, :]
    return h, h[:, :, -1]

def _hyena_filters_fft(n, p):
    f32 = jnp.float32
    t = jnp.linspace(0.0, 1.0, n, dtype=f32)[:, None]
    bands = (FILTER_EMB - 1) // 2
    w = (2.0 * math.pi / n) * jnp.arange(n, dtype=f32)[:, None]
    f = jnp.linspace(1e-4, bands - 1, bands, dtype=f32)[None, :]
    z = jnp.concatenate([t, jnp.cos(f * w), -jnp.sin(f * w)], axis=-1)
    freq = p['filt_freq'].astype(f32)
    hid = jnp.sin(freq[0] * (z @ p['filt_w1'].astype(f32) + p['filt_b1'].astype(f32)))
    hid = jnp.sin(freq[1] * (hid @ p['filt_w2'].astype(f32) + p['filt_b2'].astype(f32)))
    filt = (hid @ p['filt_w3'].astype(f32) + p['filt_b3'].astype(f32))
    filt = filt.reshape(n, HYENA_ORDER, 2, HYENA_WIDTH)
    deltas = jnp.abs(jnp.linspace(math.log(HYENA_DECAY_TARGET) / HYENA_SLOW_PCT,
                                  math.log(HYENA_DECAY_TARGET) / HYENA_FAST_PCT,
                                  HYENA_WIDTH, dtype=f32))
    window = jnp.exp(-t * deltas[None, :]) + HYENA_SHIFT
    filt = filt * window[:, None, None, :]
    fwd, bwd = filt[:, :, 0], filt[:, :, 1]
    kern = jnp.concatenate([fwd, jnp.zeros((1, HYENA_ORDER, HYENA_WIDTH), f32), bwd[:0:-1]], axis=0)
    return jnp.fft.rfft(kern, axis=0)

def _fftconv(u, kf, bias):
    n = u.shape[1]
    uf = u.astype(jnp.float32)
    y = jnp.fft.irfft(jnp.fft.rfft(uf, n=2 * n, axis=1) * kf[None], n=2 * n, axis=1)[:, :n]
    return (y + uf * bias.astype(jnp.float32)).astype(u.dtype)

def _even_mixer(h, p, h0):
    proj = h @ p['w_in']
    gate = proj[..., :RNN_WIDTH]
    xa_raw = proj[..., RNN_WIDTH:2 * RNN_WIDTH]
    hy = proj[..., 2 * RNN_WIDTH:]
    hs, h_last = _rglru(xa_raw, p, h0)
    y_a = jax.nn.gelu(gate) * (hs[0] + jnp.flip(hs[1], axis=1)).astype(h.dtype)
    u = _dwconv1d(hy, p['conv_b_w'], p['conv_b_b'])
    v, *gates = jnp.split(u, HYENA_ORDER + 1, axis=-1)
    kf = _hyena_filters_fft(h.shape[1], p)
    z = v
    for o in range(HYENA_ORDER):
        z = gates[o] * _fftconv(z, kf[:, o], p['filt_bias'][o])
    return jnp.concatenate([y_a, z], axis=-1) @ p['w_out'], h_last

def _conformer_conv(h, p, rows):
    u = h @ p['cf_w1'] + p['cf_b1']
    u = u[..., :D_MODEL] * jax.nn.sigmoid(u[..., D_MODEL:])
    if rows is None:
        u = _dwconv1d(u, p['cf_dw_w'], p['cf_dw_b'])
    else:
        u = _dwconv_vertical(u, p['cf_dw_w'], p['cf_dw_b'], rows)
    u = jax.nn.silu(_layernorm(u, p['cf_ln_g'], p['cf_ln_b']))
    return u @ p['cf_w2'] + p['cf_b2']

def _ec_moe(h, router, w1, w3, w2):
    bsz, n, _ = h.shape
    cap = EC_CAPACITY * n // N_EXPERTS
    probs = jax.nn.softmax(jnp.einsum('bnd,de->ben', h, router).astype(jnp.float32), axis=1)
    gates, idx = lax.top_k(probs, cap)
    bidx = jnp.arange(bsz)[:, None, None]
    xs = h[bidx, idx]
    a = jnp.einsum('becd,edf->becf', xs, w1)
    g = jnp.einsum('becd,edf->becf', xs, w3)
    y = jnp.einsum('becf,efd->becd', jax.nn.silu(a) * g, w2) * gates[..., None].astype(h.dtype)
    return jnp.zeros_like(h).at[bidx, idx].add(y)

def first_inputs(seed: int = 0) -> dict:
    key = jax.random.key(seed)
    ks = iter(jax.random.split(key, 48))
    f32 = jnp.float32
    D = D_MODEL

    def nrm(shape, scale):
        return jax.random.normal(next(ks), shape, f32) * scale

    x = nrm((BATCH, SEQ, D), 1.0)
    c = nrm((BATCH, D), 1.0)
    ctx = nrm((BATCH, CTX_LEN, D), 1.0)
    c_ctx = nrm((D,), 1.0)
    norm1_g = 1.0 + nrm((DEPTH, D), 0.1)
    norm2_g = 1.0 + nrm((DEPTH, D), 0.1)
    w_mod = nrm((DEPTH, D, N_MOD * D), 0.5 * D ** -0.5)
    b_mod = nrm((DEPTH, N_MOD * D), 0.01)
    w_in = nrm((N_EVEN, D, IN_WIDTH), D ** -0.5)
    conv_a_w = nrm((N_EVEN, LRU_CONV, RNN_WIDTH), LRU_CONV ** -0.5)
    conv_a_b = nrm((N_EVEN, RNN_WIDTH), 0.01)
    lru_wr = nrm((N_EVEN, 2, LRU_HEADS, LRU_HEAD_DIM, LRU_HEAD_DIM), LRU_HEAD_DIM ** -0.5)
    lru_br = nrm((N_EVEN, 2, RNN_WIDTH), 0.01)
    lru_wi = nrm((N_EVEN, 2, LRU_HEADS, LRU_HEAD_DIM, LRU_HEAD_DIM), LRU_HEAD_DIM ** -0.5)
    lru_bi = nrm((N_EVEN, 2, RNN_WIDTH), 0.01)
    lo, hi = LRU_A_MIN ** (1.0 / LRU_C), LRU_A_MAX ** (1.0 / LRU_C)
    ua = jax.random.uniform(next(ks), (N_EVEN, 2, RNN_WIDTH), f32, lo, hi)
    lru_lam = jnp.log(ua) - jnp.log1p(-ua)
    conv_b_w = nrm((N_EVEN, HYENA_SHORT_CONV, (HYENA_ORDER + 1) * HYENA_WIDTH), HYENA_SHORT_CONV ** -0.5)
    conv_b_b = nrm((N_EVEN, (HYENA_ORDER + 1) * HYENA_WIDTH), 0.01)
    filt_w1 = nrm((N_EVEN, FILTER_EMB, FILTER_HIDDEN), FILTER_EMB ** -0.5)
    filt_b1 = nrm((N_EVEN, FILTER_HIDDEN), 0.1)
    filt_w2 = nrm((N_EVEN, FILTER_HIDDEN, FILTER_HIDDEN), FILTER_HIDDEN ** -0.5)
    filt_b2 = nrm((N_EVEN, FILTER_HIDDEN), 0.1)
    filt_w3 = nrm((N_EVEN, FILTER_HIDDEN, HYENA_ORDER * 2 * HYENA_WIDTH), 0.1 * FILTER_HIDDEN ** -0.5)
    filt_b3 = nrm((N_EVEN, HYENA_ORDER * 2 * HYENA_WIDTH), 0.01)
    filt_freq = 1.0 + nrm((N_EVEN, 2, FILTER_HIDDEN), 0.1)
    filt_bias = nrm((N_EVEN, HYENA_ORDER, HYENA_WIDTH), 0.5)
    w_out = nrm((N_EVEN, RNN_WIDTH + HYENA_WIDTH, D), (RNN_WIDTH + HYENA_WIDTH) ** -0.5)
    cf_w1 = nrm((N_ODD, D, 2 * D), D ** -0.5)
    cf_b1 = nrm((N_ODD, 2 * D), 0.01)
    cf_dw_w = nrm((N_ODD, CONF_KERNEL, D), CONF_KERNEL ** -0.5)
    cf_dw_b = nrm((N_ODD, D), 0.01)
    cf_ln_g = 1.0 + nrm((N_ODD, D), 0.1)
    cf_ln_b = nrm((N_ODD, D), 0.01)
    cf_w2 = nrm((N_ODD, D, D), D ** -0.5)
    cf_b2 = nrm((N_ODD, D), 0.01)
    router = nrm((DEPTH, D, N_EXPERTS), D ** -0.5)
    exp_w1 = nrm((DEPTH, N_EXPERTS, D, EXPERT_FF), D ** -0.5)
    exp_w3 = nrm((DEPTH, N_EXPERTS, D, EXPERT_FF), D ** -0.5)
    exp_w2 = nrm((DEPTH, N_EXPERTS, EXPERT_FF, D), EXPERT_FF ** -0.5)
    final_g = 1.0 + nrm((D,), 0.1)
    return {"x": x, "c": c, "ctx": ctx, "c_ctx": c_ctx,
            "norm1_g": norm1_g, "norm2_g": norm2_g, "w_mod": w_mod, "b_mod": b_mod,
            "w_in": w_in, "conv_a_w": conv_a_w, "conv_a_b": conv_a_b,
            "lru_wr": lru_wr, "lru_br": lru_br, "lru_wi": lru_wi, "lru_bi": lru_bi, "lru_lam": lru_lam,
            "conv_b_w": conv_b_w, "conv_b_b": conv_b_b,
            "filt_w1": filt_w1, "filt_b1": filt_b1, "filt_w2": filt_w2, "filt_b2": filt_b2,
            "filt_w3": filt_w3, "filt_b3": filt_b3, "filt_freq": filt_freq, "filt_bias": filt_bias,
            "w_out": w_out,
            "cf_w1": cf_w1, "cf_b1": cf_b1, "cf_dw_w": cf_dw_w, "cf_dw_b": cf_dw_b,
            "cf_ln_g": cf_ln_g, "cf_ln_b": cf_ln_b, "cf_w2": cf_w2, "cf_b2": cf_b2,
            "router": router, "exp_w1": exp_w1, "exp_w3": exp_w3, "exp_w2": exp_w2,
            "final_g": final_g}

def first_block(x, c, ctx, c_ctx, norm1_g, norm2_g, w_mod, b_mod,
              w_in, conv_a_w, conv_a_b, lru_wr, lru_br, lru_wi, lru_bi, lru_lam,
              conv_b_w, conv_b_b, filt_w1, filt_b1, filt_w2, filt_b2, filt_w3, filt_b3,
              filt_freq, filt_bias, w_out,
              cf_w1, cf_b1, cf_dw_w, cf_dw_b, cf_ln_g, cf_ln_b, cf_w2, cf_b2,
              router, exp_w1, exp_w3, exp_w2, final_g):
    n_lat = x.shape[1]
    rows = n_lat // GRID_W
    last_ctx_layer = ((DEPTH - 1) // 2) * 2
    xl, xc = x, ctx
    for l in range(DEPTH):
        carry_ctx = l < last_ctx_layer
        sh1, sc1, g1, sh2, sc2, g2 = _adaln(c, w_mod[l], b_mod[l], N_MOD)
        hl = _modulate(_rmsnorm(xl, norm1_g[l]), sh1, sc1)
        if l % 2 == 0 or carry_ctx:
            cm = _adaln(c_ctx[None], w_mod[l], b_mod[l], N_MOD if carry_ctx else 2)
            hc = _modulate(_rmsnorm(xc, norm1_g[l]), cm[0], cm[1])
        if l % 2 == 0:
            e = l // 2
            pe = {'w_in': w_in[e], 'conv_a_w': conv_a_w[e], 'conv_a_b': conv_a_b[e],
                  'lru_wr': lru_wr[e], 'lru_br': lru_br[e], 'lru_wi': lru_wi[e], 'lru_bi': lru_bi[e],
                  'lru_lam': lru_lam[e], 'conv_b_w': conv_b_w[e], 'conv_b_b': conv_b_b[e],
                  'filt_w1': filt_w1[e], 'filt_b1': filt_b1[e], 'filt_w2': filt_w2[e],
                  'filt_b2': filt_b2[e], 'filt_w3': filt_w3[e], 'filt_b3': filt_b3[e],
                  'filt_freq': filt_freq[e], 'filt_bias': filt_bias[e], 'w_out': w_out[e]}
            h0_ctx = jnp.zeros((2, xc.shape[0], RNN_WIDTH), jnp.float32)
            if carry_ctx:
                yc, ctx_state = _even_mixer(hc, pe, h0_ctx)
            else:
                _, ctx_state = _rglru(hc @ pe['w_in'][:, RNN_WIDTH:2 * RNN_WIDTH], pe, h0_ctx)
            yl, _ = _even_mixer(hl, pe, ctx_state)
        else:
            o = l // 2
            po = {'cf_w1': cf_w1[o], 'cf_b1': cf_b1[o], 'cf_dw_w': cf_dw_w[o], 'cf_dw_b': cf_dw_b[o],
                  'cf_ln_g': cf_ln_g[o], 'cf_ln_b': cf_ln_b[o], 'cf_w2': cf_w2[o], 'cf_b2': cf_b2[o]}
            yl = _conformer_conv(hl, po, rows)
            if carry_ctx:
                yc = _conformer_conv(hc, po, None)
        xl = xl + g1 * yl
        xl = xl + g2 * _ec_moe(_modulate(_rmsnorm(xl, norm2_g[l]), sh2, sc2),
                               router[l], exp_w1[l], exp_w3[l], exp_w2[l])
        if carry_ctx:
            xc = xc + cm[2] * yc
            xc = xc + cm[5] * _ec_moe(_modulate(_rmsnorm(xc, norm2_g[l]), cm[3], cm[4]),
                                      router[l], exp_w1[l], exp_w3[l], exp_w2[l])
    return _rmsnorm(xl, final_g)


DEPTH_2 = 1

N_MIXERS = 4
MIX_WIDTH = 256
HEAD_DIM = 64
N_HEADS = 4
NORM_EPS = 1e-6
NEG_INF = -1e30

GDN_CONV = 4
GDN_CHUNK = 64

SG_CHUNK = 128
SG_GROUPS = 4
SG_GROUP_DIM = MIX_WIDTH // SG_GROUPS

RWKV_DECAY_RANK = 64
RWKV_A_RANK = 64
RWKV_GN_EPS = 64e-5
RW_WIDTH = 3 * MIX_WIDTH + RWKV_DECAY_RANK + RWKV_A_RANK

NSA_KV_DIM = HEAD_DIM
NSA_CMP_LEN = 32
NSA_CMP_STRIDE = 16
NSA_CMP_RATIO = NSA_CMP_LEN // NSA_CMP_STRIDE
NSA_CMP_HIDDEN = 64
NSA_SEL_BLOCK = 64
NSA_N_SEL = 8
NSA_FORCE_BONUS = 1e4
NSA_WINDOW = 256
NSA_Q_BLOCK = 128
NSA_SEL_Q_BLOCK = 64

IN_SPLITS = (
    3 * MIX_WIDTH,
    N_HEADS,
    N_HEADS,
    MIX_WIDTH,
    MIX_WIDTH,
    MIX_WIDTH,
    MIX_WIDTH,
    RW_WIDTH,
    MIX_WIDTH,
    MIX_WIDTH,
    6 * NSA_KV_DIM,
    3 * N_HEADS,
    MIX_WIDTH,
    N_MIXERS * D_MODEL,
)
IN_OFFSETS = tuple(sum(IN_SPLITS[: i + 1]) for i in range(len(IN_SPLITS) - 1))
D_IN = sum(IN_SPLITS)
ALIBI_SLOPES = tuple(2.0 ** (-8.0 * (h + 1) / N_HEADS) for h in range(N_HEADS))


def rmsnorm(x, gain, eps=NORM_EPS):
    x32 = x.astype(jnp.float32)
    y = x32 * lax.rsqrt(jnp.mean(x32 * x32, axis=-1, keepdims=True) + eps)
    return (y * gain.astype(jnp.float32)).astype(x.dtype)

def layernorm(x, gain, bias, eps):
    x32 = x.astype(jnp.float32)
    xc = x32 - jnp.mean(x32, axis=-1, keepdims=True)
    y = xc * lax.rsqrt(jnp.mean(xc * xc, axis=-1, keepdims=True) + eps)
    return (y * gain.astype(jnp.float32) + bias.astype(jnp.float32)).astype(x.dtype)

def l2norm(x, eps=1e-6):
    x32 = x.astype(jnp.float32)
    return (x32 * lax.rsqrt(jnp.sum(x32 * x32, axis=-1, keepdims=True) + eps)).astype(x.dtype)

def shift_prev(x):
    return jnp.pad(x, ((0, 0), (1, 0), (0, 0)))[:, :-1]

def causal_depthwise_conv(x, w):
    width, ch = w.shape
    return lax.conv_general_dilated(
        x, w[:, None, :].astype(x.dtype), window_strides=(1,),
        padding=((width - 1, 0),), dimension_numbers=('NWC', 'WIO', 'NWC'),
        feature_group_count=ch)

def masked_softmax(s, mask):
    p = jax.nn.softmax(jnp.where(mask, s, NEG_INF), axis=-1)
    return jnp.where(mask, p, 0.0)

def chunked_gated_delta_rule(q, k, v, g, beta):
    B, T, H, E = q.shape
    C = GDN_CHUNK
    N = T // C

    def chunks(t):
        t = t.reshape((B, N, C, H) + t.shape[3:])
        return jnp.moveaxis(t, (1, 3), (0, 2))

    q, k, v, g, beta = (chunks(t) for t in (q, k, v, g, beta))
    gc = jnp.cumsum(g, axis=-1)
    pos = jnp.arange(C)
    causal = pos[:, None] >= pos[None, :]
    strict = pos[:, None] > pos[None, :]
    decay = jnp.where(causal, jnp.exp(jnp.where(causal, gc[..., :, None] - gc[..., None, :], 0.0)), 0.0)
    kb = k * beta[..., None]
    a_mat = jnp.where(strict, jnp.einsum('nbhcd,nbhed->nbhce', kb, k) * decay, 0.0)
    eye = jnp.eye(C, dtype=q.dtype)
    t_inv = lax.linalg.triangular_solve(eye + a_mat, jnp.broadcast_to(eye, a_mat.shape),
                                        left_side=True, lower=True, unit_diagonal=True)
    u = t_inv @ (v * beta[..., None])
    w = t_inv @ (kb * jnp.exp(gc)[..., None])
    attn = jnp.einsum('nbhcd,nbhed->nbhce', q, k) * decay
    g_last = gc[..., -1]
    q_in = q * jnp.exp(gc)[..., None]
    k_out = k * jnp.exp(g_last[..., None] - gc)[..., None]

    def step(state, xs):
        u_n, w_n, attn_n, q_n, k_n, gl_n = xs
        v_new = u_n - w_n @ state
        o_n = q_n @ state + attn_n @ v_new
        state = state * jnp.exp(gl_n)[..., None, None] + jnp.swapaxes(k_n, -1, -2) @ v_new
        return state, o_n

    state0 = jnp.zeros((B, H, E, v.shape[-1]), q.dtype)
    _, o = lax.scan(step, state0, (u, w, attn, q_in, k_out, g_last))
    return jnp.moveaxis(o, (0, 2), (1, 3)).reshape(B, T, H, -1)

def gated_deltanet(qkv, a_logit, b_logit, z, conv_w, a_log, dt_bias, norm_w):
    B, T, _ = qkv.shape
    f32 = jnp.float32
    qkv = jax.nn.silu(causal_depthwise_conv(qkv, conv_w))
    q, k, v = jnp.split(qkv, 3, axis=-1)
    heads = lambda t: t.reshape(B, T, N_HEADS, HEAD_DIM).astype(f32)
    q = l2norm(heads(q)) * (HEAD_DIM ** -0.5)
    k = l2norm(heads(k))
    v = heads(v)
    beta = jax.nn.sigmoid(b_logit.astype(f32))
    g = -jnp.exp(a_log.astype(f32)) * jax.nn.softplus(a_logit.astype(f32) + dt_bias.astype(f32))
    o = chunked_gated_delta_rule(q, k, v, g, beta)
    o = rmsnorm(o, norm_w) * jax.nn.silu(heads(z))
    return o.reshape(B, T, MIX_WIDTH).astype(qkv.dtype)

def spatial_gating(u, v, z, ln_gain, ln_bias, w_s, b_s):
    B, T, _ = u.shape
    u = jax.nn.gelu(u)
    v = jax.nn.gelu(v).reshape(B, T, SG_GROUPS, SG_GROUP_DIM)
    v = layernorm(v, ln_gain.reshape(SG_GROUPS, SG_GROUP_DIM), ln_bias.reshape(SG_GROUPS, SG_GROUP_DIM), 1e-5)
    v = v.reshape(B, T // SG_CHUNK, SG_CHUNK, SG_GROUPS, SG_GROUP_DIM)
    tril = jnp.tril(jnp.ones((SG_CHUNK, SG_CHUNK), dtype=bool))
    w_c = jnp.where(tril, w_s, 0.0).astype(v.dtype)
    mixed = jnp.einsum('gts,bnsgc->bntgc', w_c, v) + b_s.T[:, :, None].astype(v.dtype)
    s = u * mixed.reshape(B, T, MIX_WIDTH)
    return s * jax.nn.silu(z)

def rwkv7_scan(r, w, k, v, kk, a):
    def step(S, xs):
        r_t, w_t, k_t, v_t, kk_t, a_t = xs
        sa = jnp.einsum('bhvk,bhk->bhv', S, -kk_t)
        S = (S * w_t[:, :, None, :] + sa[..., None] * (kk_t * a_t)[:, :, None, :]
             + v_t[..., None] * k_t[:, :, None, :])
        return S, jnp.einsum('bhvk,bhk->bhv', S, r_t)

    B, T, H, E = r.shape
    xs = tuple(jnp.moveaxis(t, 1, 0) for t in (r, w, k, v, kk, a))
    _, o = lax.scan(step, jnp.zeros((B, H, E, E), jnp.float32), xs)
    return jnp.moveaxis(o, 0, 1)

def rwkv7_time_mix(rw, z, mu, w_up, w0, a_up, a0, k_k, k_a, r_k, gn_gain, gn_bias):
    B, T, _ = rw.shape
    f32 = jnp.float32
    rw = (rw + mu * (shift_prev(rw) - rw)).astype(f32)
    r, k, v, wd, ad = jnp.split(
        rw, (MIX_WIDTH, 2 * MIX_WIDTH, 3 * MIX_WIDTH, 3 * MIX_WIDTH + RWKV_DECAY_RANK), axis=-1)
    w_log = -jax.nn.softplus(-(w0.astype(f32) + jnp.tanh(wd) @ w_up.astype(f32))) - 0.5
    decay = jnp.exp(-jnp.exp(w_log))
    a = jax.nn.sigmoid(a0.astype(f32) + ad @ a_up.astype(f32))
    heads = lambda t: t.reshape(B, T, N_HEADS, HEAD_DIM)
    kk = l2norm(heads(k * k_k.astype(f32)))
    k = k * (1.0 + (a - 1.0) * k_a.astype(f32))
    r_h, k_h, v_h = heads(r), heads(k), heads(v)
    o = rwkv7_scan(r_h, heads(decay), k_h, v_h, kk, heads(a))
    o = layernorm(o, gn_gain.reshape(N_HEADS, HEAD_DIM), gn_bias.reshape(N_HEADS, HEAD_DIM), RWKV_GN_EPS)
    o = o + jnp.sum(r_h * k_h * r_k.astype(f32), axis=-1, keepdims=True) * v_h
    return (o.reshape(B, T, MIX_WIDTH) * jax.nn.silu(z.astype(f32))).astype(z.dtype)

def compress_blocks(x, pos_emb, w1, w2):
    B, T, E = x.shape
    ns = T // NSA_CMP_STRIDE
    nc = ns - NSA_CMP_RATIO + 1
    c = x.reshape(B, ns, NSA_CMP_STRIDE, E)
    blocks = jnp.concatenate([c[:, j:j + nc] for j in range(NSA_CMP_RATIO)], axis=2)
    blocks = (blocks + pos_emb.astype(x.dtype)).reshape(B, nc, NSA_CMP_LEN * E)
    return jax.nn.gelu(blocks @ w1) @ w2

def nsa_compressed(q, k, v, pos_emb, w1, w2, slopes):
    B, T, H, E = q.shape
    kc = compress_blocks(k, pos_emb[0], w1[0], w2[0])
    vc = compress_blocks(v, pos_emb[1], w1[1], w2[1])
    nc = kc.shape[1]
    end = jnp.arange(nc) * NSA_CMP_STRIDE + NSA_CMP_LEN - 1
    dist = (jnp.arange(T)[:, None] - end[None, :]).astype(jnp.float32)
    s = (jnp.einsum('bthd,bnd->bhtn', q, kc).astype(jnp.float32) * (E ** -0.5)
         - slopes[:, None, None] * dist)
    p = masked_softmax(s, dist >= 0)
    return jnp.einsum('bhtn,bnd->bthd', p.astype(q.dtype), vc), p

def nsa_selected(q, k, v, p_cmp, slopes):
    B, T, H, E = q.shape
    nc = p_cmp.shape[-1]
    nsb = T // NSA_SEL_BLOCK
    n_sel = min(NSA_N_SEL, nsb)
    cs = np.arange(nc) * NSA_CMP_STRIDE
    bs = np.arange(nsb) * NSA_SEL_BLOCK
    inter = np.clip(np.minimum(cs[:, None] + NSA_CMP_LEN, bs[None, :] + NSA_SEL_BLOCK)
                    - np.maximum(cs[:, None], bs[None, :]), 0, None).astype(np.float32) / NSA_CMP_LEN
    imp = jnp.einsum('bhtn,nj->btj', p_cmp, jnp.asarray(inter))
    cur = jnp.arange(T)[:, None] // NSA_SEL_BLOCK
    blk = jnp.arange(nsb)[None, :]
    forced = (blk == 0) | (blk == cur) | (blk == cur - 1)
    score = jnp.where(blk <= cur, imp + jnp.where(forced, NSA_FORCE_BONUS, 0.0), NEG_INF)
    _, idx = lax.top_k(score, n_sel)

    kb = k.reshape(B, nsb, NSA_SEL_BLOCK, E)
    vb = v.reshape(B, nsb, NSA_SEL_BLOCK, E)
    QB = NSA_SEL_Q_BLOCK
    nqb = T // QB
    qs = jnp.moveaxis(q.reshape(B, nqb, QB, H, E), 1, 0)
    idxs = jnp.moveaxis(idx.reshape(B, nqb, QB, n_sel), 1, 0)
    t0s = jnp.arange(nqb) * QB
    bidx = jnp.arange(B)[:, None, None]

    def one_block(args):
        q_blk, idx_blk, t0 = args
        kg = kb[bidx, idx_blk]
        vg = vb[bidx, idx_blk]
        tq = t0 + jnp.arange(QB)
        pos = idx_blk[..., None] * NSA_SEL_BLOCK + jnp.arange(NSA_SEL_BLOCK)
        dist = (tq[None, :, None, None] - pos).astype(jnp.float32)[:, :, None]
        s = (jnp.einsum('bqhd,bqnsd->bqhns', q_blk, kg).astype(jnp.float32) * (E ** -0.5)
             - slopes[None, None, :, None, None] * dist)
        mask = jnp.broadcast_to(dist >= 0, s.shape)
        p = masked_softmax(s.reshape(B, QB, H, -1), mask.reshape(B, QB, H, -1)).reshape(s.shape)
        return jnp.einsum('bqhns,bqnsd->bqhd', p.astype(q_blk.dtype), vg)

    o = lax.map(one_block, (qs, idxs, t0s))
    return jnp.moveaxis(o, 0, 1).reshape(B, T, H, E)

def nsa_window(q, k, v, slopes):
    B, T, H, E = q.shape
    QB = NSA_Q_BLOCK
    nb = T // QB
    nprev = NSA_WINDOW // QB

    def band(t):
        tb = jnp.pad(t.reshape(B, nb, QB, E), ((0, 0), (nprev, 0), (0, 0), (0, 0)))
        return jnp.concatenate([tb[:, j:j + nb] for j in range(nprev + 1)], axis=2)

    kband, vband = band(k), band(v)
    qb = q.reshape(B, nb, QB, H, E)
    tq = jnp.arange(nb)[:, None] * QB + jnp.arange(QB)
    pos = jnp.arange(nb)[:, None] * QB - nprev * QB + jnp.arange((nprev + 1) * QB)
    dist = tq[:, :, None] - pos[:, None, :]
    mask = (dist >= 0) & (dist < NSA_WINDOW) & (pos[:, None, :] >= 0)
    s = (jnp.einsum('bnqhd,bnkd->bnhqk', qb, kband).astype(jnp.float32) * (E ** -0.5)
         - slopes[None, None, :, None, None] * dist.astype(jnp.float32)[None, :, None])
    p = masked_softmax(s, mask[None, :, None])
    o = jnp.einsum('bnhqk,bnkd->bnqhd', p.astype(q.dtype), vband)
    return o.reshape(B, T, H, E)

def native_sparse_attention(q, kv, gate_logit, z, cmp_pos, cmp_w1, cmp_w2):
    B, T, _ = q.shape
    q = q.reshape(B, T, N_HEADS, HEAD_DIM)
    k_c, v_c, k_s, v_s, k_w, v_w = jnp.split(kv, 6, axis=-1)
    slopes = jnp.asarray(ALIBI_SLOPES, jnp.float32)
    o_cmp, p_cmp = nsa_compressed(q, k_c, v_c, cmp_pos, cmp_w1, cmp_w2, slopes)
    o_sel = nsa_selected(q, k_s, v_s, p_cmp, slopes)
    o_win = nsa_window(q, k_w, v_w, slopes)
    g = jax.nn.sigmoid(gate_logit.reshape(B, T, N_HEADS, 3))
    o = g[..., 0:1] * o_cmp + g[..., 1:2] * o_sel + g[..., 2:3] * o_win
    return o.reshape(B, T, MIX_WIDTH) * jax.nn.silu(z)

def hybrid_layer(x, norm_gain, w_in, gdn_conv, gdn_a_log, gdn_dt_bias, gdn_norm,
                 sg_ln_gain, sg_ln_bias, sg_w_s, sg_b_s,
                 rw_mu, rw_w_up, rw_w0, rw_a_up, rw_a0, rw_k_k, rw_k_a, rw_r_k, rw_gn_gain, rw_gn_bias,
                 nsa_cmp_pos, nsa_cmp_w1, nsa_cmp_w2, w_branch, w_out):
    h = rmsnorm(x, norm_gain)
    proj = h @ w_in
    (gdn_qkv, gdn_a, gdn_b, gdn_z, sg_u, sg_v, sg_z, rw, rw_z,
     nsa_q, nsa_kv, nsa_g, nsa_z, merge) = jnp.split(proj, IN_OFFSETS, axis=-1)
    ys = (
        gated_deltanet(gdn_qkv, gdn_a, gdn_b, gdn_z, gdn_conv, gdn_a_log, gdn_dt_bias, gdn_norm),
        spatial_gating(sg_u, sg_v, sg_z, sg_ln_gain, sg_ln_bias, sg_w_s, sg_b_s),
        rwkv7_time_mix(rw, rw_z, rw_mu, rw_w_up, rw_w0, rw_a_up, rw_a0, rw_k_k, rw_k_a, rw_r_k,
                       rw_gn_gain, rw_gn_bias),
        native_sparse_attention(nsa_q, nsa_kv, nsa_g, nsa_z, nsa_cmp_pos, nsa_cmp_w1, nsa_cmp_w2),
    )
    gates = jnp.split(jax.nn.sigmoid(merge), N_MIXERS, axis=-1)
    mixed = gates[0] * (ys[0] @ w_branch[0])
    for i in range(1, N_MIXERS):
        mixed = mixed + gates[i] * (ys[i] @ w_branch[i])
    return x + mixed @ w_out

def second_inputs(seed: int = 0) -> dict:
    key = jax.random.key(seed)
    ks = jax.random.split(key, 32)
    f32 = jnp.float32
    L, D, W, H, E = DEPTH_2, D_MODEL, MIX_WIDTH, N_HEADS, HEAD_DIM
    nrm = lambda k, shape, scale: scale * jax.random.normal(k, shape, f32)
    dt = jnp.exp(jax.random.uniform(ks[5], (L, H), f32, math.log(1e-3), math.log(1e-1)))
    return {
        'x': nrm(ks[0], (BATCH, SEQ, D), 1.0),
        'norm_gain': 1.0 + nrm(ks[1], (L, D), 0.1),
        'w_in': nrm(ks[2], (L, D, D_IN), D ** -0.5),
        'gdn_conv': nrm(ks[3], (L, GDN_CONV, 3 * W), 0.5),
        'gdn_a_log': jnp.log(jax.random.uniform(ks[4], (L, H), f32, 1.0, 16.0)),
        'gdn_dt_bias': jnp.log(jnp.expm1(dt)),
        'gdn_norm': 1.0 + nrm(ks[6], (L, E), 0.1),
        'sg_ln_gain': 1.0 + nrm(ks[7], (L, W), 0.1),
        'sg_ln_bias': nrm(ks[8], (L, W), 0.02),
        'sg_w_s': nrm(ks[9], (L, SG_GROUPS, SG_CHUNK, SG_CHUNK), SG_CHUNK ** -0.5),
        'sg_b_s': 1.0 + nrm(ks[10], (L, SG_GROUPS, SG_CHUNK), 0.1),
        'rw_mu': jax.random.uniform(ks[11], (L, RW_WIDTH), f32, 0.0, 1.0),
        'rw_w_up': nrm(ks[12], (L, RWKV_DECAY_RANK, W), 0.1),
        'rw_w0': jax.random.uniform(ks[13], (L, W), f32, -6.0, -1.0),
        'rw_a_up': nrm(ks[14], (L, RWKV_A_RANK, W), 0.1),
        'rw_a0': nrm(ks[15], (L, W), 0.1),
        'rw_k_k': 0.85 + nrm(ks[16], (L, W), 0.05),
        'rw_k_a': 1.0 + nrm(ks[17], (L, W), 0.05),
        'rw_r_k': nrm(ks[18], (L, H, E), 0.1),
        'rw_gn_gain': 1.0 + nrm(ks[19], (L, W), 0.1),
        'rw_gn_bias': nrm(ks[20], (L, W), 0.02),
        'nsa_cmp_pos': nrm(ks[21], (L, 2, NSA_CMP_LEN, NSA_KV_DIM), 0.1),
        'nsa_cmp_w1': nrm(ks[22], (L, 2, NSA_CMP_LEN * NSA_KV_DIM, NSA_CMP_HIDDEN), (NSA_CMP_LEN * NSA_KV_DIM) ** -0.5),
        'nsa_cmp_w2': nrm(ks[23], (L, 2, NSA_CMP_HIDDEN, NSA_KV_DIM), NSA_CMP_HIDDEN ** -0.5),
        'w_branch': nrm(ks[24], (L, N_MIXERS, W, D), W ** -0.5),
        'w_out': nrm(ks[25], (L, D, D), D ** -0.5),
        'final_gain': 1.0 + nrm(ks[26], (D,), 0.1),
    }

def second_block(x, norm_gain, w_in, gdn_conv, gdn_a_log, gdn_dt_bias, gdn_norm,
              sg_ln_gain, sg_ln_bias, sg_w_s, sg_b_s,
              rw_mu, rw_w_up, rw_w0, rw_a_up, rw_a0, rw_k_k, rw_k_a, rw_r_k, rw_gn_gain, rw_gn_bias,
              nsa_cmp_pos, nsa_cmp_w1, nsa_cmp_w2, w_branch, w_out, final_gain):
    for l in range(DEPTH_2):
        x = hybrid_layer(
            x, norm_gain[l], w_in[l], gdn_conv[l], gdn_a_log[l], gdn_dt_bias[l], gdn_norm[l],
            sg_ln_gain[l], sg_ln_bias[l], sg_w_s[l], sg_b_s[l],
            rw_mu[l], rw_w_up[l], rw_w0[l], rw_a_up[l], rw_a0[l], rw_k_k[l], rw_k_a[l], rw_r_k[l],
            rw_gn_gain[l], rw_gn_bias[l],
            nsa_cmp_pos[l], nsa_cmp_w1[l], nsa_cmp_w2[l], w_branch[l], w_out[l])
    return rmsnorm(x, final_gain)


def setup_inputs(seed=0):
    out = dict(first_inputs(seed))
    for name, value in second_inputs(seed + 1).items():
        if name != "x":
            out[name + "_2"] = value
    return out


def reference(
    x, c, ctx, c_ctx, norm1_g, norm2_g, w_mod, b_mod, w_in, conv_a_w, conv_a_b, lru_wr, lru_br,
    lru_wi, lru_bi, lru_lam, conv_b_w, conv_b_b, filt_w1, filt_b1, filt_w2, filt_b2, filt_w3,
    filt_b3, filt_freq, filt_bias, w_out, cf_w1, cf_b1, cf_dw_w, cf_dw_b, cf_ln_g, cf_ln_b,
    cf_w2, cf_b2, router, exp_w1, exp_w3, exp_w2, final_g, norm_gain_2, w_in_2, gdn_conv_2,
    gdn_a_log_2, gdn_dt_bias_2, gdn_norm_2, sg_ln_gain_2, sg_ln_bias_2, sg_w_s_2, sg_b_s_2,
    rw_mu_2, rw_w_up_2, rw_w0_2, rw_a_up_2, rw_a0_2, rw_k_k_2, rw_k_a_2, rw_r_k_2, rw_gn_gain_2,
    rw_gn_bias_2, nsa_cmp_pos_2, nsa_cmp_w1_2, nsa_cmp_w2_2, w_branch_2, w_out_2, final_gain_2,
):
    x = first_block(
        x, c, ctx, c_ctx, norm1_g, norm2_g, w_mod, b_mod, w_in, conv_a_w, conv_a_b, lru_wr,
        lru_br, lru_wi, lru_bi, lru_lam, conv_b_w, conv_b_b, filt_w1, filt_b1, filt_w2, filt_b2,
        filt_w3, filt_b3, filt_freq, filt_bias, w_out, cf_w1, cf_b1, cf_dw_w, cf_dw_b, cf_ln_g,
        cf_ln_b, cf_w2, cf_b2, router, exp_w1, exp_w3, exp_w2, final_g,
    )
    return second_block(
        x, norm_gain_2, w_in_2, gdn_conv_2, gdn_a_log_2, gdn_dt_bias_2, gdn_norm_2,
        sg_ln_gain_2, sg_ln_bias_2, sg_w_s_2, sg_b_s_2, rw_mu_2, rw_w_up_2, rw_w0_2, rw_a_up_2,
        rw_a0_2, rw_k_k_2, rw_k_a_2, rw_r_k_2, rw_gn_gain_2, rw_gn_bias_2, nsa_cmp_pos_2,
        nsa_cmp_w1_2, nsa_cmp_w2_2, w_branch_2, w_out_2, final_gain_2,
    )


_drawn_inputs = setup_inputs


def setup_inputs(seed=0):
    import zlib

    import numpy as np

    out = dict(_drawn_inputs(seed))
    spreads = {}
    factors = {'conv_a_b': 2.772,
     'lru_br': 51.932,
     'lru_bi': 27.395,
     'conv_b_b': 6.671,
     'filt_freq': 2.904,
     'cf_b1': 8.0,
     'cf_dw_b': 7.293,
     'cf_ln_b': 8.0,
     'cf_b2': 8.0,
     'sg_ln_gain_2': 4.685,
     'sg_ln_bias_2': 32.819,
     'sg_b_s_2': 3.004,
     'rw_w_up_2': 3.293,
     'rw_a0_2': 5.545,
     'rw_k_k_2': 136.26,
     'rw_k_a_2': 3.283,
     'rw_gn_bias_2': 8.0,
     'nsa_cmp_pos_2': 4.99,
     'gdn_norm_2': 2.736,
     'rw_gn_gain_2': 2.978}
    for name, (base, spread) in spreads.items():
        noise = np.random.default_rng([zlib.crc32(name.encode()), seed]).standard_normal(out[name].shape)
        drawn = base * np.exp(spread * noise) if base else spread * noise
        out[name] = jnp.asarray(drawn.astype(out[name].dtype))
    for name, factor in factors.items():
        out[name] = (out[name] * factor).astype(out[name].dtype)
    return out
```

```python
import math
from contextlib import ExitStack, contextmanager

import numpy as np

import concourse.bass as bass
from concourse import mybir

F32 = mybir.dt.float32
ALU = mybir.AluOpType
ACT = mybir.ActivationFunctionType
AXX = mybir.AxisListType.X

P = 128
T = 512
D = 1024
KD = D // P
NT = T // P
TC = 256
NE = 16
CAP = 2 * T // NE
FF = 1024
RW = 512
KR = RW // P
HD = 64
CH = 64
NCH = T // CH
LRU_C = 8.0
EPS = 1e-6
GRID_W = 64
CF_K = 31
NMOD = 6
FEMB, FHID = 33, 64
BIG = 1e30
NCMP = T // 16 - 1
SLOPES = [2.0 ** (-8.0 * (h + 1) / 4) for h in range(4)]
NRING = 12
LEVELS = 6

VEC = [("norm1_g", 16), ("norm2_g", 16), ("b_mod", 96), ("conv_a_w", 16), ("conv_a_b", 4),
       ("lru_br", 8), ("lru_bi", 8), ("lru_lam", 8), ("conv_b_w", 36), ("conv_b_b", 12),
       ("filt_bias", 8), ("cf_b1", 16), ("cf_dw_w", CF_K * 8), ("cf_dw_b", 8), ("cf_ln_g", 8),
       ("cf_ln_b", 8), ("cf_b2", 8), ("final_g", 8), ("norm_gain_2", 8), ("gdn_conv_2", 24),
       ("sg_ln_gain_2", 2), ("sg_ln_bias_2", 2), ("rw_mu_2", 7), ("rw_w0_2", 2), ("rw_a0_2", 2),
       ("rw_k_k_2", 2), ("rw_k_a_2", 2), ("rw_r_k_2", 2), ("rw_gn_gain_2", 2), ("rw_gn_bias_2", 2),
       ("final_gain_2", 8), ("c", 8), ("c_ctx", 8),
       ("gdn_norm_2", 1), ("filt_b1", 1), ("filt_b2", 1), ("filt_freq0", 1), ("filt_freq1", 1),
       ("gdn_a_log_2", 1), ("gdn_dt_bias_2", 1)]
VOFF, _n = {}, 0
for _name, _w in VEC:
    VOFF[_name] = _n
    _n += _w
NVEC = _n

CONST = [("ident", 128), ("ones", 128), ("blk1", 128), ("i64", 64), ("strict", 64), ("incl", 64),
         ("level", LEVELS * 64), ("eye64", 512), ("reset", 512), ("sela", 256), ("selb", 256),
         ("iota", 128), ("dist", 512), ("distw", 384), ("cdist", 4 * 32), ("cmask", 4 * 32),
         ("tril", 128), ("pi", 1)]
COFF, _n = {}, 0
for _name, _w in CONST:
    COFF[_name] = _n
    _n += _w
NCONST = _n


def shape_constants():
    c = np.zeros((P, NCONST), np.float32)
    p = np.arange(P)[:, None]

    def put(name, a):
        c[:a.shape[0], COFF[name]:COFF[name] + a.shape[1]] = a

    t64 = np.arange(64)[None, :]
    put("ident", np.eye(P))
    put("ones", np.ones((P, P)))
    put("blk1", (p // 64 == np.arange(P)[None, :] // 64) * 1.0)
    put("i64", (p % 64 == t64) * 1.0)
    put("strict", (p % 64 < t64) * 1.0)
    put("incl", (p % 64 <= t64) * 1.0)
    put("level", np.concatenate([((t64 // b) % 2 == 1) * ((p % 64) // b == t64 // b - 1) * 1.0
                                 for b in (1 << i for i in range(LEVELS))], 1))
    put("eye64", np.tile((p % 64 == t64) * 1.0, (1, 8)))
    put("reset", np.tile((np.arange(T) % CH != 0)[None, :] * 1.0, (P, 1)))
    sel = np.zeros((4, 2, P))
    for h in range(4):
        sel[h, h // 2, 64 * (h % 2):64 * (h % 2) + 64] = 1.0
    put("sela", sel.reshape(4, 256))
    c[32:36, COFF["selb"]:COFF["selb"] + 256] = sel.reshape(4, 256)
    put("iota", np.tile(np.arange(P)[None, :] % 64, (P, 1)))
    m = np.arange(512)[None, :]
    d = p + 384 - m
    put("dist", np.where(d >= 0, d, BIG))
    m = np.arange(384)[None, :]
    d = p + 256 - m
    put("distw", np.where((d >= 0) & (d < 256), d, BIG))
    cd, cm = np.zeros((P, 4, 32)), np.zeros((P, 4, 32))
    for q in range(4):
        d = (128 * q + p) - (16 * np.arange(32)[None, :] + 31)
        cm[:, q] = (d >= 0) & (np.arange(32)[None, :] < NCMP)
        cd[:, q] = d * cm[:, q]
    put("cdist", cd.reshape(P, -1))
    put("cmask", cm.reshape(P, -1))
    put("tril", (p <= np.arange(P)[None, :]) * 1.0)
    put("pi", np.full((P, 1), math.pi))
    return c


def dft_constants():
    k, t = np.arange(T), np.arange(T)
    ang = 2 * np.pi * np.outer(t, k) / (2 * T)
    fwd = np.concatenate([np.cos(ang), -np.sin(ang)], 1)
    fwd[:, T] = (-1.0) ** t
    inv = np.concatenate([2 * np.cos(ang.T), -2 * np.sin(ang.T)], 0) / (2 * T)
    inv[0] = 1.0 / (2 * T)
    inv[T] = (-1.0) ** t / (2 * T)
    fwd = fwd.reshape(NT, P, 2 * T).transpose(1, 0, 2).reshape(P, -1)
    inv = inv.reshape(2 * NT, P, T).transpose(1, 0, 2).reshape(P, -1)
    tt = np.linspace(0.0, 1.0, T)[:, None]
    bands = (FEMB - 1) // 2
    w = (2.0 * math.pi / T) * np.arange(T)[:, None]
    f = np.linspace(1e-4, bands - 1, bands)[None, :]
    z = np.concatenate([tt, np.cos(f * w), -np.sin(f * w)], -1)
    deltas = np.abs(np.linspace(math.log(1e-2) / 1.5, math.log(1e-2) / 0.3, RW))
    win = np.exp(-tt * deltas[None, :]) + 0.05
    win = win.reshape(NT, P, RW).transpose(1, 0, 2).reshape(P, -1)
    return [np.ascontiguousarray(a.astype(np.float32)) for a in (fwd, inv, z.T, win)]


class Token:

    def __init__(self, sem, value, loop=None, owner=None):
        self.sem, self.value, self.loop, self.owner = sem, value, loop, owner


class Counter:

    def __init__(self, book, name, step=1):
        self.book, self.name, self.step = book, name, step
        self.sem = book.nc.alloc_semaphore(name)
        self.count = 0

    def mark(self, ins):
        ins.then_inc(self.sem, self.step)
        self.count += self.step
        return Token(self, self.count, self.book.loop)


class Book:

    def __init__(self, nc, plan):
        self.nc, self.plan, self.loop = nc, plan, None
        self.counters = {}
        self.loops = 0
        self.names = {}
        self.fresh = {}

    def counter(self, name, step=1):
        if name not in self.counters:
            self.counters[name] = Counter(self, name, step)
        return self.counters[name]

    @contextmanager
    def run(self, n):
        lid = f"loop{self.loops}"
        self.loops += 1
        base = {k: c.count for k, c in self.counters.items()}
        per = self.plan.get(lid, {})
        with self.nc.Fori(0, n) as i:
            self.loop = (lid, i, base, per)
            self.names = {}
            yield i
            self.loop = None
        seen = {k: c.count - base.get(k, 0) for k, c in self.counters.items()}
        self.fresh[lid] = dict(seen, marks={k: t.value - base.get(t.sem.name, 0) for k, t in self.names.items()})
        for k, c in self.counters.items():
            c.count = base.get(k, 0) + n * seen[k]
        self.last = (lid, base, seen, n)

    def after(self, tok):
        lid, base, seen, n = self.last
        return Token(tok.sem, tok.value + (n - 1) * seen[tok.sem.name])

    def value(self, tok):
        if tok.loop is None:
            return tok.value
        lid, i, base, per = tok.loop
        assert self.loop is not None and self.loop[0] == lid
        return i * per.get(tok.sem.name, 0) + tok.value

    def name(self, key, tok):
        self.names[key] = tok
        return tok

    def later(self, key, counter):
        lid, i, base, per = self.loop
        return Token(counter, base.get(counter.name, 0) + per.get("marks", {}).get(key, 1), self.loop)

    def before(self, key, counter):
        lid, i, base, per = self.loop
        rise = per.get(counter.name, 0)
        off = per.get("marks", {}).get(key, 0)
        start = base.get(counter.name, 0)
        assert start - rise + off > 0 or not per, (key, start, rise)
        return Token(counter, start - rise + off, self.loop)


class Program:
    def __init__(self, nc, a, plan):
        self.nc, self.a = nc, a
        self.book = Book(nc, plan)
        b = self.book
        self.eng = {"pe": nc.tensor, "dve": nc.vector, "act": nc.scalar, "pool": nc.gpsimd, "sp": nc.sync}
        self.cnt = {k: b.counter(f"{k}_done") for k in self.eng}
        self.latest = {k: None for k in self.eng}
        self.loads = 0

    def wait(self, engine, *toks):
        for t in toks:
            if t is not None:
                self.eng[engine].wait_ge(t.sem.sem, self.book.value(t))

    def _step(self, engine, ins):
        t = self.cnt[engine].mark(ins)
        self.wait(engine, t)
        self.latest[engine] = t
        return t

    def dve(self, ins):
        return self._step("dve", ins)

    def act(self, ins):
        return self._step("act", ins)

    def pool(self, ins):
        return self._step("pool", ins)

    def pe(self, ins):
        t = self.cnt["pe"].mark(ins)
        self.latest["pe"] = t
        return t

    def load(self, dst, src, stream, engine="sync"):
        c = self.book.counter("dma_" + stream, 16)
        e = {"sync": self.nc.sync, "act": self.nc.scalar}[engine]
        return c.mark(e.dma_start(dst, src))

    def fence(self, *extra, skip=None):
        toks = [t for t in self.latest.values() if t is not None] + list(extra)
        for e in self.eng:
            if e == skip:
                continue
            for t in toks:
                if t.sem is not self.cnt[e]:
                    self.wait(e, t)

    def settle(self):
        for k, c in self.cnt.items():
            if c.count:
                self.latest[k] = Token(c, c.count)

    def mm(self, out, lhsT, rhs, start=True, stop=True):
        return self.nc.tensor.matmul(out, lhsT, rhs, start=start, stop=stop, skip_group_check=True)

    def take(self, bank):
        one = self.con("ident", 0, 32)
        self.mm(bank[0:32, 0:1], one, one[:, 0:1])

    def sb(self, stack, name, shape):
        return stack.enter_context(self.nc.sbuf_tensor(name, shape, F32))

    def vec(self, name, i=0, n=1, parts=P):
        o = VOFF[name] + i
        return self.V[0:parts, o:o + n]

    def con(self, name, i=0, n=None, p0=0, p1=P):
        o = COFF[name] + i
        return self.C[p0:p1, o:o + (n if n is not None else dict(CONST)[name] - i)]


def fm3(ap, n):
    return ap.rearrange("p (n t) -> p n t", n=n)


def build(nc, a, plan):
    g = Program(nc, a, plan)
    book, wait, dve, act, pe, mm = g.book, g.wait, g.dve, g.act, g.pe, g.mm
    v, s, tn = nc.vector, nc.scalar, nc.tensor
    top = ExitStack()
    with top:
        g.V = g.sb(top, "vecs", [P, NVEC])
        g.C = g.sb(top, "consts", [P, NCONST])
        X = g.sb(top, "residual", [P, KD, T])
        H = g.sb(top, "normed", [P, KD, T])
        R = g.sb(top, "rms", [P, T])
        SQ = g.sb(top, "squares", [P, 2, T])
        W = g.sb(top, "wring", [P, 2, KD, P])
        MOD = g.sb(top, "mods", [P, 2, 48, 2])
        SM = g.sb(top, "small", [P, 256])
        bank = [top.enter_context(nc.psum_tensor(f"bank{i}", [P, 512], F32)) for i in range(8)]
        vec, con = g.vec, g.con
        ident = con("ident")

        t_v = g.load(g.V[:, :], a["vecs"], "vecs")
        t_c = g.load(g.C[:, :], a["consts"], "consts")
        t_x = g.load(X[:, :, :], a["x_fm"].rearrange("p (k t) -> p k t", k=KD), "x")
        for e in ("dve", "act", "pe", "pool"):
            wait(e, t_v, t_c, t_x)
        for _ in range(40):
            dve(v.memset(SM[:, 0:1], 0.0))
            act(s.copy(SM[:, 1:2], g.C[:, 0:1]))
            pe(mm(bank[0][0:32, 0:32], ident[:, 0:32], ident[:, 0:32]))
        g.fence()

        def rms_rows(src, kd, n, eps, out, width):
            b = bank[7]
            free = [None, None]
            for k in range(kd):
                wait("dve", free[k % 2])
                t = dve(v.tensor_tensor(SQ[:, k % 2, 0:n], src(k), src(k), ALU.mult))
                wait("pe", t)
                free[k % 2] = pe(mm(b[:, 0:n], con("ones"), SQ[:, k % 2, 0:n], k == 0, k == kd - 1))
            wait("dve", free[(kd - 1) % 2])
            rsqrt(b[:, 0:n], 1.0 / width, eps, out[:, 0:n])

        def rsqrt(psum, scale, eps, out):
            t = dve(v.tensor_scalar(out, psum, scale, eps, ALU.mult, ALU.add))
            wait("act", t)
            t = act(s.activation(out, out, ACT.Sqrt))
            wait("dve", t)
            dve(v.reciprocal(out, out))

        def project(n_chunks, wsrc, rhs, n, evac, kd=KD):
            assert n_chunks % 2 == 0
            with book.run(n_chunks // 2) as i:
                for j in range(2):
                    wait("sp", book.before(f"mm{j}", g.cnt["pe"]))
                    t_w = g.load(W[:, j, 0:kd, :], wsrc(i * 2 + j), f"w{j}")
                    wait("pe", t_w, book.before(f"ev{j}", g.cnt[evac_engine(j)]))
                    for k in range(kd):
                        ins = mm(bank[j][:, 0:n], W[:, j, k, :], rhs(k), k == 0, k == kd - 1)
                    t_m = book.name(f"mm{j}", pe(ins))
                    wait(evac_engine(j), t_m)
                    book.name(f"ev{j}", evac(i * 2 + j, bank[j][:, 0:n], evac_engine(j)))
            g.settle()
            g.fence()

        def evac_engine(j):
            return "dve"

        def wblock(name):
            return lambda i: a[name][bass.ds(i, 1), :, :].rearrange("o p (k c) -> p (o k) c", c=P)

        def adaln(layer):
            with ExitStack() as st:
                wm = g.sb(st, f"wmod{layer}", [P, 4, KD, 512])
                cs = g.sb(st, f"cs{layer}", [P, KD, 32])
                row = g.sb(st, f"mrow{layer}", [P, 512])
                g.fence()
                dve(v.memset(cs[:, :, :], 0.0))
                wait("act", g.latest["dve"])
                act(s.activation(cs[:, :, 0], vec("c", 0, 8), ACT.Silu))
                t = act(s.activation(cs[:, :, 1], vec("c_ctx", 0, 8), ACT.Silu))
                wait("pe", t)
                wait("dve", t)
                src = a["w_mod"][layer].rearrange("(k p) c -> p k c", p=P)
                with book.run(3) as i:
                    wait("sp", book.before("mm", g.cnt["pe"]))
                    for q in range(4):
                        wait("pe", g.load(wm[:, q, :, :], src[:, :, bass.ds((i * 4 + q) * 512, 512)], f"wm{q}"))
                    wait("pe", book.before("row", g.cnt["dve"]))
                    for k in range(KD):
                        for q in range(4):
                            ins = mm(bank[0][32 * q:32 * q + 32, :], cs[:, k, :], wm[:, q, k, :], k == 0, k == KD - 1)
                    t = book.name("mm", pe(ins))
                    wait("dve", t)
                    t = book.name("row", dve(v.tensor_copy(row[:, :], bank[0][:, :])))
                    wait("pe", t)
                    for j in range(4):
                        ins = tn.transpose(bank[1][:, j * P:(j + 1) * P], row[:, j * P:(j + 1) * P], ident)
                    t = pe(ins)
                    wait("dve", t)
                    for j in range(4):
                        for r in range(2):
                            o = MOD[:, layer, bass.ds(i * 16 + j, 4, 4), r]
                            dve(v.tensor_copy(o, bank[1][:, j * P + r:(j + 1) * P:32]))
                g.settle()
                g.fence()
                for r in range(2):
                    dve(v.tensor_tensor(MOD[:, layer, :, r], MOD[:, layer, :, r], vec("b_mod", 48 * layer, 48), ALU.add))
                g.fence()

        GA = g.sb(top, "gains", [P, 5, 8])

        def gain_of(slot, norm, off, layer, scale_chunk, r=0):
            dve(v.tensor_scalar(GA[:, slot, :], MOD[:, layer, scale_chunk:scale_chunk + 8, r], 1.0, None, ALU.add))
            dve(v.tensor_tensor(GA[:, slot, :], GA[:, slot, :], vec(norm, off, 8), ALU.mult))

        def modulate(src, n, slot, shift, dst):
            for k in range(KD):
                dve(v.tensor_tensor(dst(k), src(k), R[:, 0:n], ALU.mult))
                if shift is None:
                    dve(v.tensor_scalar(dst(k), dst(k), GA[:, slot, k:k + 1], None, ALU.mult))
                else:
                    dve(v.tensor_scalar(dst(k), dst(k), GA[:, slot, k:k + 1], shift(k), ALU.mult, ALU.add))

        def softplus(x, tmp, tmp2, tmp3):
            wait("act", g.latest["dve"])
            act(s.activation(tmp, x, ACT.Abs))
            act(s.activation(tmp, tmp, ACT.Exp, scale=-1.0))
            wait("dve", g.latest["act"])
            dve(v.tensor_scalar(tmp2, tmp, 2.0, None, ALU.add))
            dve(v.reciprocal(tmp2, tmp2))
            dve(v.tensor_tensor(tmp, tmp, tmp2, ALU.mult))
            dve(v.tensor_tensor(tmp2, tmp, tmp, ALU.mult))
            dve(v.tensor_scalar(tmp3, tmp2, 1.0 / 15, None, ALU.mult))
            for d in (13, 11, 9, 7, 5, 3):
                dve(v.scalar_tensor_tensor(out=tmp3, in0=tmp3, scalar=1.0 / d, in1=tmp2, op0=ALU.add, op1=ALU.mult))
            dve(v.scalar_tensor_tensor(out=tmp, in0=tmp3, scalar=1.0, in1=tmp, op0=ALU.add, op1=ALU.mult))
            dve(v.tensor_scalar(x, x, 0.0, None, ALU.max))
            dve(v.scalar_tensor_tensor(out=x, in0=tmp, scalar=2.0, in1=x, op0=ALU.mult, op1=ALU.add))

        def dwconv(dst, src, n, wname, w0, stride, ntap, lead, bname=None, b0=0):
            if bname is None:
                dve(v.tensor_scalar(dst[:, 0:n], src[:, 0:n], vec(wname, w0 + lead * stride), None, ALU.mult))
            else:
                dve(v.tensor_scalar(dst[:, 0:n], src[:, 0:n], vec(wname, w0 + lead * stride), vec(bname, b0),
                                    ALU.mult, ALU.add))
            for j in range(ntap):
                d = j - lead
                if d == 0:
                    continue
                lo, hi = max(0, -d), min(n, n - d)
                dve(v.scalar_tensor_tensor(out=dst[:, lo:hi], in0=src[:, lo + d:hi + d], scalar=vec(wname, w0 + j * stride),
                                           in1=dst[:, lo:hi], op0=ALU.mult, op1=ALU.add))

        EXTRA = {}

        LW = g.sb(top, "lru_state", [P, 2, 4])
        SPL = g.sb(top, "lru_rate", [P, 3, 8])

        def rglru(raw, n, gw, out, context):
            with ExitStack() as st:
                xa = g.sb(st, f"xa{n}", [P, T])
                ta = g.sb(st, f"lru_a{n}", [P, T])
                tu = g.sb(st, f"lru_u{n}", [P, T])
                t1 = g.sb(st, f"lru_t{n}", [P, T])
                g.fence()
                for k in range(KR):
                    dwconv(xa, raw(k), n, "conv_a_w", k, KR, 4, 1, "conv_a_b", k)
                    wait("pe", g.latest["dve"])
                    for d in range(2):
                        j = d * KR + k
                        wait("pe", g.latest["act"])
                        mm(bank[0][:, 0:n], gw[:, 2 * j, :], xa[:, 0:n])
                        t = pe(mm(bank[1][:, 0:n], gw[:, 2 * j + 1, :], xa[:, 0:n]))
                        wait("act", t, g.latest["dve"])
                        act(s.activation(ta[:, 0:n], bank[0][:, 0:n], ACT.Sigmoid, bias=vec("lru_br", j)))
                        t = act(s.activation(tu[:, 0:n], bank[1][:, 0:n], ACT.Sigmoid, bias=vec("lru_bi", j)))
                        wait("dve", t)
                        dve(v.tensor_scalar(ta[:, 0:n], ta[:, 0:n], SPL[:, 0, j:j + 1], -LRU_C, ALU.mult, ALU.mult))
                        wait("act", g.latest["dve"])
                        t = act(s.activation(t1[:, 0:n], ta[:, 0:n], ACT.Tanh))
                        act(s.activation(ta[:, 0:n], ta[:, 0:n], ACT.Tanh, scale=0.5))
                        wait("dve", g.latest["act"])
                        dve(v.tensor_tensor(tu[:, 0:n], tu[:, 0:n], xa[:, 0:n], ALU.mult))
                        q1, q2 = SQ[:, 0, 0:n], SQ[:, 1, 0:n]
                        dve(v.tensor_scalar(q1, t1[:, 0:n], -1.0, 1.0, ALU.mult, ALU.add))
                        dve(v.reciprocal(q1, q1))
                        dve(v.scalar_tensor_tensor(out=q1, in0=t1[:, 0:n], scalar=-2.0, in1=q1, op0=ALU.mult, op1=ALU.mult))
                        wait("act", g.latest["dve"])
                        act(s.activation(q1, q1, ACT.Sqrt))
                        dve(v.tensor_scalar(q2, ta[:, 0:n], -1.0, 1.0, ALU.mult, ALU.add))
                        dve(v.reciprocal(q2, q2))
                        dve(v.scalar_tensor_tensor(out=ta[:, 0:n], in0=ta[:, 0:n], scalar=1.0, in1=q2, op0=ALU.add, op1=ALU.mult))
                        wait("dve", g.latest["act"])
                        dve(v.tensor_tensor(tu[:, 0:n], tu[:, 0:n], q1, ALU.mult))
                        o = out(d, k)
                        init = 0.0 if context else LW[:, d, k:k + 1]
                        if d == 0:
                            dve(v.tensor_tensor_scan(o[:, 0:n], ta[:, 0:n], tu[:, 0:n], init, ALU.mult, ALU.add))
                        else:
                            dve(v.tensor_tensor_scan(o[:, n - 1::-1] if n == T else o[:, n - 1::-1], ta[:, n - 1::-1],
                                                     tu[:, n - 1::-1], init, ALU.mult, ALU.add))
                        if context:
                            e = n - 1 if d == 0 else 0
                            dve(v.tensor_copy(LW[:, d, k:k + 1], o[:, e:e + 1]))
                g.fence()

        def layer0_mixer():
            gain_of(0, "norm1_g", 0, 0, 8)
            gain_of(1, "norm1_g", 0, 0, 8, 1)
            with ExitStack() as st:
                gw = g.sb(st, "lru_w", [P, 16, P])
                g.fence()
                dve(v.memset(gw[:, :, :], 0.0))
                wait("sp", g.latest["dve"])
                t1 = g.load(gw[0:64, :, 0:64], a["lru_w"][0], "lru_w0")
                t2 = g.load(gw[64:128, :, 64:128], a["lru_w"][1], "lru_w1")
                wait("pe", t1, t2)
                dve(v.tensor_scalar(SPL[:, 0, :], vec("lru_lam", 0, 8), -1.0, None, ALU.mult))
                softplus(SPL[:, 0, :], SPL[:, 1, :], SPL[:, 2, :], SM[:, 0:8])
                with ExitStack() as cx:
                    xc = g.sb(cx, "ctx", [P, KD, TC])
                    ra = g.sb(cx, "ctx_raw", [P, KR, TC])
                    hs = g.sb(cx, "ctx_h", [P, 2, TC])
                    g.fence()
                    t = g.load(xc[:, :, :], a["ctx_fm"].rearrange("p (k t) -> p k t", k=KD), "ctx")
                    wait("dve", t)
                    rms_rows(lambda k: xc[:, k, :], KD, TC, EPS, R, D)
                    modulate(lambda k: xc[:, k, :], TC, 1, lambda k: MOD[:, 0, k, 1:2], lambda k: xc[:, k, :])
                    g.fence()

                    def ev(i, ps, e):
                        return dve(v.tensor_copy(ra[:, bass.ds(i, 1), :].rearrange("p o t -> p (o t)"), ps))

                    src = wblock("w_in")
                    project(KR, lambda i: src(i + KR), lambda k: xc[:, k, :], TC, ev)
                    rglru(lambda k: ra[:, k, :], TC, gw, lambda d, k: hs[:, d, :], True)
                rms_rows(lambda k: X[:, k, :], KD, T, EPS, R, D)
                modulate(lambda k: X[:, k, :], T, 0, lambda k: MOD[:, 0, k, 0:1], lambda k: H[:, k, :])
                pr = g.sb(st, "proj", [P, 20, T])
                g.fence()

                def ev(i, ps, e):
                    return dve(v.tensor_copy(pr[:, bass.ds(i, 1), :].rearrange("p o t -> p (o t)"), ps))

                project(20, wblock("w_in"), lambda k: H[:, k, :], T, ev)
                ht = g.sb(st, "lru_h", [P, 2, KR, T])
                g.fence()
                rglru(lambda k: pr[:, KR + k, :], T, gw, lambda d, k: ht[:, d, k, :], False)
                for k in range(KR):
                    act(s.activation(pr[:, k, :], pr[:, k, :], ACT.Gelu_apprx_tanh))
                    dve(v.tensor_tensor(ht[:, 0, k, :], ht[:, 0, k, :], ht[:, 1, k, :], ALU.add))
                    wait("dve", g.latest["act"])
                    dve(v.tensor_tensor(H[:, k, :], ht[:, 0, k, :], pr[:, k, :], ALU.mult))
                g.fence()
                for k in range(12):
                    tmp = ht[:, 0, k % 4, :]
                    dwconv(tmp, pr[:, 8 + k, :], T, "conv_b_w", k, 12, 3, 1, "conv_b_b", k)
                    dve(v.tensor_copy(pr[:, 8 + k, :], tmp))
                g.fence()
                hyena(st, lambda k: pr[:, 8 + k, :], lambda o, k: pr[:, 12 + 4 * o + k, :], ht, lambda k: H[:, KR + k, :], pr)


            def ev(i, ps, e):
                xi = X[:, bass.ds(i, 1), :].rearrange("p o t -> p (o t)")
                return dve(v.scalar_tensor_tensor(out=xi, in0=ps, scalar=MOD[:, 0, bass.ds(i + 16, 1), 0:1].rearrange("p a b -> p (a b)"),
                                                  in1=xi, op0=ALU.mult, op1=ALU.add))

            project(KD, wblock("w_out"), lambda k: H[:, k, :], T, ev)

        def hyena(outer, zin, gate, ztm, zout, pr):
            ztm = ztm[:, 0, :, :]
            with ExitStack() as st:
                fw = g.sb(st, "dft", [P, NT, 2 * T])
                sd = g.sb(st, "filt_sd", [P, 2, NT, RW])
                kf = g.sb(st, "spectrum", [P, 9, RW])
                hid = g.sb(st, "hidden", [FHID + 1, 2, T])
                w3 = g.sb(st, "filt_w3", [FHID + 1, 4, RW])
                w12 = g.sb(st, "filt_w12", [FHID, 2, FHID])
                zf = g.sb(st, "filt_z", [FEMB, T])
                win = g.sb(st, "window", [P, NT, RW])
                g.fence()
                tt = [g.load(fw[:, :, :], a["dft"].rearrange("p (k t) -> p k t", k=NT), "dft"),
                      g.load(w3[0:FHID, :, :], a["filt_w3"].rearrange("p (q c) -> p q c", q=4), "fw3"),
                      g.load(w3[FHID:FHID + 1, :, :], a["filt_b3"].rearrange("p (q c) -> p q c", q=4), "fb3"),
                      g.load(w12[0:FEMB, 0, :], a["filt_w1"], "fw1"),
                      g.load(w12[:, 1, :], a["filt_w2"], "fw2"),
                      g.load(zf[:, :], a["filt_z"], "fz"),
                      g.load(win[:, :, :], a["window"].rearrange("p (k t) -> p k t", k=NT), "win")]
                wait("pe", *tt)
                wait("dve", *tt)
                t_in = dve(v.memset(hid[FHID:FHID + 1, :, :], 1.0))

                def sine(ps, layer, dst):
                    f = vec(f"filt_freq{layer}", parts=FHID)
                    dve(v.tensor_scalar(dst, ps, vec(f"filt_b{layer + 1}", parts=FHID), f, ALU.add, ALU.mult))
                    q = SQ[0:FHID, 0, :]
                    dve(v.tensor_scalar(q, dst, 1.0 / (2 * math.pi), 12582912.0, ALU.mult, ALU.add))
                    dve(v.tensor_scalar(q, q, -12582912.0, None, ALU.add))
                    c1 = 6.28125
                    dve(v.scalar_tensor_tensor(out=dst, in0=q, scalar=-c1, in1=dst, op0=ALU.mult, op1=ALU.add))
                    dve(v.scalar_tensor_tensor(out=dst, in0=q, scalar=-(2 * math.pi - c1), in1=dst, op0=ALU.mult, op1=ALU.add))
                    dve(v.tensor_scalar(dst, dst, 3.1415925, -3.1415925, ALU.min, ALU.max))
                    wait("act", g.latest["dve"])
                    act(s.activation(dst, dst, ACT.Sin))
                    wait("pe", g.latest["act"])

                t = pe(mm(bank[0][0:FHID, :], w12[0:FEMB, 0, :], zf[:, :]))
                wait("dve", t)
                sine(bank[0][0:FHID, :], 0, hid[0:FHID, 0, :])
                t = pe(mm(bank[1][0:FHID, :], w12[:, 1, :], hid[0:FHID, 0, :]))
                wait("dve", t)
                sine(bank[1][0:FHID, :], 1, hid[0:FHID, 1, :])
                for o in range(2):
                    for n in range(NT):
                        fb = [bank[2 * (n % 2)], bank[2 * (n % 2) + 1]]
                        wait("pe", g.latest["dve"])
                        for q in range(2):
                            ins = mm(fb[q][:, :], hid[:, 1, n * P:(n + 1) * P], w3[:, 2 * o + q, :])
                        t = pe(ins)
                        wait("dve", t)
                        f0, f1 = SQ[:, 0, :], SQ[:, 1, :]
                        dve(v.tensor_tensor(f0, fb[0][:, :], win[:, n, :], ALU.mult))
                        dve(v.tensor_tensor(f1, fb[1][:, :], win[:, n, :], ALU.mult))
                        if n == 0:
                            dve(v.memset(SQ[0:1, 1, :], 0.0))
                        dve(v.tensor_tensor(sd[:, 0, n, :], f0, f1, ALU.add))
                        dve(v.tensor_tensor(sd[:, 1, n, :], f0, f1, ALU.subtract))
                    wait("pe", g.latest["dve"])
                    done = []
                    for m in range(9):
                        b = bank[m % 8]
                        if m == 8:
                            wait("pe", done[0])
                        col = m * P if m < 8 else T
                        for k in range(NT):
                            ins = mm(b[:, :], fw[:, k, col:col + P], sd[:, 1 if 4 <= m < 8 else 0, k, :], k == 0, k == NT - 1)
                        t = pe(ins)
                        wait("act", t)
                        done.append(act(s.copy(kf[:, m, :], b[:, :])))
                    wait("dve", g.latest["act"])
                    dve(v.tensor_copy(SM[:, 128:130], g.C[:, 0:2]))
                    dve(v.tensor_copy(SQ[0:1, 0, :], kf[0:1, 8, :]))
                    dve(v.tensor_copy(kf[:, 8, :], kf[:, 0, :]))
                    dve(v.tensor_copy(kf[0:1, 8, :], SQ[0:1, 0, :]))
                    dve(v.memset(kf[0:1, 4, :], 0.0))
                    g.fence()
                    for n in range(NT):
                        for k in range(KR):
                            ins = tn.transpose(bank[n][:, k * P:(k + 1) * P], zin(k)[:, n * P:(n + 1) * P], ident)
                        t = pe(ins)
                        wait("dve", t)
                        dve(v.tensor_copy(ztm[:, n, :], bank[n][:, :]))
                    g.fence()
                    ys = sd.rearrange("p a k c -> p (a k) c") if False else sd
                    for m in range(NT):
                        br, bi = bank[2 * m], bank[2 * m + 1]
                        for k in range(NT):
                            mm(br[:, :], fw[:, k, m * P:(m + 1) * P], ztm[:, k, :], k == 0, k == NT - 1)
                        for k in range(NT):
                            ins = mm(bi[:, :], fw[:, k, T + m * P:T + (m + 1) * P], ztm[:, k, :], k == 0, k == NT - 1)
                        t = pe(ins)
                        wait("dve", t)
                        kr, ki = kf[:, m, :], kf[:, 4 + m, :]
                        kr2 = kf[:, 8, :] if m == 0 else kr
                        q0, q1 = SQ[:, 0, :], SQ[:, 1, :]
                        dve(v.tensor_tensor(q0, br[:, :], kr, ALU.mult))
                        dve(v.tensor_tensor(q1, bi[:, :], ki, ALU.mult))
                        dve(v.tensor_tensor(sd[:, 0, m, :], q0, q1, ALU.subtract))
                        dve(v.tensor_tensor(q0, br[:, :], ki, ALU.mult))
                        dve(v.tensor_tensor(q1, bi[:, :], kr2, ALU.mult))
                        dve(v.tensor_tensor(sd[:, 1, m, :], q0, q1, ALU.add))
                    g.fence()
                    t = g.load(kf[:, 0:8, :], a["idft"].rearrange("p (k t) -> p k t", k=8), "idft")
                    wait("pe", t)
                    for k in range(KR):
                        for m in range(8):
                            ins = mm(bank[k][:, :], sd[:, m // 4, m % 4, k * P:(k + 1) * P], kf[:, m, :], m == 0, m == 7)
                        t = pe(ins)
                        wait("dve", t)
                        dst = zin(k) if o == 0 else zout(k)
                        dve(v.scalar_tensor_tensor(out=zin(k), in0=zin(k), scalar=vec("filt_bias", 4 * o + k),
                                                   in1=bank[k][:, :], op0=ALU.mult, op1=ALU.add))
                        dve(v.tensor_tensor(dst, zin(k), gate(o, k), ALU.mult))
                    g.fence()

        def moe(layer):
            sh, sc, gt = (24, 32, 40)
            L = f"_{layer}"
            with ExitStack() as st:
                ring = g.sb(st, "experts" + L, [P, NRING, 2, FF])
                HT = g.sb(st, "h_tm" + L, [P, NT, D])
                rt = g.sb(st, "router" + L, [P, KD, NE])
                pb = g.sb(st, "probs" + L, [P, NT, NE + 2])
                sl = g.sb(st, "slots" + L, [P, NT, NE + 2])
                pe_t = g.sb(st, "probs_e" + L, [NE, T])
                wk = g.sb(st, "topk" + L, [NE, 2, T])
                mx = g.sb(st, "max8" + L, [NE, 8])
                PM = g.sb(st, "pick" + L, [P, NT, 2, CAP])
                PG = g.sb(st, "give" + L, [P, NT, 2, CAP])
                PT = g.sb(st, "give_t" + L, [P, T])
                xr = W[:, 0, :, :].rearrange("p k c -> p (k c)")
                xs = W[:, 1, :, :]
                hs = SQ
                hT = g.sb(st, "hs_t" + L, [P, 2, 4, P])
                yy = g.sb(st, "y" + L, [P, D])
                g.fence()
                t = g.load(rt[:, :, :], a["router"][layer].rearrange("p (k e) -> p k e", k=KD), "router")
                wait("pe", t)
                gain_of(2, "norm2_g", 8 * layer, layer, sc)
                rms_rows(lambda k: X[:, k, :], KD, T, EPS, R, D)
                modulate(lambda k: X[:, k, :], T, 2, lambda k: MOD[:, layer, sh + k, 0:1], lambda k: H[:, k, :])
                wait("pe", g.latest["dve"])
                for k in range(KD):
                    ins = mm(bank[0][0:NE, :], rt[:, k, :], H[:, k, :], k == 0, k == KD - 1)
                t = pe(ins)
                wait("dve", t)
                t_l = dve(v.tensor_copy(pe_t[:, :], bank[0][0:NE, :]))
                wait("pe", t_l)
                for n in range(NT):
                    ins = tn.transpose(bank[1][:, n * NE:(n + 1) * NE], pe_t[:, n * P:(n + 1) * P], ident[0:NE, 0:NE])
                t_lt = pe(ins)
                for n in range(NT):
                    for h in range(2):
                        b = bank[4 + (2 * n + h) % 4]
                        if n >= 2:
                            wait("pe", t_h[2 * n + h - 4])
                        elif n + h == 0:
                            t_h = []
                        for k in range(4):
                            ins = tn.transpose(b[:, k * P:(k + 1) * P], H[:, 4 * h + k, n * P:(n + 1) * P], ident)
                        t = pe(ins)
                        wait("act", t)
                        t_h.append(act(s.copy(HT[:, n, 512 * h:512 * h + 512], b[:, :])))
                wait("dve", t_lt)
                lg = bank[1][:, 0:NT * NE].rearrange("p (n e) -> p n e", n=NT)
                pr = pb[:, :, 0:NE]
                dve(v.tensor_reduce(SM[:, 0:NT], lg, AXX, ALU.max))
                dve(v.tensor_tensor(pr, lg, SM[:, 0:NT].unsqueeze(2).broadcast_to([P, NT, NE]), ALU.subtract))
                wait("act", g.latest["dve"])
                act(s.activation(pr, pr, ACT.Exp))
                wait("dve", g.latest["act"])
                dve(v.tensor_reduce(SM[:, 8:8 + NT], pr, AXX, ALU.add))
                dve(v.reciprocal(SM[:, 8:8 + NT], SM[:, 8:8 + NT]))
                dve(v.tensor_tensor(pr, pr, SM[:, 8:8 + NT].unsqueeze(2).broadcast_to([P, NT, NE]), ALU.mult))
                wait("pe", g.latest["dve"])
                for n in range(NT):
                    ins = tn.transpose(bank[2][0:NE, n * P:(n + 1) * P], pb[:, n, 0:NE], ident)
                t = pe(ins)
                wait("dve", t)
                dve(v.tensor_copy(wk[:, 0, :], bank[2][0:NE, :]))
                for r in range(CAP // 8):
                    dve(v.max(mx[:, :], wk[:, r % 2, :]))
                    dve(v.match_replace(wk[:, (r + 1) % 2, :], mx[:, :], wk[:, r % 2, :], -1.0))
                dve(v.tensor_scalar(wk[:, 1, :], wk[:, 0, :], -1.0, None, ALU.is_equal))
                dve(v.memset(pe_t[:, :], 1.0))
                dve(v.tensor_tensor_scan(wk[:, 0, :], pe_t[:, :], wk[:, 1, :], 0.0, ALU.mult, ALU.add))
                dve(v.tensor_tensor(wk[:, 0, :], wk[:, 0, :], wk[:, 1, :], ALU.mult))
                dve(v.tensor_scalar(wk[:, 0, :], wk[:, 0, :], -1.0, None, ALU.add))
                wait("pe", g.latest["dve"])
                for n in range(NT):
                    ins = tn.transpose(bank[3][:, n * NE:(n + 1) * NE], wk[:, 0, n * P:(n + 1) * P], ident[0:NE, 0:NE])
                t = pe(ins)
                dve(v.memset(sl[:, :, :], -1.0))
                dve(v.memset(pb[:, :, NE:NE + 2], 0.0))
                dve(v.memset(yy[:, :], 0.0))
                dve(v.memset(PT[:, :], 0.0))
                wait("dve", t)
                dve(v.tensor_copy(sl[:, :, 0:NE], bank[3][:, 0:NT * NE].rearrange("p (n e) -> p n e", n=NT)))
                w = {q: a[f"exp_w{q}"][layer].rearrange("e (j k p) f -> e j p k f", j=4, p=P) for q in (1, 3, 2)}
                iota = con("iota", 0, CAP).unsqueeze(1).unsqueeze(1).broadcast_to([P, NT, 2, CAP])
                order = [(q, e, j) for e in range(2) for j in range(4) for q in (1, 3)]
                order += [(2, e, j) for j in range(4) for e in range(2)]
                place = {x: n % NRING for n, x in enumerate(order)}

                def pick(pair):
                    so = sl[:, :, bass.ds(pair * 2, 2)].unsqueeze(3).broadcast_to([P, NT, 2, CAP])
                    return dve(v.tensor_tensor(PM[:, :, :, :], iota, so, ALU.is_equal))

                def give(pair):
                    po = pb[:, :, bass.ds(pair * 2, 2)].unsqueeze(3).broadcast_to([P, NT, 2, CAP])
                    return dve(v.tensor_tensor(PG[:, :, :, :], PM[:, :, :, :], po, ALU.mult))

                def gather():
                    for h in range(2):
                        for n in range(NT):
                            ins = mm(bank[6 + h][:, :], PM[:, n, :, :], HT[:, n, 512 * h:512 * h + 512], n == 0, n == NT - 1)
                        t = pe(ins)
                        wait("act", t)
                        t_x = act(s.copy(xr[:, 512 * h:512 * h + 512], bank[6 + h][:, :]))
                    return t, t_x

                def turn(t_x):
                    wait("pe", t_x)
                    for h in range(2):
                        for k in range(4):
                            ins = tn.transpose(bank[6 + h][:, k * P:(k + 1) * P], xr[:, (4 * h + k) * P:(4 * h + k + 1) * P], ident)
                        t = pe(ins)
                        wait("act", t)
                        t_xs = act(s.copy(xs[:, 4 * h:4 * h + 4, :], bank[6 + h][:, :].rearrange("p (k c) -> p k c", k=4)))
                    return t, t_xs

                def scatter(last_adds):
                    adds = []
                    for k in range(KD):
                        b = bank[4 + k % 2]
                        wait("pe", last_adds[k] if k < 2 else adds[k - 2])
                        t = pe(mm(b[:, :], yy[:, k * P:(k + 1) * P], PT[:, :]))
                        wait("dve", t)
                        adds.append(dve(v.scalar_tensor_tensor(out=X[:, k, :], in0=b[:, :], scalar=MOD[:, layer, gt + k, 0:1],
                                                               in1=X[:, k, :], op0=ALU.mult, op1=ALU.add)))
                    return t, adds

                t = pick(0)
                wait("pe", t, g.latest["act"])
                t, t_x = gather()
                wait("dve", t)
                give(0)
                turn(t_x)
                g.fence(skip="sp")
                with book.run(NE // 2) as i:
                    cpe, cdve, cact = g.cnt["pe"], g.cnt["dve"], g.cnt["act"]
                    tw = {}
                    for n, (q, e, j) in enumerate(order):
                        if n < NRING:
                            wait("sp", book.before(f"use{n}", cpe))
                        else:
                            wait("sp", book.later(f"use{n - NRING}x", cpe))
                        tw[q, e, j] = g.load(ring[:, place[q, e, j], :, :],
                                             w[q][bass.ds(i * 2 + e, 1), j].rearrange("o p k f -> p (o k) f"),
                                             f"ring{place[q, e, j]}")

                    def used(x, t):
                        n = order.index(x)
                        if n < len(order) - NRING:
                            book.name(f"use{n}x", t)
                        if n >= len(order) - NRING:
                            book.name(f"use{n - (len(order) - NRING)}", t)

                    def up(e):
                        for j in range(4):
                            for q, m in ((0, 1), (1, 3)):
                                wait("pe", tw[m, e, j])
                                for k in range(2):
                                    for f in range(2):
                                        ins = mm(bank[2 * e + q][64 * f:64 * f + 64, :], xs[:, 2 * j + k, 64 * e:64 * e + 64],
                                                 ring[:, place[m, e, j], k, 512 * f:512 * f + 512], j + k == 0, j == 3 and k == 1)
                                t = pe(ins)
                                used((m, e, j), t)
                        wait("act", t)
                        t_s = act(s.activation(hs[:, e, :], bank[2 * e][:, :], ACT.Silu))
                        wait("dve", t_s)
                        return dve(v.tensor_tensor(hs[:, e, :], hs[:, e, :], bank[2 * e + 1][:, :], ALU.mult))

                    def turn_hidden(e, t_hs):
                        wait("pe", t_hs)
                        for k in range(4):
                            ins = tn.transpose(bank[4 + e][:, k * P:(k + 1) * P], hs[:, e, k * P:(k + 1) * P], ident)
                        t = pe(ins)
                        wait("act", t)
                        return act(s.copy(hT[:, e, :, :], bank[4 + e][:, :].rearrange("p (k c) -> p k c", k=4)))

                    wait("dve", book.before("gather", cpe))
                    t_pm = pick(i + 1)
                    wait("pe", book.before("xs", cact), book.before("yy", cact))
                    t_h0 = up(0)
                    t_sc, adds = scatter([book.before("hT0", cact), book.before("hT1", cact)])
                    for n in range(NT):
                        ins = tn.transpose(bank[7][:, n * P:(n + 1) * P], PG[:, n, :, :].rearrange("p e c -> p (e c)"), ident)
                    t = pe(ins)
                    wait("act", t)
                    t_pt = act(s.copy(PT[:, :], bank[7][:, :]))
                    wait("dve", t)
                    give(i + 1)
                    t_h1 = up(1)
                    wait("pe", adds[6])
                    t_ht0 = book.name("hT0", turn_hidden(0, t_h0))
                    wait("pe", t_pm, t_pt)
                    t, t_x = gather()
                    book.name("gather", t)
                    wait("pe", adds[7])
                    t_ht1 = book.name("hT1", turn_hidden(1, t_h1))
                    _, t_xs = turn(t_x)
                    book.name("xs", t_xs)
                    wait("pe", t_ht0, t_ht1)
                    for j in range(4):
                        for e in range(2):
                            wait("pe", tw[2, e, j])
                        for k in range(2):
                            kk = 2 * j + k
                            for f in range(2):
                                for e in range(2):
                                    ins = mm(bank[f][64 * e:64 * e + 64, :], hT[:, e, kk % 4, 64 * (kk // 4):64 * (kk // 4) + 64],
                                             ring[:, place[2, e, j], k, 512 * f:512 * f + 512], kk == 0, kk == 7)
                        t = pe(ins)
                        used((2, 0, j), t)
                        used((2, 1, j), t)
                    wait("act", t)
                    for f in range(2):
                        t_y = act(s.copy(yy[:, 512 * f:512 * f + 512], bank[f][:, :]))
                    book.name("yy", t_y)
                g.settle()
                g.fence()
                scatter([None, None])
                g.fence()

        def layer1_mixer():
            gain_of(0, "norm1_g", 8, 1, 8)
            rms_rows(lambda k: X[:, k, :], KD, T, EPS, R, D)
            modulate(lambda k: X[:, k, :], T, 0, lambda k: MOD[:, 1, k, 0:1], lambda k: H[:, k, :])
            with ExitStack() as st:
                U = g.sb(st, "cf_u", [P, KD, T])
                Y = g.sb(st, "cf_y", [P, KD, T])
                gs = g.sb(st, "cf_sig", [P, T])
                g.fence()

                def row(tile, i):
                    return tile[:, bass.ds(i, 1), :].rearrange("p o t -> p (o t)")

                def ev_a(i, ps, e):
                    return dve(v.tensor_scalar(row(U, i), ps, g.V[:, bass.ds(i + VOFF["cf_b1"], 1)], None, ALU.add))

                project(KD, wblock("cf_w1"), lambda k: H[:, k, :], T, ev_a)

                def ev_g(i, ps, e):
                    dve(v.tensor_scalar(gs[:, :], ps, g.V[:, bass.ds(i + VOFF["cf_b1"] + 8, 1)], None, ALU.add))
                    wait("act", g.latest["dve"])
                    act(s.activation(gs[:, :], gs[:, :], ACT.Sigmoid))
                    wait("dve", g.latest["act"])
                    return dve(v.tensor_tensor(row(U, i), row(U, i), gs[:, :], ALU.mult))

                src = wblock("cf_w1")
                project(KD, lambda i: src(i + KD), lambda k: H[:, k, :], T, ev_g)
                rows = T // GRID_W
                half = (CF_K - 1) // 2
                for k in range(KD):
                    dve(v.tensor_scalar(Y[:, k, :], U[:, k, :], vec("cf_dw_w", half * 8 + k), vec("cf_dw_b", k), ALU.mult, ALU.add))
                    for j in range(-(rows - 1), rows):
                        if j == 0 or abs(j) > half:
                            continue
                        lo, hi = max(0, -j * GRID_W), min(T, T - j * GRID_W)
                        dve(v.scalar_tensor_tensor(out=Y[:, k, lo:hi], in0=U[:, k, lo + j * GRID_W:hi + j * GRID_W],
                                                   scalar=vec("cf_dw_w", (half + j) * 8 + k), in1=Y[:, k, lo:hi],
                                                   op0=ALU.mult, op1=ALU.add))
                wait("pe", g.latest["dve"])
                for k in range(KD):
                    ins = mm(bank[0][:, :], con("ones"), Y[:, k, :], k == 0, k == KD - 1)
                t = pe(ins)
                wait("dve", t)
                dve(v.tensor_scalar(gs[:, :], bank[0][:, :], -1.0 / D, None, ALU.mult))
                for k in range(KD):
                    dve(v.tensor_tensor(Y[:, k, :], Y[:, k, :], gs[:, :], ALU.add))
                rms_rows(lambda k: Y[:, k, :], KD, T, EPS, R, D)
                for k in range(KD):
                    t = dve(v.tensor_tensor(Y[:, k, :], Y[:, k, :], R[:, :], ALU.mult))
                    wait("act", t)
                    act(s.activation(H[:, k, :], Y[:, k, :], ACT.Silu, bias=vec("cf_ln_b", k), scale=vec("cf_ln_g", k)))
                dve(v.tensor_tensor(SM[:, 0:8], MOD[:, 1, 16:24, 0], vec("cf_b2", 0, 8), ALU.mult))
                for k in range(KD):
                    dve(v.tensor_scalar(X[:, k, :], X[:, k, :], SM[:, k:k + 1], None, ALU.add))
                g.fence()

                def ev(i, ps, e):
                    return dve(v.scalar_tensor_tensor(out=row(X, i), in0=ps,
                                                      scalar=MOD[:, 1, bass.ds(i + 16, 1), 0:1].rearrange("p a b -> p (a b)"),
                                                      in1=row(X, i), op0=ALU.mult, op1=ALU.add))

                project(KD, wblock("cf_w2"), lambda k: H[:, k, :], T, ev)

        def plain_norm(name, dst):
            rms_rows(lambda k: X[:, k, :], KD, T, EPS, R, D)
            for k in range(KD):
                dve(v.scalar_tensor_tensor(out=dst[:, k, :], in0=X[:, k, :], scalar=vec(name, k), in1=R[:, :],
                                           op0=ALU.mult, op1=ALU.mult))

        stages = a.get("stages", 99)
        adaln(0)
        layer0_mixer()
        if stages > 1:
            moe(0)
        if stages > 2:
            adaln(1)
            layer1_mixer()
        if stages > 3:
            moe(1)
        if stages > 4:
            plain_norm("final_g", X)
            second_block(g, a, X, H, R, SQ, W, SM, bank, project, wblock, softplus, rsqrt, plain_norm, dwconv)
            plain_norm("final_gain_2", X)
        g.fence()
        t = g.load(a["out"].rearrange("p (k t) -> p k t", k=KD), X[:, :, :], "out")
        wait("sp", t)
    return book.fresh


QKV, GZ, SU, SV, SZ, RK, RZ, NQ, NKV, NZ, NPROJ = 0, 6, 8, 10, 12, 14, 21, 23, 25, 28, 30


def second_block(g, a, X, H, R, SQ, W, SM, bank, project, wblock, softplus, rsqrt, plain_norm, dwconv):
    nc, book, wait, dve, act, pe, mm = g.nc, g.book, g.wait, g.dve, g.act, g.pe, g.mm
    v, s, tn = nc.vector, nc.scalar, nc.tensor
    vec, con = g.vec, g.con
    ident = con("ident")
    halves = [slice(0, 64), slice(64, 128)]
    outer = ExitStack()
    with outer:
        PJ = g.sb(outer, "proj2", [P, NPROJ, T])
        SL = g.sb(outer, "proj2_small", [96, T])
        YS = g.sb(outer, "mixer_out", [P, 8, T])
        g.fence()
        plain_norm("norm_gain_2", H)
        t = g.load(W[:, 0, :, 0:96], a["w_small"].rearrange("p (k c) -> p k c", c=96), "w0")
        wait("pe", t, g.latest["dve"])
        for k in range(KD):
            ins = mm(bank[0][0:96, :], W[:, 0, k, 0:96], H[:, k, :], k == 0, k == KD - 1)
        t = pe(ins)
        wait("dve", t)
        dve(v.tensor_copy(SL[:, :], bank[0][0:96, :]))
        g.fence()

        def ev(i, ps, e):
            return dve(v.tensor_copy(PJ[:, bass.ds(i, 1), :].rearrange("p o t -> p (o t)"), ps))

        project(NPROJ, wblock("w_in_2"), lambda k: H[:, k, :], T, ev)

        def head_sums(src, b):
            wait("pe", g.latest["dve"], g.latest["act"])
            t = pe(mm(bank[b][:, :], con("blk1"), src))
            wait("dve", t)
            return bank[b][:, :]

        def silu_into(dst, z):
            wait("act", g.latest["dve"])
            t = act(s.activation(z, z, ACT.Silu))
            wait("dve", t)
            dve(v.tensor_tensor(dst, dst, z, ALU.mult))

        def tile_products(b, left, right, after=()):
            wait("pe", g.latest["dve"], g.latest["act"])
            for n in range(NCH):
                for r in halves:
                    ins = mm(bank[b][r, n * CH:(n + 1) * CH], left[r, n * CH:(n + 1) * CH], right[r, n * CH:(n + 1) * CH])
            t = pe(ins)
            wait("dve", t)
            return bank[b][:, :]

        def to_rows(b, src, dst):
            wait("pe", g.latest["dve"], g.latest["act"])
            for n in range(NCH):
                for r in halves:
                    ins = mm(bank[b][r, n * CH:(n + 1) * CH], src[r, n * CH:(n + 1) * CH], con("i64")[r, :])
            t = pe(ins)
            wait("dve", t)
            dve(v.tensor_copy(dst, bank[b][:, :]))

        def masked(dst, ps, mask):
            dve(v.tensor_tensor(fm3(dst, NCH), fm3(ps, NCH), mask.unsqueeze(1).broadcast_to([P, NCH, CH]), ALU.mult))

        def last_of_chunk(x):
            return fm3(x, NCH)[:, :, CH - 1:CH].broadcast_to([P, NCH, CH])

        def delta(name, AT, TIL, QT, AQ, KH, lam, add, keys, out):
            with ExitStack() as st:
                TM_ = g.sb(st, name + "_inv", [P, 2, T])
                TT = g.sb(st, name + "_inv_t", [P, 2, T])
                MM_ = g.sb(st, name + "_lt_t", [P, 2, T])
                LT = g.sb(st, name + "_level", [P, 2, T])
                G = g.sb(st, name + "_state", [P, 2, HD])
                xr = g.sb(st, name + "_x", [P, 2, HD])
                ur = g.sb(st, name + "_u", [P, 2, HD])
                g.fence()
                for p in range(2):
                    dve(v.tensor_copy(TM_[:, p, :], con("eye64")))
                    dve(v.tensor_copy(TT[:, p, :], con("eye64")))
                g.fence()
                with book.run(LEVELS) as lv:
                    mask = g.C[:, bass.ds(lv * 64 + COFF["level"], 64)].unsqueeze(1).broadcast_to([P, NCH, CH])
                    for p in range(2):
                        wait("dve", book.before(f"m{p}", g.cnt["pe"]))
                        t_l = dve(v.tensor_tensor(fm3(LT[:, p, :], NCH), fm3(AT[:, p, :], NCH), mask, ALU.mult))
                        wait("pe", t_l)
                        g.take(bank[p])
                        for n in range(NCH):
                            c = slice(n * CH, (n + 1) * CH)
                            for r in halves:
                                ins = mm(bank[p][r, c], LT[r, p, c], TM_[r, p, c])
                        t = book.name(f"m{p}", pe(ins))
                        wait("act", t, book.before(f"t{p}", g.cnt["pe"]))
                        t_m = act(s.copy(MM_[:, p, :], bank[p][:, :]))
                        wait("pe", t_m)
                        g.take(bank[2 + p])
                        for n in range(NCH):
                            c = slice(n * CH, (n + 1) * CH)
                            for r in halves:
                                mm(bank[2 + p][r, c], TT[r, p, c], MM_[r, p, c])
                                ins = mm(bank[4 + p][r, c], MM_[r, p, c], TT[r, p, c])
                        t = book.name(f"t{p}", pe(ins))
                        wait("dve", t)
                        dve(v.tensor_tensor(TM_[:, p, :], TM_[:, p, :], bank[2 + p][:, :], ALU.add))
                        t = dve(v.tensor_tensor(TT[:, p, :], TT[:, p, :], bank[4 + p][:, :], ALU.add))
                g.settle()
                g.fence()
                dve(v.memset(G[:, :, :], 0.0))
                for n in range(NCH):
                    c = slice(n * CH, (n + 1) * CH)
                    wait("pe", g.latest["dve"])
                    for p in range(2):
                        o = slice(p * HD, (p + 1) * HD)
                        for r in halves:
                            if keys:
                                mm(bank[0][r, o], keys[0][r, p, c], keys[2][r, p, c], True, False)
                            ins = mm(bank[0][r, o], TIL[r, p, c], G[r, p, :], not keys, True)
                    t = pe(ins)
                    wait("dve", t)
                    x2, p2 = xr[:, :, :], bank[0][:, 0:2 * HD].rearrange("p (a d) -> p a d", a=2)
                    if keys:
                        dve(v.tensor_copy(x2, p2))
                    else:
                        dve(v.tensor_tensor(x2, p2, add[:, :, c], ALU.add))
                    wait("pe", g.latest["dve"])
                    for p in range(2):
                        for r in halves:
                            ins = mm(bank[1][r, p * HD:(p + 1) * HD], TT[r, p, c], xr[r, p, :])
                    t = pe(ins)
                    wait("dve", t)
                    dve(v.tensor_copy(ur[:, :, :], bank[1][:, 0:2 * HD].rearrange("p (a d) -> p a d", a=2)))
                    wait("pe", g.latest["dve"], g.latest["act"])
                    for p in range(2):
                        for r in halves:
                            mm(bank[2][r, p * CH:(p + 1) * CH], G[r, p, :], QT[r, p, c], True, False)
                            mm(bank[2][r, p * CH:(p + 1) * CH], ur[r, p, :], AQ[r, p, c], False, not keys)
                            if keys:
                                mm(bank[2][r, p * CH:(p + 1) * CH], keys[2][r, p, c], keys[1][r, p, c], False, True)
                            mm(bank[3][r, p * HD:(p + 1) * HD], KH[r, p, c], ur[r, p, :], True, not keys)
                            if keys:
                                mm(bank[3][r, p * HD:(p + 1) * HD], keys[3][r, p, c], keys[2][r, p, c], False, True)
                    t = pe(tn.matmul(bank[4][0:32, 0:32], ident[:, 0:32], ident[:, 0:32], start=True, stop=True))
                    wait("dve", t)
                    wait("act", t)
                    for p in range(2):
                        dve(v.scalar_tensor_tensor(out=G[:, p, :], in0=G[:, p, :], scalar=lam[:, p, n:n + 1],
                                                   in1=bank[3][:, p * HD:(p + 1) * HD], op0=ALU.mult, op1=ALU.add))
                        act(s.copy(out(p)[:, c], bank[2][:, p * CH:(p + 1) * CH]))
                g.fence()

        def deltanet():
            with ExitStack() as st:
                tiles = {n: g.sb(st, "gdn_" + n, [P, 2, T]) for n in ("at", "til", "qt", "aq", "kh", "bv")}
                lam = g.sb(st, "gdn_lam", [P, 2, NCH])
                B = g.sb(st, "gdn_gc", [P, T])
                BB = g.sb(st, "gdn_beta", [P, T])
                E = g.sb(st, "gdn_e", [P, T])
                DD = g.sb(st, "gdn_decay", [P, T])
                bc = g.sb(st, "gdn_col", [P, NCH])
                g.fence()
                for k in range(6):
                    dwconv(B, PJ[:, k, :], T, "gdn_conv_2", k, 6, 4, 3)
                    wait("act", g.latest["dve"])
                    act(s.activation(PJ[:, k, :], B[:, :], ACT.Silu))
                    wait("dve", g.latest["act"])
                for k in range(4):
                    dve(v.tensor_tensor(B[:, :], PJ[:, k, :], PJ[:, k, :], ALU.mult))
                    ps = head_sums(B[:, :], 0)
                    rsqrt(ps, 1.0, 1e-6, E[:, :])
                    dve(v.tensor_tensor(PJ[:, k, :], PJ[:, k, :], E[:, :], ALU.mult))
                    if k < 2:
                        dve(v.tensor_scalar(PJ[:, k, :], PJ[:, k, :], HD ** -0.5, None, ALU.mult))
                x, t1, t2, t3 = SL[0:4, :], B[0:4, :], BB[0:4, :], E[0:4, :]
                dve(v.tensor_scalar(x, x, vec("gdn_dt_bias_2", parts=4), None, ALU.add))
                softplus(x, t1, t2, t3)
                wait("act", g.latest["dve"])
                act(s.activation(SM[0:4, 0:1], vec("gdn_a_log_2", parts=4), ACT.Exp))
                act(s.activation(SL[32:36, :], SL[32:36, :], ACT.Sigmoid))
                wait("dve", g.latest["act"])
                dve(v.tensor_scalar(x, x, SM[0:4, 0:1], -1.0, ALU.mult, ALU.mult))
                dve(v.tensor_tensor_scan(t1, con("reset", p1=4), x, 0.0, ALU.mult, ALU.add))
                dve(v.tensor_copy(x, t1))
                for p in range(2):
                    q, k, val = PJ[:, p, :], PJ[:, 2 + p, :], PJ[:, 4 + p, :]
                    wait("pe", g.latest["dve"], g.latest["act"])
                    mm(bank[0][:, :], con("sela", p * P, P, 0, 4), SL[0:4, :])
                    t = pe(mm(bank[1][:, :], con("selb", p * P, P, 32, 36), SL[32:36, :]))
                    wait("dve", t)
                    dve(v.tensor_copy(B[:, :], bank[0][:, :]))
                    dve(v.tensor_copy(BB[:, :], bank[1][:, :]))
                    dve(v.tensor_tensor(fm3(E[:, :], NCH), fm3(B[:, :], NCH),
                                        con("i64").unsqueeze(1).broadcast_to([P, NCH, CH]), ALU.mult))
                    dve(v.tensor_reduce(bc[:, :], fm3(E[:, :], NCH), AXX, ALU.add))
                    dve(v.tensor_tensor(fm3(DD[:, :], NCH), fm3(B[:, :], NCH),
                                        bc[:, :].unsqueeze(2).broadcast_to([P, NCH, CH]), ALU.subtract))
                    dve(v.tensor_scalar(DD[:, :], DD[:, :], 0.0, None, ALU.min))
                    dve(v.tensor_tensor(fm3(E[:, :], NCH), last_of_chunk(B[:, :]), fm3(B[:, :], NCH), ALU.subtract))
                    wait("act", g.latest["dve"])
                    act(s.activation(DD[:, :], DD[:, :], ACT.Exp))
                    act(s.activation(E[:, :], E[:, :], ACT.Exp))
                    act(s.activation(B[:, :], B[:, :], ACT.Exp))
                    wait("dve", g.latest["act"])
                    dve(v.tensor_copy(lam[:, p, :], fm3(B[:, :], NCH)[:, :, CH - 1]))
                    dve(v.tensor_tensor(tiles["qt"][:, p, :], q, B[:, :], ALU.mult))
                    dve(v.scalar_tensor_tensor(out=tiles["til"][:, p, :], in0=k, scalar=-1.0, in1=B[:, :], op0=ALU.mult, op1=ALU.mult))
                    dve(v.tensor_tensor(tiles["til"][:, p, :], tiles["til"][:, p, :], BB[:, :], ALU.mult))
                    dve(v.tensor_tensor(E[:, :], E[:, :], k, ALU.mult))
                    to_rows(2, E[:, :], tiles["kh"][:, p, :])
                    dve(v.tensor_tensor(E[:, :], val, BB[:, :], ALU.mult))
                    to_rows(3, E[:, :], tiles["bv"][:, p, :])
                    ps = tile_products(4, k, k)
                    dve(v.tensor_tensor(E[:, :], ps, DD[:, :], ALU.mult))
                    dve(v.scalar_tensor_tensor(out=E[:, :], in0=E[:, :], scalar=-1.0, in1=BB[:, :], op0=ALU.mult, op1=ALU.mult))
                    masked(tiles["at"][:, p, :], E[:, :], con("strict"))
                    ps = tile_products(5, k, q)
                    dve(v.tensor_tensor(E[:, :], ps, DD[:, :], ALU.mult))
                    masked(tiles["aq"][:, p, :], E[:, :], con("incl"))
                delta("gdn", tiles["at"], tiles["til"], tiles["qt"], tiles["aq"], tiles["kh"], lam, tiles["bv"], None,
                      lambda p: YS[:, p, :])
                for p in range(2):
                    dve(v.tensor_tensor(B[:, :], YS[:, p, :], YS[:, p, :], ALU.mult))
                    ps = head_sums(B[:, :], 0)
                    rsqrt(ps, 1.0 / HD, EPS, E[:, :])
                    dve(v.scalar_tensor_tensor(out=YS[:, p, :], in0=YS[:, p, :], scalar=vec("gdn_norm_2"), in1=E[:, :],
                                               op0=ALU.mult, op1=ALU.mult))
                    silu_into(YS[:, p, :], PJ[:, GZ + p, :])
                g.fence()

        def head_norm(x, eps, tmp, r, b):
            ps = head_sums(x, b)
            dve(v.scalar_tensor_tensor(out=x, in0=ps, scalar=-1.0 / HD, in1=x, op0=ALU.mult, op1=ALU.add))
            dve(v.tensor_tensor(tmp, x, x, ALU.mult))
            ps = head_sums(tmp, b + 1)
            rsqrt(ps, 1.0 / HD, eps, r)
            dve(v.tensor_tensor(x, x, r, ALU.mult))

        def rwkv():
            with ExitStack() as st:
                tiles = {n: g.sb(st, "rw_" + n, [P, 2, T]) for n in ("at", "til", "qt", "aq", "kh", "aak", "ark", "v", "kv")}
                lam = g.sb(st, "rw_lam", [P, 2, NCH])
                up = g.sb(st, "rw_up", [P, 256])
                g.fence()
                t = g.load(up[:, :], a["rw_up"], "rwup")
                wait("pe", t)
                z = [PJ[:, k, :] for k in range(6)]
                for k in range(7):
                    x = PJ[:, RK + k, :]
                    dve(v.tensor_tensor(z[0][:, 1:T], x[:, 0:T - 1], x[:, 1:T], ALU.subtract))
                    dve(v.tensor_scalar(z[0][:, 0:1], x[:, 0:1], -1.0, None, ALU.mult))
                    dve(v.scalar_tensor_tensor(out=x, in0=z[0], scalar=vec("rw_mu_2", k), in1=x, op0=ALU.mult, op1=ALU.add))
                wa = PJ[:, RK + 6, :]
                wait("act", g.latest["dve"])
                act(s.activation(wa[0:64, :], wa[0:64, :], ACT.Tanh))
                for p in range(2):
                    r, k, val = PJ[:, RK + p, :], PJ[:, RK + 2 + p, :], PJ[:, RK + 4 + p, :]
                    wait("pe", g.latest["act"], g.latest["dve"])
                    mm(bank[0][:, :], up[0:64, p * P:(p + 1) * P], wa[0:64, :])
                    t = pe(mm(bank[1][:, :], up[64:128, p * P:(p + 1) * P], wa[64:128, :]))
                    wait("act", t)
                    lw, L, aa, kk, e = z[0], z[1], z[2], z[3], R[:, :]
                    act(s.activation(lw, bank[0][:, :], ACT.Sigmoid, bias=vec("rw_w0_2", p)))
                    act(s.activation(aa, bank[1][:, :], ACT.Sigmoid, bias=vec("rw_a0_2", p)))
                    wait("dve", g.latest["act"])
                    dve(v.tensor_scalar(lw, lw, -math.exp(-0.5), None, ALU.mult))
                    dve(v.tensor_tensor_scan(L, con("reset"), lw, 0.0, ALU.mult, ALU.add))
                    dve(v.tensor_scalar(kk, k, vec("rw_k_k_2", p), None, ALU.mult))
                    dve(v.tensor_tensor(e, kk, kk, ALU.mult))
                    ps = head_sums(e, 2)
                    rsqrt(ps, 1.0, 1e-6, e)
                    dve(v.tensor_tensor(kk, kk, e, ALU.mult))
                    dve(v.tensor_scalar(e, aa, 1.0, vec("rw_k_a_2", p), ALU.subtract, ALU.mult))
                    dve(v.scalar_tensor_tensor(out=k, in0=e, scalar=1.0, in1=k, op0=ALU.add, op1=ALU.mult))
                    dve(v.tensor_tensor(aa, aa, kk, ALU.mult))
                    dve(v.scalar_tensor_tensor(out=e, in0=r, scalar=vec("rw_r_k_2", p), in1=k, op0=ALU.mult, op1=ALU.mult))
                    ps = head_sums(e, 3)
                    dve(v.tensor_tensor(z[4 + p], ps, val, ALU.mult))
                    dve(v.tensor_tensor(lw, L, lw, ALU.subtract))
                    wait("act", g.latest["dve"])
                    act(s.activation(lw, lw, ACT.Exp))
                    act(s.activation(e, L, ACT.Exp))
                    wait("dve", g.latest["act"])
                    dve(v.scalar_tensor_tensor(out=tiles["til"][:, p, :], in0=kk, scalar=-1.0, in1=lw, op0=ALU.mult, op1=ALU.mult))
                    dve(v.tensor_tensor(tiles["qt"][:, p, :], r, e, ALU.mult))
                    dve(v.tensor_copy(lam[:, p, :], fm3(e, NCH)[:, :, CH - 1]))
                    dve(v.tensor_tensor(fm3(lw, NCH), last_of_chunk(L), fm3(L, NCH), ALU.subtract))
                    wait("act", g.latest["dve"])
                    act(s.activation(lw, lw, ACT.Exp))
                    act(s.activation(L, L, ACT.Exp, scale=-1.0))
                    wait("dve", g.latest["act"])
                    dve(v.tensor_tensor(e, aa, lw, ALU.mult))
                    to_rows(4, e, tiles["kh"][:, p, :])
                    dve(v.tensor_tensor(e, k, lw, ALU.mult))
                    to_rows(5, e, tiles["kv"][:, p, :])
                    to_rows(6, val, tiles["v"][:, p, :])
                    dve(v.tensor_tensor(aa, aa, L, ALU.mult))
                    dve(v.tensor_tensor(k, k, L, ALU.mult))
                    masked(tiles["at"][:, p, :], tile_products(7, aa, tiles["til"][:, p, :]), con("strict"))
                    masked(tiles["aak"][:, p, :], tile_products(0, k, tiles["til"][:, p, :]), con("strict"))
                    masked(tiles["aq"][:, p, :], tile_products(1, aa, tiles["qt"][:, p, :]), con("incl"))
                    masked(tiles["ark"][:, p, :], tile_products(2, k, tiles["qt"][:, p, :]), con("incl"))
                    g.fence()
                delta("rw", tiles["at"], tiles["til"], tiles["qt"], tiles["aq"], tiles["kh"], lam, None,
                      (tiles["aak"], tiles["ark"], tiles["v"], tiles["kv"]), lambda p: YS[:, 4 + p, :])
                for p in range(2):
                    y = YS[:, 4 + p, :]
                    head_norm(y, 64e-5, z[0], R[:, :], 0)
                    dve(v.tensor_scalar(y, y, vec("rw_gn_gain_2", p), vec("rw_gn_bias_2", p), ALU.mult, ALU.add))
                    dve(v.tensor_tensor(y, y, z[4 + p], ALU.add))
                    silu_into(y, PJ[:, RZ + p, :])
                g.fence()

        def spatial():
            with ExitStack() as st:
                ws = g.sb(st, "sg_w", [P, 4, P])
                bs = g.sb(st, "sg_b", [1, 4, P])
                vt = g.sb(st, "sg_v", [P, 4, 256])
                tmp = g.sb(st, "sg_tmp", [P, T])
                g.fence()
                t1 = g.load(ws[:, :, :], a["sg_w"].rearrange("p (g t) -> p g t", g=4), "sgw")
                t2 = g.load(bs[:, :, :], a["sg_b"].rearrange("o (g t) -> o g t", g=4), "sgb")
                wait("dve", t1)
                wait("pe", t2)
                dve(v.tensor_tensor(ws[:, :, :], ws[:, :, :], con("tril").unsqueeze(1).broadcast_to([P, 4, P]), ALU.mult))
                for k in range(2):
                    act(s.activation(PJ[:, SU + k, :], PJ[:, SU + k, :], ACT.Gelu_apprx_tanh))
                    act(s.activation(PJ[:, SV + k, :], PJ[:, SV + k, :], ACT.Gelu_apprx_tanh))
                wait("dve", g.latest["act"])
                for k in range(2):
                    x = PJ[:, SV + k, :]
                    head_norm(x, 1e-5, tmp[:, :], R[:, :], 0)
                    dve(v.tensor_scalar(x, x, vec("sg_ln_gain_2", k), vec("sg_ln_bias_2", k), ALU.mult, ALU.add))
                wait("pe", g.latest["dve"])
                for n in range(NT):
                    for k in range(2):
                        ins = tn.transpose(bank[2 + n % 2][:, k * P:(k + 1) * P], PJ[:, SV + k, n * P:(n + 1) * P], ident)
                    t = pe(ins)
                    wait("dve", t)
                    dve(v.tensor_copy(vt[:, n, :], bank[2 + n % 2][:, 0:256]))
                    wait("pe", g.latest["dve"])
                for k in range(2):
                    b = bank[4 + k]
                    for n in range(NT):
                        for j, r in enumerate(halves):
                            o = b[r, n * P:(n + 1) * P]
                            mm(o, vt[:, n, (2 * k + j) * 64:(2 * k + j + 1) * 64], ws[:, 2 * k + j, :], True, False)
                            ins = mm(o, con("ones", 0, 64, 0, 1), bs[:, 2 * k + j, :], False, True)
                    t = pe(tn.matmul(bank[6][0:32, 0:32], ident[:, 0:32], ident[:, 0:32], start=True, stop=True))
                    wait("dve", t)
                    y = YS[:, 2 + k, :]
                    dve(v.tensor_tensor(y, PJ[:, SU + k, :], b[:, :], ALU.mult))
                    silu_into(y, PJ[:, SZ + k, :])
                g.fence()

        def attention():
            NS = 512 + 384 + 32
            with ExitStack() as st:
                ks = g.sb(st, "ks", [P, T])
                kw = g.sb(st, "kw", [P, T])
                kc = g.sb(st, "kc", [P, 32])
                vs = g.sb(st, "vs", [P, NT, 2, HD])
                vc = g.sb(st, "vc", [32, HD])
                gt = g.sb(st, "gates", [P, NT, 12])
                cw = g.sb(st, "cmp_w1", [P, 32, HD])
                cw2 = g.sb(st, "cmp_w2", [P, HD])
                cp = g.sb(st, "cmp_pos", [P, 32])
                xc = g.sb(st, "cmp_x", [P, 32, NCMP])
                hc = g.sb(st, "cmp_h", [P, 32])
                nb = g.sb(st, "cmp_fill", [P, 4, 32])
                ps_ = g.sb(st, "scores", [P, 4, NS])
                pt = g.sb(st, "scores_t", [P, 2, 8 * P])
                ms = g.sb(st, "softmax", [P, 2, 12])
                g.fence()
                t = [g.load(cw[:, :, :], a["cmp_w1"].rearrange("p (j h) -> p j h", j=32), "cw1"),
                     g.load(cw2[:, :], a["cmp_w2"], "cw2"), g.load(cp[:, :], a["cmp_pos"], "cpos")]
                wait("pe", *t)
                wait("dve", *t)
                KC_, KS_, KW_ = (PJ[:, NKV + i, :] for i in range(3))
                for dst, src in ((ks, KS_), (kw, KW_)):
                    dve(v.tensor_copy(dst[0:64, :], src[0:64, :]))
                    dve(v.tensor_copy(dst[64:128, :], src[0:64, :]))
                for k in range(2):
                    dve(v.tensor_scalar(PJ[:, NQ + k, :], PJ[:, NQ + k, :], HD ** -0.5, None, ALU.mult))
                wait("act", g.latest["dve"])
                act(s.activation(SL[64:96, :], SL[64:96, :], ACT.Sigmoid))
                wait("pe", g.latest["dve"], g.latest["act"])
                for n in range(NT):
                    for q, src in enumerate((KS_, KW_)):
                        tn.transpose(bank[n][:, q * P:(q + 1) * P], src[:, n * P:(n + 1) * P], ident)
                    ins = tn.transpose(bank[n][:, 256:352], SL[:, n * P:(n + 1) * P], ident[0:96, 0:96])
                t = pe(ins)
                wait("dve", t)
                for n in range(NT):
                    dve(v.tensor_copy(vs[:, n, :, :], bank[n][:, 0:256].rearrange("p (q c) -> p q c", q=2)[:, :, 64:128]))
                    dve(v.tensor_copy(gt[:, n, :], bank[n][:, 320:332]))
                for h in range(2):
                    src = KC_[:, 16 * h:16 * h + 16 * NCMP].rearrange("p (n j) -> p j n", j=16)
                    dve(v.tensor_tensor(xc[:, 16 * h:16 * h + 16, :], src,
                                        cp[:, 16 * h:16 * h + 16].unsqueeze(2).broadcast_to([P, 16, NCMP]), ALU.add))
                wait("pe", g.latest["dve"])
                for r in halves:
                    for j in range(32):
                        mm(bank[4][r, 0:NCMP], cw[r, j, :], xc[r, j, :], j == 0, j == 31)
                t = pe(tn.matmul(bank[5][0:32, 0:32], ident[:, 0:32], ident[:, 0:32], start=True, stop=True))
                wait("act", t)
                act(s.activation(hc[:, 0:NCMP], bank[4][:, 0:NCMP], ACT.Gelu_apprx_tanh))
                wait("pe", g.latest["act"])
                for r in halves:
                    mm(bank[6][r, 0:NCMP], cw2[0:64, :], hc[0:64, 0:NCMP])
                mm(bank[7][0:NCMP, 0:HD], hc[64:128, 0:NCMP], cw2[64:128, :])
                t = pe(tn.matmul(bank[5][0:32, 0:32], ident[:, 0:32], ident[:, 0:32], start=True, stop=True))
                wait("dve", t)
                dve(v.tensor_copy(kc[:, 0:NCMP], bank[6][:, 0:NCMP]))
                dve(v.tensor_copy(vc[0:NCMP, :], bank[7][0:NCMP, 0:HD]))
                cm = con("cmask").rearrange("p (q n) -> p q n", q=4)
                cd = con("cdist").rearrange("p (q n) -> p q n", q=4)
                dve(v.tensor_scalar(nb[:, :, :], cm, BIG, -BIG, ALU.mult, ALU.add))
                g.fence()
                for c in range(NT):
                    n1, n2 = c + 1, min(c + 1, 3)
                    wait("pe", g.latest["dve"], g.latest["act"])
                    for h in range(4):
                        r = halves[h % 2]
                        q = PJ[r, NQ + h // 2, c * P:(c + 1) * P]
                        mm(bank[2 * h][:, 0:n1 * P], q, ks[r, 0:n1 * P])
                        mm(bank[2 * h + 1][:, 0:n2 * P], q, kw[r, (c + 1 - n2) * P:(c + 1) * P])
                        ins = mm(bank[2 * h + 1][:, 384:384 + NCMP], q, kc[r, 0:NCMP])
                    t = pe(tn.matmul(bank[7][0:32, 448:480], ident[:, 0:32], ident[:, 0:32], start=True, stop=True))
                    wait("dve", t)
                    spans = [(0, n1 * P), (512, 512 + n2 * P), (896, 896 + NCMP)]
                    for h in range(4):
                        dst = ps_[:, h, :]
                        dve(v.scalar_tensor_tensor(out=dst[:, 0:n1 * P], in0=con("dist", 384 - P * c), scalar=-SLOPES[h],
                                                   in1=bank[2 * h][:, 0:n1 * P], op0=ALU.mult, op1=ALU.add))
                        dve(v.scalar_tensor_tensor(out=dst[:, 512:512 + n2 * P], in0=con("distw", 384 - P * n2), scalar=-SLOPES[h],
                                                   in1=bank[2 * h + 1][:, 0:n2 * P], op0=ALU.mult, op1=ALU.add))
                        x = dst[:, 896:896 + NCMP]
                        dve(v.scalar_tensor_tensor(out=x, in0=cd[:, c, 0:NCMP], scalar=-SLOPES[h],
                                                   in1=bank[2 * h + 1][:, 384:384 + NCMP], op0=ALU.mult, op1=ALU.add))
                        dve(v.tensor_tensor(x, x, cm[:, c, 0:NCMP], ALU.mult))
                        dve(v.tensor_tensor(x, x, nb[:, c, 0:NCMP], ALU.add))
                        for b, (lo, hi) in enumerate(spans):
                            dve(v.tensor_reduce(ms[:, 0, 3 * h + b:3 * h + b + 1], dst[:, lo:hi], AXX, ALU.max, negate=True))
                        wait("act", g.latest["dve"])
                        for b, (lo, hi) in enumerate(spans):
                            i = 3 * h + b
                            act(s.activation(dst[:, lo:hi], dst[:, lo:hi], ACT.Exp, bias=ms[:, 0, i:i + 1], accum_out=ms[:, 1, i:i + 1]))
                    wait("dve", g.latest["act"])
                    dve(v.reciprocal(ms[:, 1, :], ms[:, 1, :]))
                    go = ms[:, 0, :]
                    order = (1, 2, 0)
                    for h in range(4):
                        for b in range(3):
                            i = 3 * h + b
                            dve(v.tensor_tensor(ms[:, 0, i:i + 1], ms[:, 1, i:i + 1],
                                                gt[:, c, 3 * h + order[b]:3 * h + order[b] + 1], ALU.mult))
                    for h in range(4):
                        dst = ps_[:, h, :]
                        for b, (lo, hi) in enumerate(spans):
                            i = 3 * h + b
                            dve(v.tensor_scalar(dst[:, lo:hi], dst[:, lo:hi], ms[:, 0, i:i + 1], None, ALU.mult))
                        dve(v.tensor_tensor(dst[:, 896:896 + NCMP], dst[:, 896:896 + NCMP], cm[:, c, 0:NCMP], ALU.mult))
                        wait("pe", g.latest["dve"])
                        blocks = [(j * P, P, vs[:, j, 0, :]) for j in range(n1)]
                        blocks += [(512 + j * P, P, vs[:, c + 1 - n2 + j, 1, :]) for j in range(n2)]
                        blocks += [(896, NCMP, vc[0:NCMP, :])]
                        bb = [bank[(2 * h) % 4], bank[(2 * h) % 4 + 1]]
                        for j, (o, w, _) in enumerate(blocks):
                            ins = tn.transpose(bb[j // 4][0:w, (j % 4) * P:(j % 4 + 1) * P], ps_[:, h, o:o + w], ident)
                        t = pe(ins)
                        wait("act", t)
                        nbk = len(blocks)
                        for j in range(0, nbk - 1, 4):
                            m = min(4, nbk - 1 - j)
                            act(s.copy(pt[:, h % 2, j * P:(j + m) * P], bb[j // 4][:, 0:m * P]))
                        j = nbk - 1
                        act(s.copy(pt[0:NCMP, h % 2, j * P:(j + 1) * P], bb[j // 4][0:NCMP, (j % 4) * P:(j % 4 + 1) * P]))
                        wait("pe", g.latest["act"])
                        ob = bank[4 + h // 2]
                        for j, (o, w, val) in enumerate(blocks):
                            ins = mm(ob[halves[h % 2], 0:P], val, pt[0:w, h % 2, j * P:(j + 1) * P], j == 0, j == nbk - 1)
                        t = pe(ins)
                        if h % 2:
                            wait("act", t)
                            act(s.copy(YS[:, 6 + h // 2, c * P:(c + 1) * P], ob[:, 0:P]))
                    g.fence()
                for k in range(2):
                    silu_into(YS[:, 6 + k, :], PJ[:, NZ + k, :])
                g.fence()

        spatial()
        deltanet()
        rwkv()
        attention()
        with ExitStack() as st:
            mix = g.sb(st, "mixed", [P, KD, T])
            wm = g.sb(st, "merge_w", [P, 5, KD, P])
            sg = g.sb(st, "merge_g", [P, 4, T])
            g.fence()
            with book.run(KD) as m:
                cpe, cdve, cact = g.cnt["pe"], g.cnt["dve"], g.cnt["act"]
                tw = []
                for q in range(5):
                    wait("sp", book.before(f"mw{q}", cpe))
                    src = wblock("w_in_2")(m + NPROJ + 8 * q) if q < 4 else wblock("w_branch")(m)
                    tw.append(g.load(wm[:, q, :, :], src, f"merge{q}"))
                for q in range(4):
                    wait("pe", tw[q], book.before(f"mg{q}", cact))
                    for k in range(KD):
                        ins = mm(bank[q][:, :], wm[:, q, k, :], H[:, k, :], k == 0, k == KD - 1)
                    t = book.name(f"mw{q}", pe(ins))
                    wait("act", t, book.before(f"ms{q}", cdve))
                    book.name(f"mg{q}", act(s.activation(sg[:, q, :], bank[q][:, :], ACT.Sigmoid)))
                wait("pe", tw[4])
                t_y = []
                for q in range(4):
                    wait("pe", book.before(f"ms{q}", cdve))
                    for k in range(2):
                        ins = mm(bank[4 + q][:, :], wm[:, 4, 2 * q + k, :], YS[:, 2 * q + k, :], k == 0, k == 1)
                    t_y.append(pe(ins))
                book.name("mw4", t_y[-1])
                wait("dve", g.latest["act"])
                row = mix[:, bass.ds(m, 1), :].rearrange("p o t -> p (o t)")
                for q in range(4):
                    wait("dve", t_y[q])
                    if q == 0:
                        t = dve(v.tensor_tensor(row, sg[:, 0, :], bank[4][:, :], ALU.mult))
                    else:
                        t = dve(v.tensor_tensor(sg[:, q, :], sg[:, q, :], bank[4 + q][:, :], ALU.mult))
                        t = dve(v.tensor_tensor(row, row, sg[:, q, :], ALU.add))
                    book.name(f"ms{q}", t)
            g.settle()
            g.fence()

            def ev_out(i, ps, e):
                xi = X[:, bass.ds(i, 1), :].rearrange("p o t -> p (o t)")
                return dve(v.tensor_tensor(xi, ps, xi, ALU.add))

            project(KD, wblock("w_out_2"), lambda k: mix[:, k, :], T, ev_out)


def columns(x):
    return np.ascontiguousarray(x).reshape(-1, P).T


def weight_blocks(w):
    k, n = w.shape
    return np.ascontiguousarray(w.reshape(k // P, P, n // P, P).transpose(2, 1, 0, 3).reshape(n // P, P, -1))


def feature_major(x):
    t, d = x.shape
    return np.ascontiguousarray(x.T.reshape(d // P, P, t).transpose(1, 0, 2).reshape(P, -1))


def arrange(inp):
    A = {k: np.asarray(x) for k, x in inp.items()}
    vecs = np.zeros((P, NVEC), np.float32)
    for name, w in VEC:
        o = VOFF[name]
        if name in ("filt_freq0", "filt_freq1"):
            vecs[:FHID, o] = A["filt_freq"][0, int(name[-1])]
        elif name in ("filt_b1", "filt_b2"):
            vecs[:FHID, o] = A[name][0]
        elif name in ("gdn_a_log_2", "gdn_dt_bias_2"):
            vecs[:4, o] = A[name][0]
        elif name == "gdn_norm_2":
            vecs[:64, o] = A[name][0]
            vecs[64:, o] = A[name][0]
        else:
            vecs[:, o:o + w] = columns(A[name])
    f = {"vecs": vecs, "consts": shape_constants()}
    f["dft"], f["idft"], f["filt_z"], f["window"] = dft_constants()
    f["x_fm"] = feature_major(A["x"][0])
    f["ctx_fm"] = feature_major(A["ctx"][0])
    f["w_mod"] = A["w_mod"]
    f["w_in"] = weight_blocks(A["w_in"][0])
    lw = np.stack([A["lru_wr"][0], A["lru_wi"][0]], 2).reshape(2, 4, 2, 2, 64, 64)
    f["lru_w"] = np.ascontiguousarray(lw.transpose(2, 4, 0, 1, 3, 5).reshape(2, 64, 16, 64))
    f["filt_w1"], f["filt_w2"], f["filt_w3"], f["filt_b3"] = (A["filt_w1"][0], A["filt_w2"][0], A["filt_w3"][0],
                                                             A["filt_b3"][0:1])
    for n in ("w_out", "cf_w1", "cf_w2", "w_out_2"):
        f[n] = weight_blocks(A[n][0])
    f["router"] = np.ascontiguousarray(A["router"].reshape(2, KD, P, NE).transpose(0, 2, 1, 3).reshape(2, P, -1))
    for n in ("exp_w1", "exp_w3", "exp_w2"):
        f[n] = A[n]
    w2 = A["w_in_2"][0]
    cols = np.r_[0:768, 776:3592, 3604:7956]
    f["w_in_2"] = weight_blocks(w2[:, cols])
    small = np.zeros((D, 96), np.float32)
    small[:, 0:4], small[:, 32:36], small[:, 64:76] = w2[:, 768:772], w2[:, 772:776], w2[:, 3592:3604]
    f["w_small"] = np.ascontiguousarray(small.reshape(KD, P, 96).transpose(1, 0, 2).reshape(P, -1))
    f["rw_up"] = np.concatenate([A["rw_w_up_2"][0], A["rw_a_up_2"][0]], 0)
    f["sg_w"] = np.ascontiguousarray(A["sg_w_s_2"][0].transpose(2, 0, 1).reshape(P, -1))
    f["sg_b"] = A["sg_b_s_2"][0].reshape(1, -1)
    f["cmp_w1"] = np.ascontiguousarray(A["nsa_cmp_w1_2"][0].reshape(2, 32, 64, 64).transpose(0, 2, 1, 3).reshape(P, -1))
    f["cmp_w2"] = A["nsa_cmp_w2_2"][0].reshape(P, 64)
    f["cmp_pos"] = np.ascontiguousarray(A["nsa_cmp_pos_2"][0].transpose(0, 2, 1).reshape(P, 32))
    f["w_branch"] = weight_blocks(A["w_branch_2"][0].reshape(D, D))
    return {k: np.ascontiguousarray(x) for k, x in f.items()}


def program(make, shapes):
    plan = {}
    for _ in range(2):
        nc = make()
        a = {n: nc.dram_tensor("in_" + n, shape, F32, kind="ExternalInput").ap() for n, shape in shapes.items()}
        a["out"] = nc.dram_tensor("out_0", (P, KD * T), F32, kind="ExternalOutput").ap()
        plan, before = build(nc, a, plan), plan
    assert plan == before
    return nc


def kernel(**inputs):
    import concourse.bacc as bacc
    from concourse.bass_utils import run_bass_kernel_spmd

    f = arrange(inputs)
    nc = program(lambda: bacc.Bacc("TRN2", target_bir_lowering=False, num_devices=1), {n: x.shape for n, x in f.items()})
    r = run_bass_kernel_spmd(nc, [{"in_" + n: x for n, x in f.items()}], core_ids=[0])
    out = r.results[0]["out_0"].reshape(P, KD, T)
    return np.ascontiguousarray(out.transpose(2, 1, 0).reshape(1, T, D))
```

```python
import math
from contextlib import ExitStack, contextmanager

import numpy as np

import concourse.bass as bass
from concourse import mybir

F32 = mybir.dt.float32
ALU = mybir.AluOpType
ACT = mybir.ActivationFunctionType
AXX = mybir.AxisListType.X

P = 128
T = 512
D = 1024
KD = D // P
NT = T // P
TC = 256
NE = 16
CAP = 2 * T // NE
FF = 1024
RW = 512
KR = RW // P
HD = 64
CH = 64
NCH = T // CH
LRU_C = 8.0
EPS = 1e-6
GRID_W = 64
CF_K = 31
NMOD = 6
FEMB, FHID = 33, 64
BIG = 1e30
NCMP = T // 16 - 1
SLOPES = [2.0 ** (-8.0 * (h + 1) / 4) for h in range(4)]
NRING = 12
LEVELS = 6

VEC = [("norm1_g", 16), ("norm2_g", 16), ("b_mod", 96), ("conv_a_w", 16), ("conv_a_b", 4),
       ("lru_br", 8), ("lru_bi", 8), ("lru_lam", 8), ("conv_b_w", 36), ("conv_b_b", 12),
       ("filt_bias", 8), ("cf_b1", 16), ("cf_dw_w", CF_K * 8), ("cf_dw_b", 8), ("cf_ln_g", 8),
       ("cf_ln_b", 8), ("cf_b2", 8), ("final_g", 8), ("norm_gain_2", 8), ("gdn_conv_2", 24),
       ("sg_ln_gain_2", 2), ("sg_ln_bias_2", 2), ("rw_mu_2", 7), ("rw_w0_2", 2), ("rw_a0_2", 2),
       ("rw_k_k_2", 2), ("rw_k_a_2", 2), ("rw_r_k_2", 2), ("rw_gn_gain_2", 2), ("rw_gn_bias_2", 2),
       ("final_gain_2", 8), ("c", 8), ("c_ctx", 8),
       ("gdn_norm_2", 1), ("filt_b1", 1), ("filt_b2", 1), ("filt_freq0", 1), ("filt_freq1", 1),
       ("gdn_a_log_2", 1), ("gdn_dt_bias_2", 1)]
VOFF, _n = {}, 0
for _name, _w in VEC:
    VOFF[_name] = _n
    _n += _w
NVEC = _n

CONST = [("ident", 128), ("ones", 128), ("blk1", 128), ("i64", 64), ("strict", 64), ("incl", 64),
         ("level", LEVELS * 64), ("eye64", 512), ("reset", 512), ("sela", 256), ("selb", 256),
         ("iota", 128), ("dist", 512), ("distw", 384), ("cdist", 4 * 32), ("cmask", 4 * 32),
         ("tril", 128), ("pi", 1)]
COFF, _n = {}, 0
for _name, _w in CONST:
    COFF[_name] = _n
    _n += _w
NCONST = _n


def shape_constants():
    c = np.zeros((P, NCONST), np.float32)
    p = np.arange(P)[:, None]

    def put(name, a):
        c[:a.shape[0], COFF[name]:COFF[name] + a.shape[1]] = a

    t64 = np.arange(64)[None, :]
    put("ident", np.eye(P))
    put("ones", np.ones((P, P)))
    put("blk1", (p // 64 == np.arange(P)[None, :] // 64) * 1.0)
    put("i64", (p % 64 == t64) * 1.0)
    put("strict", (p % 64 < t64) * 1.0)
    put("incl", (p % 64 <= t64) * 1.0)
    put("level", np.concatenate([((t64 // b) % 2 == 1) * ((p % 64) // b == t64 // b - 1) * 1.0
                                 for b in (1 << i for i in range(LEVELS))], 1))
    put("eye64", np.tile((p % 64 == t64) * 1.0, (1, 8)))
    put("reset", np.tile((np.arange(T) % CH != 0)[None, :] * 1.0, (P, 1)))
    sel = np.zeros((4, 2, P))
    for h in range(4):
        sel[h, h // 2, 64 * (h % 2):64 * (h % 2) + 64] = 1.0
    put("sela", sel.reshape(4, 256))
    c[32:36, COFF["selb"]:COFF["selb"] + 256] = sel.reshape(4, 256)
    put("iota", np.tile(np.arange(P)[None, :] % 64, (P, 1)))
    m = np.arange(512)[None, :]
    d = p + 384 - m
    put("dist", np.where(d >= 0, d, BIG))
    m = np.arange(384)[None, :]
    d = p + 256 - m
    put("distw", np.where((d >= 0) & (d < 256), d, BIG))
    cd, cm = np.zeros((P, 4, 32)), np.zeros((P, 4, 32))
    for q in range(4):
        d = (128 * q + p) - (16 * np.arange(32)[None, :] + 31)
        cm[:, q] = (d >= 0) & (np.arange(32)[None, :] < NCMP)
        cd[:, q] = d * cm[:, q]
    put("cdist", cd.reshape(P, -1))
    put("cmask", cm.reshape(P, -1))
    put("tril", (p <= np.arange(P)[None, :]) * 1.0)
    put("pi", np.full((P, 1), math.pi))
    return c


def dft_constants():
    k, t = np.arange(T), np.arange(T)
    ang = 2 * np.pi * np.outer(t, k) / (2 * T)
    fwd = np.concatenate([np.cos(ang), -np.sin(ang)], 1)
    fwd[:, T] = (-1.0) ** t
    inv = np.concatenate([2 * np.cos(ang.T), -2 * np.sin(ang.T)], 0) / (2 * T)
    inv[0] = 1.0 / (2 * T)
    inv[T] = (-1.0) ** t / (2 * T)
    fwd = fwd.reshape(NT, P, 2 * T).transpose(1, 0, 2).reshape(P, -1)
    inv = inv.reshape(2 * NT, P, T).transpose(1, 0, 2).reshape(P, -1)
    tt = np.linspace(0.0, 1.0, T)[:, None]
    bands = (FEMB - 1) // 2
    w = (2.0 * math.pi / T) * np.arange(T)[:, None]
    f = np.linspace(1e-4, bands - 1, bands)[None, :]
    z = np.concatenate([tt, np.cos(f * w), -np.sin(f * w)], -1)
    deltas = np.abs(np.linspace(math.log(1e-2) / 1.5, math.log(1e-2) / 0.3, RW))
    win = np.exp(-tt * deltas[None, :]) + 0.05
    win = win.reshape(NT, P, RW).transpose(1, 0, 2).reshape(P, -1)
    return [np.ascontiguousarray(a.astype(np.float32)) for a in (fwd, inv, z.T, win)]


class Token:

    def __init__(self, sem, value, loop=None, owner=None):
        self.sem, self.value, self.loop, self.owner = sem, value, loop, owner


class Counter:

    def __init__(self, book, name, step=1):
        self.book, self.name, self.step = book, name, step
        self.sem = book.nc.alloc_semaphore(name)
        self.count = 0

    def mark(self, ins):
        ins.then_inc(self.sem, self.step)
        self.count += self.step
        return Token(self, self.count, self.book.loop)


class Book:

    def __init__(self, nc, plan):
        self.nc, self.plan, self.loop = nc, plan, None
        self.counters = {}
        self.loops = 0
        self.names = {}
        self.fresh = {}

    def counter(self, name, step=1):
        if name not in self.counters:
            self.counters[name] = Counter(self, name, step)
        return self.counters[name]

    @contextmanager
    def run(self, n):
        lid = f"loop{self.loops}"
        self.loops += 1
        base = {k: c.count for k, c in self.counters.items()}
        per = self.plan.get(lid, {})
        with self.nc.Fori(0, n) as i:
            self.loop = (lid, i, base, per)
            self.names = {}
            yield i
            self.loop = None
        seen = {k: c.count - base.get(k, 0) for k, c in self.counters.items()}
        self.fresh[lid] = dict(seen, marks={k: t.value - base.get(t.sem.name, 0) for k, t in self.names.items()})
        for k, c in self.counters.items():
            c.count = base.get(k, 0) + n * seen[k]
        self.last = (lid, base, seen, n)

    def after(self, tok):
        lid, base, seen, n = self.last
        return Token(tok.sem, tok.value + (n - 1) * seen[tok.sem.name])

    def value(self, tok):
        if tok.loop is None:
            return tok.value
        lid, i, base, per = tok.loop
        assert self.loop is not None and self.loop[0] == lid
        return i * per.get(tok.sem.name, 0) + tok.value

    def name(self, key, tok):
        self.names[key] = tok
        return tok

    def later(self, key, counter):
        lid, i, base, per = self.loop
        return Token(counter, base.get(counter.name, 0) + per.get("marks", {}).get(key, 1), self.loop)

    def before(self, key, counter):
        lid, i, base, per = self.loop
        rise = per.get(counter.name, 0)
        off = per.get("marks", {}).get(key, 0)
        start = base.get(counter.name, 0)
        assert start - rise + off > 0 or not per, (key, start, rise)
        return Token(counter, start - rise + off, self.loop)


class Program:
    def __init__(self, nc, a, plan):
        self.nc, self.a = nc, a
        self.book = Book(nc, plan)
        b = self.book
        self.eng = {"pe": nc.tensor, "dve": nc.vector, "act": nc.scalar, "pool": nc.gpsimd, "sp": nc.sync}
        self.cnt = {k: b.counter(f"{k}_done") for k in self.eng}
        self.latest = {k: None for k in self.eng}
        self.background = None
        self.bank_free = {5: None}

    def wait(self, engine, *toks):
        for t in toks:
            if t is not None:
                self.eng[engine].wait_ge(t.sem.sem, self.book.value(t))

    def _step(self, engine, ins):
        t = self.cnt[engine].mark(ins)
        self.wait(engine, t)
        self.latest[engine] = t
        return t

    def dve(self, ins):
        return self._step("dve", ins)

    def act(self, ins):
        return self._step("act", ins)

    def pool(self, ins):
        return self._step("pool", ins)

    def pe(self, ins):
        t = self.cnt["pe"].mark(ins)
        self.latest["pe"] = t
        return t

    def load(self, dst, src, stream, engine="sync"):
        c = self.book.counter("dma_" + stream, 16)
        e = {"sync": self.nc.sync, "act": self.nc.scalar}[engine]
        return c.mark(e.dma_start(dst, src))

    def fence(self, *extra, skip=None):
        toks = [t for t in self.latest.values() if t is not None] + list(extra)
        for e in self.eng:
            if e == skip:
                continue
            for t in toks:
                if t.sem is not self.cnt[e]:
                    self.wait(e, t)

    def settle(self):
        for k, c in self.cnt.items():
            if c.count:
                self.latest[k] = Token(c, c.count)

    def mm(self, out, lhsT, rhs, start=True, stop=True):
        return self.nc.tensor.matmul(out, lhsT, rhs, start=start, stop=stop, skip_group_check=True)

    def spare(self):
        if self.background is not None:
            next(self.background, None)

    def sb_top(self, name, shape):
        return self.sb(self.top_stack, name, shape)

    def take(self, bank):
        one = self.con("ident", 0, 32)
        self.mm(bank[0:32, 0:1], one, one[:, 0:1])

    def sb(self, stack, name, shape):
        return stack.enter_context(self.nc.sbuf_tensor(name, shape, F32))

    def vec(self, name, i=0, n=1, parts=P):
        o = VOFF[name] + i
        return self.V[0:parts, o:o + n]

    def con(self, name, i=0, n=None, p0=0, p1=P):
        o = COFF[name] + i
        return self.C[p0:p1, o:o + (n if n is not None else dict(CONST)[name] - i)]


def fm3(ap, n):
    return ap.rearrange("p (n t) -> p n t", n=n)


def build(nc, a, plan):
    g = Program(nc, a, plan)
    book, wait, dve, act, pe, mm = g.book, g.wait, g.dve, g.act, g.pe, g.mm
    v, s, tn = nc.vector, nc.scalar, nc.tensor
    top = ExitStack()
    with top:
        g.V = g.sb(top, "vecs", [P, NVEC])
        g.C = g.sb(top, "consts", [P, NCONST])
        X = g.sb(top, "residual", [P, KD, T])
        H = g.sb(top, "normed", [P, KD, T])
        R = g.sb(top, "rms", [P, T])
        SQ = g.sb(top, "squares", [P, 2, T])
        W = g.sb(top, "wring", [P, 2, KD, P])
        MOD = g.sb(top, "mods", [P, 2, 48, 2])
        SM = g.sb(top, "small", [P, 64])
        mrow = g.sb(top, "mod_rows", [P, 512])
        bank = [top.enter_context(nc.psum_tensor(f"bank{i}", [P, 512], F32)) for i in range(8)]
        vec, con = g.vec, g.con
        ident = con("ident")

        t_v = g.load(g.V[:, :], a["vecs"], "vecs")
        t_c = g.load(g.C[:, :], a["consts"], "consts")
        t_x = g.load(X[:, :, :], a["x_fm"].rearrange("p (k t) -> p k t", k=KD), "x")
        for e in ("dve", "act", "pe", "pool"):
            wait(e, t_v, t_c, t_x)
        for _ in range(40):
            dve(v.memset(SM[:, 0:1], 0.0))
            act(s.copy(SM[:, 1:2], g.C[:, 0:1]))
            pe(mm(bank[0][0:32, 0:32], ident[:, 0:32], ident[:, 0:32]))
        g.fence()

        def rms_rows(src, kd, n, eps, out, width):
            b = bank[7]
            free = [None, None]
            wait("act", g.latest["dve"])
            for k in range(kd):
                wait("act", free[k % 2])
                t = act(s.activation(SQ[:, k % 2, 0:n], src(k), ACT.Square))
                wait("pe", t)
                free[k % 2] = pe(mm(b[:, 0:n], con("ones"), SQ[:, k % 2, 0:n], k == 0, k == kd - 1))
                g.spare()
            wait("dve", free[(kd - 1) % 2])
            rsqrt(b[:, 0:n], 1.0 / width, eps, out[:, 0:n])

        def rsqrt(psum, scale, eps, out):
            t = dve(v.tensor_scalar(out, psum, scale, eps, ALU.mult, ALU.add))
            wait("act", t)
            t = act(s.activation(out, out, ACT.Sqrt))
            wait("dve", t)
            dve(v.reciprocal(out, out))

        def project(n_chunks, wsrc, rhs, n, evac, kd=KD):
            assert n_chunks % 2 == 0
            with book.run(n_chunks // 2) as i:
                for j in range(2):
                    wait("sp", book.before(f"mm{j}", g.cnt["pe"]))
                    t_w = g.load(W[:, j, 0:kd, :], wsrc(i * 2 + j), f"w{j}")
                    wait("pe", t_w, book.before(f"ev{j}", g.cnt[evac_engine(j)]))
                    for k in range(kd):
                        ins = mm(bank[j][:, 0:n], W[:, j, k, :], rhs(k), k == 0, k == kd - 1)
                    t_m = book.name(f"mm{j}", pe(ins))
                    wait(evac_engine(j), t_m)
                    book.name(f"ev{j}", evac(i * 2 + j, bank[j][:, 0:n], evac_engine(j)))
            g.settle()
            g.fence()

        def evac_engine(j):
            return "dve"

        def wblock(name):
            return lambda i: a[name][bass.ds(i, 1), :, :].rearrange("o p (k c) -> p (o k) c", c=P)

        def adaln_steps(layer, wm, cs):
            src = a["w_mod"][layer].rearrange("(k p) c -> k p c", p=P)
            used, loaded = {}, {}

            def fetch(n):
                if n < 24:
                    wait("sp", used.get(n - 4))
                    loaded[n] = g.load(wm[:, n % 4, :], src[n % KD][:, (n // KD) * 2048:(n // KD + 1) * 2048], f"wm{n % 4}")

            for n in range(4):
                fetch(n)
            t_row = None
            for n in range(24):
                i, k = n // KD, n % KD
                wait("pe", loaded[n], t_row if k == 0 else None)
                for q in range(4):
                    ins = mm(bank[4][32 * q:32 * q + 32, :], cs[:, k, :], wm[:, n % 4, 512 * q:512 * q + 512], k == 0, k == KD - 1)
                used[n] = pe(ins)
                fetch(n + 4)
                if k == KD - 1:
                    wait("dve", used[n], g.bank_free[5])
                    t_row = dve(v.tensor_copy(mrow[:, :], bank[4][:, :]))
                    wait("pe", t_row)
                    for j in range(4):
                        ins = tn.transpose(bank[5][:, j * P:(j + 1) * P], mrow[:, j * P:(j + 1) * P], ident)
                    wait("dve", pe(ins))
                    turned = bank[5][:, :].rearrange("p (j q r) -> p q j r", q=4, r=32)
                    bias = vec("b_mod", 48 * layer + 16 * i, 16).rearrange("p (q j) -> p q j", q=4)
                    for r in range(2):
                        o = MOD[:, layer, 16 * i:16 * i + 16, r].rearrange("p (q j) -> p q j", q=4)
                        g.bank_free[5] = dve(v.tensor_tensor(o, turned[:, :, :, r], bias, ALU.add))
                yield

        GA = g.sb(top, "gains", [P, 5, 8])

        def gain_of(slot, norm, off, layer, scale_chunk, r=0):
            dve(v.tensor_scalar(GA[:, slot, :], MOD[:, layer, scale_chunk:scale_chunk + 8, r], 1.0, None, ALU.add))
            dve(v.tensor_tensor(GA[:, slot, :], GA[:, slot, :], vec(norm, off, 8), ALU.mult))

        def modulate(src, n, slot, shift, dst):
            for k in range(KD):
                t = dve(v.scalar_tensor_tensor(out=dst(k), in0=src(k), scalar=GA[:, slot, k:k + 1], in1=R[:, 0:n],
                                               op0=ALU.mult, op1=ALU.mult))
                wait("act", t)
                act(s.activation(dst(k), dst(k), ACT.Identity, bias=shift(k)))

        def softplus(x, tmp, tmp2, tmp3):
            wait("act", g.latest["dve"])
            act(s.activation(tmp, x, ACT.Abs))
            act(s.activation(tmp, tmp, ACT.Exp, scale=-1.0))
            wait("dve", g.latest["act"])
            dve(v.tensor_scalar(tmp2, tmp, 2.0, None, ALU.add))
            dve(v.reciprocal(tmp2, tmp2))
            dve(v.tensor_tensor(tmp, tmp, tmp2, ALU.mult))
            dve(v.tensor_tensor(tmp2, tmp, tmp, ALU.mult))
            dve(v.tensor_scalar(tmp3, tmp2, 1.0 / 15, None, ALU.mult))
            for d in (13, 11, 9, 7, 5, 3):
                dve(v.scalar_tensor_tensor(out=tmp3, in0=tmp3, scalar=1.0 / d, in1=tmp2, op0=ALU.add, op1=ALU.mult))
            dve(v.scalar_tensor_tensor(out=tmp, in0=tmp3, scalar=1.0, in1=tmp, op0=ALU.add, op1=ALU.mult))
            dve(v.tensor_scalar(x, x, 0.0, None, ALU.max))
            dve(v.scalar_tensor_tensor(out=x, in0=tmp, scalar=2.0, in1=x, op0=ALU.mult, op1=ALU.add))

        def dwconv(dst, src, n, wname, w0, stride, ntap, lead, bname=None, b0=0):
            if bname is None:
                t = dve(v.tensor_scalar(dst[:, 0:n], src[:, 0:n], vec(wname, w0 + lead * stride), None, ALU.mult))
            else:
                t = dve(v.tensor_scalar(dst[:, 0:n], src[:, 0:n], vec(wname, w0 + lead * stride), vec(bname, b0),
                                    ALU.mult, ALU.add))
            for j in range(ntap):
                d = j - lead
                if d == 0:
                    continue
                lo, hi = max(0, -d), min(n, n - d)
                t = dve(v.scalar_tensor_tensor(out=dst[:, lo:hi], in0=src[:, lo + d:hi + d], scalar=vec(wname, w0 + j * stride),
                                           in1=dst[:, lo:hi], op0=ALU.mult, op1=ALU.add))
            return t

        LW = g.sb(top, "lru_state", [P, 2, 4])
        SPL = g.sb(top, "lru_rate", [P, 3, 8])

        def rglru(raw, n, gw, hh, ig, hs, context):
            t_e = {}
            xa = g.sb_top(f"xa{n}", [P, 2, n])
            for k in range(KR):
                x = xa[:, k % 2, :]
                dwconv(x, raw(k), n, "conv_a_w", k, KR, 4, 1, "conv_a_b", k)
                t = dve(v.tensor_copy(raw(k), x))
                wait("pe", t)
                for d in range(2):
                    j, b = d * KR + k, 2 * (k % 2) if d == 0 else 2 * (k % 2) + 1
                    b0, b1 = bank[0 + 2 * d], bank[1 + 2 * d]
                    wait("pe", t_e.get(d))
                    mm(b0[:, 0:n], gw[:, 2 * j, :], raw(k))
                    t = pe(mm(b1[:, 0:n], gw[:, 2 * j + 1, :], raw(k)))
                    wait("act", t)
                    act(s.activation(hh[:, j, :], b0[:, 0:n], ACT.Sigmoid, bias=vec("lru_br", j)))
                    t_e[d] = act(s.activation(ig[:, j, :], b1[:, 0:n], ACT.Sigmoid, bias=vec("lru_bi", j)))
                    act(s.activation(hh[:, j, :], hh[:, j, :], ACT.Tanh, scale=SPL[:, 1, j:j + 1]))
                    g.spare()
            t_s = []
            for j in range(8):
                t_s.append(act(s.activation(hs[:, j, :], hh[:, j, :], ACT.Sqrt, scale=-1.0)))
            for j in range(8):
                d, k = j // KR, j % KR
                h_, i_, s_, q = hh[:, j, :], ig[:, j, :], hs[:, j, :], xa[:, 0, :]
                wait("dve", t_s[0 if j == 0 else j])
                dve(v.tensor_scalar(q, h_, -1.0, 1.0, ALU.mult, ALU.add))
                dve(v.reciprocal(q, q))
                dve(v.scalar_tensor_tensor(out=h_, in0=h_, scalar=1.0, in1=q, op0=ALU.add, op1=ALU.mult))
                dve(v.scalar_tensor_tensor(out=q, in0=q, scalar=2.0, in1=s_, op0=ALU.mult, op1=ALU.mult))
                dve(v.tensor_tensor(i_, i_, raw(k), ALU.mult))
                dve(v.tensor_tensor(i_, i_, q, ALU.mult))
                init = 0.0 if context else LW[:, d, k:k + 1]
                if d == 0:
                    dve(v.tensor_tensor_scan(s_, h_, i_, init, ALU.mult, ALU.add))
                else:
                    dve(v.tensor_tensor_scan(s_[:, ::-1], h_[:, ::-1], i_[:, ::-1], init, ALU.mult, ALU.add))
                if context:
                    e = n - 1 if d == 0 else 0
                    dve(v.tensor_copy(LW[:, d, k:k + 1], s_[:, e:e + 1]))
                g.spare()

        def sine(ps, layer, dst):
            f = vec(f"filt_freq{layer}", parts=FHID)
            dve(v.tensor_scalar(dst, ps, vec(f"filt_b{layer + 1}", parts=FHID), f, ALU.add, ALU.mult))
            q = R[0:FHID, :]
            dve(v.tensor_scalar(q, dst, 1.0 / (2 * math.pi), 12582912.0, ALU.mult, ALU.add))
            dve(v.tensor_scalar(q, q, -12582912.0, None, ALU.add))
            c1 = 6.28125
            dve(v.scalar_tensor_tensor(out=dst, in0=q, scalar=-c1, in1=dst, op0=ALU.mult, op1=ALU.add))
            dve(v.scalar_tensor_tensor(out=dst, in0=q, scalar=-(2 * math.pi - c1), in1=dst, op0=ALU.mult, op1=ALU.add))
            dve(v.tensor_scalar(dst, dst, 3.1415925, -3.1415925, ALU.min, ALU.max))
            wait("act", g.latest["dve"])
            act(s.activation(dst, dst, ACT.Sin))
            wait("pe", g.latest["act"])

        def spectrum_steps(st, fw, kf):
            sd = g.sb(st, "filt_sd", [P, 2, NT, RW])
            hid = g.sb(st, "hidden", [FHID + 1, 2, T])
            w3 = g.sb(st, "filt_w3", [FHID + 1, 4, RW])
            w12 = g.sb(st, "filt_w12", [FHID, 2, FHID])
            zf = g.sb(st, "filt_z", [FEMB, T])
            win = g.sb(st, "window", [P, NT, RW])
            tt = [g.load(w3[0:FHID, :, :], a["filt_w3"].rearrange("p (q c) -> p q c", q=4), "fw3", "act"),
                  g.load(w3[FHID:FHID + 1, :, :], a["filt_b3"].rearrange("p (q c) -> p q c", q=4), "fb3", "act"),
                  g.load(w12[0:FEMB, 0, :], a["filt_w1"], "fw1", "act"),
                  g.load(w12[:, 1, :], a["filt_w2"], "fw2", "act"),
                  g.load(zf[:, :], a["filt_z"], "fz", "act"),
                  g.load(win[:, :, :], a["window"].rearrange("p (k t) -> p k t", k=NT), "win", "act")]
            t_fw = g.load(fw[:, :, :], a["dft"].rearrange("p (k t) -> p k t", k=NT), "dft", "act")
            wait("pe", *tt)
            wait("dve", *tt)
            dve(v.memset(hid[FHID:FHID + 1, :, :], 1.0))
            t = pe(mm(bank[0][0:FHID, :], w12[0:FEMB, 0, :], zf[:, :]))
            yield
            wait("dve", t)
            sine(bank[0][0:FHID, :], 0, hid[0:FHID, 0, :])
            t = pe(mm(bank[1][0:FHID, :], w12[:, 1, :], hid[0:FHID, 0, :]))
            yield
            wait("dve", t)
            sine(bank[1][0:FHID, :], 1, hid[0:FHID, 1, :])
            wait("pe", t_fw)
            t_kf = None
            for o in range(2):
                t_f = {}
                for n in range(NT):
                    fb = [bank[2 * (n % 2)], bank[2 * (n % 2) + 1]]
                    wait("pe", t_f.get(n - 2), g.latest["dve"] if n == 0 else None)
                    for q in range(2):
                        ins = mm(fb[q][:, :], hid[:, 1, n * P:(n + 1) * P], w3[:, 2 * o + q, :])
                    wait("dve", pe(ins), t_kf)
                    f0, f1 = SQ[:, 0, :], SQ[:, 1, :]
                    dve(v.tensor_tensor(f0, fb[0][:, :], win[:, n, :], ALU.mult))
                    t_f[n] = dve(v.tensor_tensor(f1, fb[1][:, :], win[:, n, :], ALU.mult))
                    if n == 0:
                        dve(v.memset(SQ[0:1, 1, :], 0.0))
                    dve(v.tensor_tensor(sd[:, 0, n, :], f0, f1, ALU.add))
                    t_sd = dve(v.tensor_tensor(sd[:, 1, n, :], f0, f1, ALU.subtract))
                    yield
                done = []
                wait("pe", t_sd)
                for m in range(9):
                    b = bank[m % 4]
                    wait("pe", t_f[3 if m < 2 else 2] if m < 4 else done[m - 4])
                    col = m * P if m < 8 else T
                    for k in range(NT):
                        ins = mm(b[:, :], fw[:, k, col:col + P], sd[:, 1 if 4 <= m < 8 else 0, k, :], k == 0, k == NT - 1)
                    t_kf = pe(ins)
                    wait("act", t_kf)
                    done.append(act(s.copy(kf[:, o, m, :], b[:, :])))
                    yield
                wait("dve", done[-1])
                dve(v.tensor_copy(SQ[0:1, 0, :], kf[0:1, o, 8, :]))
                dve(v.tensor_copy(kf[:, o, 8, :], kf[:, o, 0, :]))
                dve(v.tensor_copy(kf[0:1, o, 8, :], SQ[0:1, 0, :]))
                dve(v.memset(kf[0:1, o, 4, :], 0.0))
            yield

        def layer0_mixer():
            with ExitStack() as st:
                kf = g.sb(st, "spectrum", [P, 2, 9, RW])
                fw = g.sb(st, "dft", [P, NT, 2 * T])
                gw = g.sb(st, "lru_w", [P, 16, P])
                with ExitStack() as early:
                    wm = g.sb(early, "wmod", [P, 4, 2048])
                    cs = g.sb(early, "cond", [P, KD, 32])
                    dve(v.memset(cs[:, :, :], 0.0))
                    wait("act", g.latest["dve"])
                    act(s.activation(cs[:, :, 0], vec("c", 0, 8), ACT.Silu))
                    act(s.activation(cs[:, :, 1], vec("c_ctx", 0, 8), ACT.Silu))
                    dve(v.memset(gw[:, :, :], 0.0))
                    g.fence()
                    with ExitStack() as gen:
                        spec = spectrum_steps(gen, fw, kf)
                        for _ in adaln_steps(0, wm, cs):
                            next(spec, None)
                        for _ in spec:
                            pass
                        g.fence()
                    t1 = g.load(gw[0:64, :, 0:64], a["lru_w"][0], "lru_w0")
                    t2 = g.load(gw[64:128, :, 64:128], a["lru_w"][1], "lru_w1")
                    wait("pe", t1, t2)
                    gain_of(0, "norm1_g", 0, 0, 8)
                    gain_of(1, "norm1_g", 0, 0, 8, 1)
                    dve(v.tensor_scalar(SPL[:, 0, :], vec("lru_lam", 0, 8), -1.0, None, ALU.mult))
                    softplus(SPL[:, 0, :], SPL[:, 1, :], SPL[:, 2, :], SM[:, 0:8])
                    t = dve(v.tensor_scalar(SPL[:, 1, :], SPL[:, 0, :], -0.5 * LRU_C, None, ALU.mult))
                    wait("act", t)
                    g.background = adaln_steps(1, wm, cs)
                    with ExitStack() as cx:
                        xc = g.sb(cx, "ctx", [P, KD, TC])
                        ra = g.sb(cx, "ctx_raw", [P, KR, TC])
                        hc = g.sb(cx, "ctx_lru", [P, 3, 8, TC])
                        t = g.load(xc[:, :, :], a["ctx_fm"].rearrange("p (k t) -> p k t", k=KD), "ctx", "act")
                        wait("act", t)
                        wait("dve", t)
                        rms_rows(lambda k: xc[:, k, :], KD, TC, EPS, R, D)
                        modulate(lambda k: xc[:, k, :], TC, 1, lambda k: MOD[:, 0, k, 1:2], lambda k: xc[:, k, :])
                        g.fence()

                        def ev(i, ps, e):
                            return dve(v.tensor_copy(ra[:, bass.ds(i, 1), :].rearrange("p o t -> p (o t)"), ps))

                        src = wblock("w_in")
                        project(KR, lambda i: src(i + KR), lambda k: xc[:, k, :], TC, ev)
                        g.top_stack = cx
                        rglru(lambda k: ra[:, k, :], TC, gw, hc[:, 0, :, :], hc[:, 1, :, :], hc[:, 2, :, :], True)
                        rms_rows(lambda k: X[:, k, :], KD, T, EPS, R, D)
                        for _ in g.background:
                            pass
                        g.background = None
                        g.fence()
                modulate(lambda k: X[:, k, :], T, 0, lambda k: MOD[:, 0, k, 0:1], lambda k: H[:, k, :])
                pr = g.sb(st, "proj", [P, 20, T])
                g.fence()

                def ev(i, ps, e):
                    return dve(v.tensor_copy(pr[:, bass.ds(i, 1), :].rearrange("p o t -> p (o t)"), ps))

                project(20, wblock("w_in"), lambda k: H[:, k, :], T, ev)
                with ExitStack() as lru:
                    hl = g.sb(lru, "lru_g", [P, 8, T])
                    ht = g.sb(lru, "lru_h", [P, 8, T])
                    g.top_stack = lru
                    g.fence()
                    rglru(lambda k: pr[:, KR + k, :], T, gw, hl, H, ht, False)
                    t_g = [act(s.activation(pr[:, k, :], pr[:, k, :], ACT.Gelu_apprx_tanh)) for k in range(KR)]
                    for k in range(KR):
                        dve(v.tensor_tensor(ht[:, k, :], ht[:, k, :], ht[:, KR + k, :], ALU.add))
                        wait("dve", t_g[k])
                        dve(v.tensor_tensor(H[:, k, :], ht[:, k, :], pr[:, k, :], ALU.mult))
                    t_c = []
                    for k in range(12):
                        tmp = ht[:, k % 8, :]
                        wait("dve", t_c[k - 8] if k >= 8 else None)
                        t = dwconv(tmp, pr[:, 8 + k, :], T, "conv_b_w", k, 12, 3, 1, "conv_b_b", k)
                        wait("act", t)
                        t_c.append(act(s.copy(pr[:, 8 + k, :], tmp)))
                    g.fence()
                hyena(lambda k: pr[:, 8 + k, :], lambda o, k: pr[:, 12 + 4 * o + k, :],
                      H[:, KR:2 * KR, :], lambda k: H[:, KR + k, :], fw, kf)

            def ev(i, ps, e):
                xi = X[:, bass.ds(i, 1), :].rearrange("p o t -> p (o t)")
                return dve(v.scalar_tensor_tensor(out=xi, in0=ps, scalar=MOD[:, 0, bass.ds(i + 16, 1), 0:1].rearrange("p a b -> p (a b)"),
                                                  in1=xi, op0=ALU.mult, op1=ALU.add))

            project(KD, wblock("w_out"), lambda k: H[:, k, :], T, ev)

        def hyena(zin, gate, ztm, zout, fw, kf):
            with ExitStack() as st:
                sd = g.sb(st, "z_spectrum", [P, 2, NT, RW])
                inv = g.sb(st, "idft", [P, 8, T])
                g.fence()
                t_inv = g.load(inv[:, :, :], a["idft"].rearrange("p (k t) -> p k t", k=8), "idft")
                wait("pe", t_inv)
                for o in range(2):
                    wait("pe", g.latest["dve"])
                    t_z = []
                    for n in range(NT):
                        for k in range(KR):
                            ins = tn.transpose(bank[n][:, k * P:(k + 1) * P], zin(k)[:, n * P:(n + 1) * P], ident)
                        t = pe(ins)
                        wait("act", t)
                        t_z.append(act(s.copy(ztm[:, n, :], bank[n][:, :])))
                    wait("pe", *t_z)
                    t_free = {}
                    for m in range(NT):
                        br, bi = bank[(2 * m + 4) % 8], bank[(2 * m + 5) % 8]
                        for k in range(NT):
                            mm(br[:, :], fw[:, k, m * P:(m + 1) * P], ztm[:, k, :], k == 0, k == NT - 1)
                        for k in range(NT):
                            ins = mm(bi[:, :], fw[:, k, T + m * P:T + (m + 1) * P], ztm[:, k, :], k == 0, k == NT - 1)
                        t = pe(ins)
                        wait("dve", t)
                        kr, ki = kf[:, o, m, :], kf[:, o, 4 + m, :]
                        kr2 = kf[:, o, 8, :] if m == 0 else kr
                        q0, q1 = SQ[:, 0, :], SQ[:, 1, :]
                        dve(v.tensor_tensor(q0, br[:, :], kr, ALU.mult))
                        dve(v.tensor_tensor(q1, bi[:, :], ki, ALU.mult))
                        dve(v.tensor_tensor(sd[:, 0, m, :], q0, q1, ALU.subtract))
                        dve(v.tensor_tensor(q0, br[:, :], ki, ALU.mult))
                        dve(v.tensor_tensor(q1, bi[:, :], kr2, ALU.mult))
                        dve(v.tensor_tensor(sd[:, 1, m, :], q0, q1, ALU.add))
                    wait("pe", g.latest["dve"])
                    for k in range(KR):
                        for m in range(8):
                            ins = mm(bank[k][:, :], sd[:, m // 4, m % 4, k * P:(k + 1) * P], inv[:, m, :], m == 0, m == 7)
                        t = pe(ins)
                        wait("dve", t)
                        dst = zin(k) if o == 0 else zout(k)
                        dve(v.scalar_tensor_tensor(out=zin(k), in0=zin(k), scalar=vec("filt_bias", 4 * o + k),
                                                   in1=bank[k][:, :], op0=ALU.mult, op1=ALU.add))
                        dve(v.tensor_tensor(dst, zin(k), gate(o, k), ALU.mult))
                g.fence()

        def moe(layer):
            sh, sc, gt = (24, 32, 40)
            L = f"_{layer}"
            with ExitStack() as st:
                ring = g.sb(st, "experts" + L, [P, NRING, 2, FF])
                HT = g.sb(st, "h_tm" + L, [P, NT, D])
                rt = g.sb(st, "router" + L, [P, KD, NE])
                pb = g.sb(st, "probs" + L, [P, NT, NE + 2])
                sl = g.sb(st, "slots" + L, [P, NT, NE + 2])
                pe_t = g.sb(st, "probs_e" + L, [NE, T])
                wk = g.sb(st, "topk" + L, [NE, 2, T])
                mx = g.sb(st, "max8" + L, [NE, 8])
                PM = g.sb(st, "pick" + L, [P, NT, 2, CAP])
                PG = g.sb(st, "give" + L, [P, NT, 2, CAP])
                PT = g.sb(st, "give_t" + L, [P, T])
                xr = W[:, 0, :, :].rearrange("p k c -> p (k c)")
                xs = W[:, 1, :, :]
                hs = SQ
                hT = g.sb(st, "hs_t" + L, [P, 2, 4, P])
                yy = g.sb(st, "y" + L, [P, D])
                g.fence()
                t = g.load(rt[:, :, :], a["router"][layer].rearrange("p (k e) -> p k e", k=KD), "router")
                wait("pe", t)
                gain_of(2, "norm2_g", 8 * layer, layer, sc)
                rms_rows(lambda k: X[:, k, :], KD, T, EPS, R, D)
                modulate(lambda k: X[:, k, :], T, 2, lambda k: MOD[:, layer, sh + k, 0:1], lambda k: H[:, k, :])
                wait("pe", g.latest["dve"], g.latest["act"])
                for k in range(KD):
                    ins = mm(bank[0][0:NE, :], rt[:, k, :], H[:, k, :], k == 0, k == KD - 1)
                t = pe(ins)
                wait("dve", t)
                t_l = dve(v.tensor_copy(pe_t[:, :], bank[0][0:NE, :]))
                wait("pe", t_l)
                for n in range(NT):
                    ins = tn.transpose(bank[1][:, n * NE:(n + 1) * NE], pe_t[:, n * P:(n + 1) * P], ident[0:NE, 0:NE])
                t_lt = pe(ins)
                for n in range(NT):
                    for h in range(2):
                        b = bank[4 + (2 * n + h) % 4]
                        if n >= 2:
                            wait("pe", t_h[2 * n + h - 4])
                        elif n + h == 0:
                            t_h = []
                        for k in range(4):
                            ins = tn.transpose(b[:, k * P:(k + 1) * P], H[:, 4 * h + k, n * P:(n + 1) * P], ident)
                        t = pe(ins)
                        wait("act", t)
                        t_h.append(act(s.copy(HT[:, n, 512 * h:512 * h + 512], b[:, :])))
                wait("dve", t_lt)
                lg = bank[1][:, 0:NT * NE].rearrange("p (n e) -> p n e", n=NT)
                pr = pb[:, :, 0:NE]
                dve(v.tensor_reduce(SM[:, 0:NT], lg, AXX, ALU.max))
                dve(v.tensor_tensor(pr, lg, SM[:, 0:NT].unsqueeze(2).broadcast_to([P, NT, NE]), ALU.subtract))
                wait("act", g.latest["dve"])
                act(s.activation(pr, pr, ACT.Exp))
                wait("dve", g.latest["act"])
                dve(v.tensor_reduce(SM[:, 8:8 + NT], pr, AXX, ALU.add))
                dve(v.reciprocal(SM[:, 8:8 + NT], SM[:, 8:8 + NT]))
                dve(v.tensor_tensor(pr, pr, SM[:, 8:8 + NT].unsqueeze(2).broadcast_to([P, NT, NE]), ALU.mult))
                wait("pe", g.latest["dve"])
                for n in range(NT):
                    ins = tn.transpose(bank[2][0:NE, n * P:(n + 1) * P], pb[:, n, 0:NE], ident)
                t = pe(ins)
                wait("dve", t)
                dve(v.tensor_copy(wk[:, 0, :], bank[2][0:NE, :]))
                for r in range(CAP // 8):
                    dve(v.max(mx[:, :], wk[:, r % 2, :]))
                    dve(v.match_replace(wk[:, (r + 1) % 2, :], mx[:, :], wk[:, r % 2, :], -1.0))
                dve(v.tensor_scalar(wk[:, 1, :], wk[:, 0, :], -1.0, None, ALU.is_equal))
                dve(v.memset(pe_t[:, :], 1.0))
                dve(v.tensor_tensor_scan(wk[:, 0, :], pe_t[:, :], wk[:, 1, :], 0.0, ALU.mult, ALU.add))
                dve(v.tensor_tensor(wk[:, 0, :], wk[:, 0, :], wk[:, 1, :], ALU.mult))
                dve(v.tensor_scalar(wk[:, 0, :], wk[:, 0, :], -1.0, None, ALU.add))
                wait("pe", g.latest["dve"])
                for n in range(NT):
                    ins = tn.transpose(bank[3][:, n * NE:(n + 1) * NE], wk[:, 0, n * P:(n + 1) * P], ident[0:NE, 0:NE])
                t = pe(ins)
                dve(v.memset(sl[:, :, :], -1.0))
                dve(v.memset(pb[:, :, NE:NE + 2], 0.0))
                dve(v.memset(yy[:, :], 0.0))
                dve(v.memset(PT[:, :], 0.0))
                wait("dve", t)
                dve(v.tensor_copy(sl[:, :, 0:NE], bank[3][:, 0:NT * NE].rearrange("p (n e) -> p n e", n=NT)))
                w = {q: a[f"exp_w{q}"][layer].rearrange("e (j k p) f -> e j p k f", j=4, p=P) for q in (1, 3, 2)}
                iota = con("iota", 0, CAP).unsqueeze(1).unsqueeze(1).broadcast_to([P, NT, 2, CAP])
                order = [(q, e, j) for e in range(2) for j in range(4) for q in (1, 3)]
                order += [(2, e, j) for j in range(4) for e in range(2)]
                place = {x: n % NRING for n, x in enumerate(order)}

                def pick(pair):
                    so = sl[:, :, bass.ds(pair * 2, 2)].unsqueeze(3).broadcast_to([P, NT, 2, CAP])
                    return dve(v.tensor_tensor(PM[:, :, :, :], iota, so, ALU.is_equal))

                def give(pair):
                    po = pb[:, :, bass.ds(pair * 2, 2)].unsqueeze(3).broadcast_to([P, NT, 2, CAP])
                    return dve(v.tensor_tensor(PG[:, :, :, :], PM[:, :, :, :], po, ALU.mult))

                def gather():
                    for h in range(2):
                        for n in range(NT):
                            ins = mm(bank[6 + h][:, :], PM[:, n, :, :], HT[:, n, 512 * h:512 * h + 512], n == 0, n == NT - 1)
                        t = pe(ins)
                        wait("act", t)
                        t_x = act(s.copy(xr[:, 512 * h:512 * h + 512], bank[6 + h][:, :]))
                    return t, t_x

                def turn(t_x):
                    wait("pe", t_x)
                    for h in range(2):
                        for k in range(4):
                            ins = tn.transpose(bank[6 + h][:, k * P:(k + 1) * P], xr[:, (4 * h + k) * P:(4 * h + k + 1) * P], ident)
                        t = pe(ins)
                        wait("act", t)
                        t_xs = act(s.copy(xs[:, 4 * h:4 * h + 4, :], bank[6 + h][:, :].rearrange("p (k c) -> p k c", k=4)))
                    return t, t_xs

                def scatter(last_adds):
                    adds = []
                    for k in range(KD):
                        b = bank[4 + k % 2]
                        wait("pe", last_adds[k] if k < 2 else adds[k - 2])
                        t = pe(mm(b[:, :], yy[:, k * P:(k + 1) * P], PT[:, :]))
                        wait("dve", t)
                        adds.append(dve(v.scalar_tensor_tensor(out=X[:, k, :], in0=b[:, :], scalar=MOD[:, layer, gt + k, 0:1],
                                                               in1=X[:, k, :], op0=ALU.mult, op1=ALU.add)))
                    return t, adds

                t = pick(0)
                wait("pe", t, g.latest["act"])
                t, t_x = gather()
                wait("dve", t)
                give(0)
                turn(t_x)
                g.fence(skip="sp")
                with book.run(NE // 2) as i:
                    cpe, cdve, cact = g.cnt["pe"], g.cnt["dve"], g.cnt["act"]
                    tw = {}
                    for n, (q, e, j) in enumerate(order):
                        if n < NRING:
                            wait("sp", book.before(f"use{n}", cpe))
                        else:
                            wait("sp", book.later(f"use{n - NRING}x", cpe))
                        tw[q, e, j] = g.load(ring[:, place[q, e, j], :, :],
                                             w[q][bass.ds(i * 2 + e, 1), j].rearrange("o p k f -> p (o k) f"),
                                             f"ring{place[q, e, j]}")

                    def used(x, t):
                        n = order.index(x)
                        if n < len(order) - NRING:
                            book.name(f"use{n}x", t)
                        if n >= len(order) - NRING:
                            book.name(f"use{n - (len(order) - NRING)}", t)

                    def up(e):
                        for j in range(4):
                            for q, m in ((0, 1), (1, 3)):
                                wait("pe", tw[m, e, j])
                                for k in range(2):
                                    for f in range(2):
                                        ins = mm(bank[2 * e + q][64 * f:64 * f + 64, :], xs[:, 2 * j + k, 64 * e:64 * e + 64],
                                                 ring[:, place[m, e, j], k, 512 * f:512 * f + 512], j + k == 0, j == 3 and k == 1)
                                t = pe(ins)
                                used((m, e, j), t)
                        wait("act", t)
                        t_s = act(s.activation(hs[:, e, :], bank[2 * e][:, :], ACT.Silu))
                        wait("dve", t_s)
                        return dve(v.tensor_tensor(hs[:, e, :], hs[:, e, :], bank[2 * e + 1][:, :], ALU.mult))

                    def turn_hidden(e, t_hs):
                        wait("pe", t_hs)
                        for k in range(4):
                            ins = tn.transpose(bank[4 + e][:, k * P:(k + 1) * P], hs[:, e, k * P:(k + 1) * P], ident)
                        t = pe(ins)
                        wait("act", t)
                        return act(s.copy(hT[:, e, :, :], bank[4 + e][:, :].rearrange("p (k c) -> p k c", k=4)))

                    wait("dve", book.before("gather", cpe))
                    t_pm = pick(i + 1)
                    wait("pe", book.before("xs", cact), book.before("yy", cact))
                    t_h0 = up(0)
                    t_sc, adds = scatter([book.before("hT0", cact), book.before("hT1", cact)])
                    for n in range(NT):
                        ins = tn.transpose(bank[7][:, n * P:(n + 1) * P], PG[:, n, :, :].rearrange("p e c -> p (e c)"), ident)
                    t = pe(ins)
                    wait("act", t)
                    t_pt = act(s.copy(PT[:, :], bank[7][:, :]))
                    wait("dve", t)
                    give(i + 1)
                    t_h1 = up(1)
                    wait("pe", adds[6])
                    t_ht0 = book.name("hT0", turn_hidden(0, t_h0))
                    wait("pe", t_pm, t_pt)
                    t, t_x = gather()
                    book.name("gather", t)
                    wait("pe", adds[7])
                    t_ht1 = book.name("hT1", turn_hidden(1, t_h1))
                    _, t_xs = turn(t_x)
                    book.name("xs", t_xs)
                    wait("pe", t_ht0, t_ht1)
                    for j in range(4):
                        for e in range(2):
                            wait("pe", tw[2, e, j])
                        for k in range(2):
                            kk = 2 * j + k
                            for f in range(2):
                                for e in range(2):
                                    ins = mm(bank[f][64 * e:64 * e + 64, :], hT[:, e, kk % 4, 64 * (kk // 4):64 * (kk // 4) + 64],
                                             ring[:, place[2, e, j], k, 512 * f:512 * f + 512], kk == 0, kk == 7)
                        t = pe(ins)
                        used((2, 0, j), t)
                        used((2, 1, j), t)
                    wait("act", t)
                    for f in range(2):
                        t_y = act(s.copy(yy[:, 512 * f:512 * f + 512], bank[f][:, :]))
                    book.name("yy", t_y)
                g.settle()
                g.fence()
                scatter([None, None])
                g.fence()

        def layer1_mixer():
            gain_of(0, "norm1_g", 8, 1, 8)
            rms_rows(lambda k: X[:, k, :], KD, T, EPS, R, D)
            modulate(lambda k: X[:, k, :], T, 0, lambda k: MOD[:, 1, k, 0:1], lambda k: H[:, k, :])
            with ExitStack() as st:
                U = g.sb(st, "cf_u", [P, KD, T])
                Y = g.sb(st, "cf_y", [P, KD, T])
                gs = g.sb(st, "cf_sig", [P, T])
                g.fence()

                def row(tile, i):
                    return tile[:, bass.ds(i, 1), :].rearrange("p o t -> p (o t)")

                def ev_a(i, ps, e):
                    return dve(v.tensor_scalar(row(U, i), ps, g.V[:, bass.ds(i + VOFF["cf_b1"], 1)], None, ALU.add))

                project(KD, wblock("cf_w1"), lambda k: H[:, k, :], T, ev_a)
                rows = T // GRID_W
                half = (CF_K - 1) // 2
                tap = [g.sb(st, "cf_taps", [P, 2 * rows]), g.sb(st, "cf_in", [P, T]), g.sb(st, "cf_out", [P, T])]
                g.fence()

                def ev_g(i, ps, e):
                    t = dve(v.tensor_scalar(gs[:, :], ps, g.V[:, bass.ds(i + VOFF["cf_b1"] + 8, 1)], None, ALU.add))
                    wait("act", t)
                    t_g = act(s.activation(gs[:, :], gs[:, :], ACT.Sigmoid))
                    w, u, y = tap
                    taps = g.V[:, VOFF["cf_dw_w"]:VOFF["cf_dw_w"] + CF_K * 8].rearrange("p (j k) -> p j k", k=8)
                    dve(v.tensor_copy(w[:, 0:2 * rows - 1],
                                      taps[:, half - rows + 1:half + rows, bass.ds(i, 1)].rearrange("p j o -> p (j o)")))
                    dve(v.tensor_copy(w[:, 2 * rows - 1:2 * rows], g.V[:, bass.ds(i + VOFF["cf_dw_b"], 1)]))
                    wait("dve", t_g)
                    dve(v.tensor_tensor(u[:, :], row(U, i), gs[:, :], ALU.mult))
                    mid = rows - 1
                    dve(v.tensor_scalar(y[:, :], u[:, :], w[:, mid:mid + 1], w[:, 2 * rows - 1:2 * rows], ALU.mult, ALU.add))
                    for j in range(-(rows - 1), rows):
                        if j:
                            lo, hi = max(0, -j * GRID_W), min(T, T - j * GRID_W)
                            dve(v.scalar_tensor_tensor(out=y[:, lo:hi], in0=u[:, lo + j * GRID_W:hi + j * GRID_W],
                                                       scalar=w[:, mid + j:mid + j + 1], in1=y[:, lo:hi],
                                                       op0=ALU.mult, op1=ALU.add))
                    dve(v.tensor_copy(row(Y, i), y[:, :]))
                    return t

                src = wblock("cf_w1")
                project(KD, lambda i: src(i + KD), lambda k: H[:, k, :], T, ev_g)
                wait("pe", g.latest["dve"])
                for k in range(KD):
                    ins = mm(bank[0][:, :], con("ones"), Y[:, k, :], k == 0, k == KD - 1)
                t = pe(ins)
                wait("dve", t)
                dve(v.tensor_scalar(gs[:, :], bank[0][:, :], -1.0 / D, None, ALU.mult))
                for k in range(KD):
                    t = dve(v.tensor_tensor(Y[:, k, :], Y[:, k, :], gs[:, :], ALU.add))
                rms_rows(lambda k: Y[:, k, :], KD, T, EPS, R, D)
                for k in range(KD):
                    t = dve(v.tensor_tensor(Y[:, k, :], Y[:, k, :], R[:, :], ALU.mult))
                    wait("act", t)
                    act(s.activation(H[:, k, :], Y[:, k, :], ACT.Silu, bias=vec("cf_ln_b", k), scale=vec("cf_ln_g", k)))
                dve(v.tensor_tensor(SM[:, 0:8], MOD[:, 1, 16:24, 0], vec("cf_b2", 0, 8), ALU.mult))
                for k in range(KD):
                    dve(v.tensor_scalar(X[:, k, :], X[:, k, :], SM[:, k:k + 1], None, ALU.add))
                g.fence()

                def ev(i, ps, e):
                    return dve(v.scalar_tensor_tensor(out=row(X, i), in0=ps,
                                                      scalar=MOD[:, 1, bass.ds(i + 16, 1), 0:1].rearrange("p a b -> p (a b)"),
                                                      in1=row(X, i), op0=ALU.mult, op1=ALU.add))

                project(KD, wblock("cf_w2"), lambda k: H[:, k, :], T, ev)

        def plain_norm(name, dst):
            rms_rows(lambda k: X[:, k, :], KD, T, EPS, R, D)
            for k in range(KD):
                dve(v.scalar_tensor_tensor(out=dst[:, k, :], in0=X[:, k, :], scalar=vec(name, k), in1=R[:, :],
                                           op0=ALU.mult, op1=ALU.mult))

        stages = a.get("stages", 99)
        layer0_mixer()
        if stages > 1:
            moe(0)
        if stages > 2:
            layer1_mixer()
        if stages > 3:
            moe(1)
        if stages > 4:
            plain_norm("final_g", X)
            second_block(g, a, X, H, R, SQ, W, SM, bank, project, wblock, softplus, rsqrt, plain_norm, dwconv)
            plain_norm("final_gain_2", X)
        g.fence()
        t = g.load(a["out"].rearrange("p (k t) -> p k t", k=KD), X[:, :, :], "out")
        wait("sp", t)
    return book.fresh


QKV, GZ, SU, SV, SZ, RK, RZ, NQ, NKV, NZ, NPROJ = 0, 6, 8, 10, 12, 14, 21, 23, 25, 28, 30


def second_block(g, a, X, H, R, SQ, W, SM, bank, project, wblock, softplus, rsqrt, plain_norm, dwconv):
    nc, book, wait, dve, act, pe, mm = g.nc, g.book, g.wait, g.dve, g.act, g.pe, g.mm
    v, s, tn = nc.vector, nc.scalar, nc.tensor
    vec, con = g.vec, g.con
    ident = con("ident")
    halves = [slice(0, 64), slice(64, 128)]
    outer = ExitStack()
    with outer:
        PJ = g.sb(outer, "proj2", [P, NPROJ, T])
        SL = g.sb(outer, "proj2_small", [96, T])
        YS = g.sb(outer, "mixer_out", [P, 8, T])
        g.fence()
        plain_norm("norm_gain_2", H)
        t = g.load(W[:, 0, :, 0:96], a["w_small"].rearrange("p (k c) -> p k c", c=96), "w0")
        wait("pe", t, g.latest["dve"])
        for k in range(KD):
            ins = mm(bank[0][0:96, :], W[:, 0, k, 0:96], H[:, k, :], k == 0, k == KD - 1)
        t = pe(ins)
        wait("dve", t)
        dve(v.tensor_copy(SL[:, :], bank[0][0:96, :]))
        g.fence()

        def ev(i, ps, e):
            return dve(v.tensor_copy(PJ[:, bass.ds(i, 1), :].rearrange("p o t -> p (o t)"), ps))

        project(NPROJ, wblock("w_in_2"), lambda k: H[:, k, :], T, ev)

        def head_sums(src, b):
            wait("pe", g.latest["dve"], g.latest["act"])
            t = pe(mm(bank[b][:, :], con("blk1"), src))
            wait("dve", t)
            return bank[b][:, :]

        def silu_into(dst, z):
            wait("act", g.latest["dve"])
            t = act(s.activation(z, z, ACT.Silu))
            wait("dve", t)
            dve(v.tensor_tensor(dst, dst, z, ALU.mult))

        def tile_products(b, left, right, after=()):
            wait("pe", g.latest["dve"], g.latest["act"])
            for n in range(NCH):
                for r in halves:
                    ins = mm(bank[b][r, n * CH:(n + 1) * CH], left[r, n * CH:(n + 1) * CH], right[r, n * CH:(n + 1) * CH])
            t = pe(ins)
            wait("dve", t)
            return bank[b][:, :]

        def to_rows(b, src, dst):
            wait("pe", g.latest["dve"], g.latest["act"])
            for n in range(NCH):
                for r in halves:
                    ins = mm(bank[b][r, n * CH:(n + 1) * CH], src[r, n * CH:(n + 1) * CH], con("i64")[r, :])
            t = pe(ins)
            wait("dve", t)
            dve(v.tensor_copy(dst, bank[b][:, :]))

        def masked(dst, ps, mask):
            dve(v.tensor_tensor(fm3(dst, NCH), fm3(ps, NCH), mask.unsqueeze(1).broadcast_to([P, NCH, CH]), ALU.mult))

        def last_of_chunk(x):
            return fm3(x, NCH)[:, :, CH - 1:CH].broadcast_to([P, NCH, CH])

        def delta(name, AT, TIL, QT, AQ, KH, lam, add, keys, out):
            with ExitStack() as st:
                TM_ = g.sb(st, name + "_inv", [P, 2, T])
                TT = g.sb(st, name + "_inv_t", [P, 2, T])
                MM_ = g.sb(st, name + "_lt_t", [P, 2, T])
                LT = g.sb(st, name + "_level", [P, 2, T])
                G = g.sb(st, name + "_state", [P, 2, HD])
                xr = g.sb(st, name + "_x", [P, 2, HD])
                ur = g.sb(st, name + "_u", [P, 2, HD])
                g.fence()
                for p in range(2):
                    dve(v.tensor_copy(TM_[:, p, :], con("eye64")))
                    dve(v.tensor_copy(TT[:, p, :], con("eye64")))
                g.fence()
                with book.run(LEVELS) as lv:
                    mask = g.C[:, bass.ds(lv * 64 + COFF["level"], 64)].unsqueeze(1).broadcast_to([P, NCH, CH])
                    for p in range(2):
                        wait("dve", book.before(f"m{p}", g.cnt["pe"]))
                        t_l = dve(v.tensor_tensor(fm3(LT[:, p, :], NCH), fm3(AT[:, p, :], NCH), mask, ALU.mult))
                        wait("pe", t_l)
                        g.take(bank[p])
                        for n in range(NCH):
                            c = slice(n * CH, (n + 1) * CH)
                            for r in halves:
                                ins = mm(bank[p][r, c], LT[r, p, c], TM_[r, p, c])
                        t = book.name(f"m{p}", pe(ins))
                        wait("act", t, book.before(f"t{p}", g.cnt["pe"]))
                        t_m = act(s.copy(MM_[:, p, :], bank[p][:, :]))
                        wait("pe", t_m)
                        g.take(bank[2 + p])
                        for n in range(NCH):
                            c = slice(n * CH, (n + 1) * CH)
                            for r in halves:
                                mm(bank[2 + p][r, c], TT[r, p, c], MM_[r, p, c])
                                ins = mm(bank[4 + p][r, c], MM_[r, p, c], TT[r, p, c])
                        t = book.name(f"t{p}", pe(ins))
                        wait("dve", t)
                        dve(v.tensor_tensor(TM_[:, p, :], TM_[:, p, :], bank[2 + p][:, :], ALU.add))
                        t = dve(v.tensor_tensor(TT[:, p, :], TT[:, p, :], bank[4 + p][:, :], ALU.add))
                g.settle()
                g.fence()
                dve(v.memset(G[:, :, :], 0.0))
                for n in range(NCH):
                    c = slice(n * CH, (n + 1) * CH)
                    wait("pe", g.latest["dve"])
                    for p in range(2):
                        o = slice(p * HD, (p + 1) * HD)
                        for r in halves:
                            if keys:
                                mm(bank[0][r, o], keys[0][r, p, c], keys[2][r, p, c], True, False)
                            ins = mm(bank[0][r, o], TIL[r, p, c], G[r, p, :], not keys, True)
                    t = pe(ins)
                    wait("dve", t)
                    x2, p2 = xr[:, :, :], bank[0][:, 0:2 * HD].rearrange("p (a d) -> p a d", a=2)
                    if keys:
                        dve(v.tensor_copy(x2, p2))
                    else:
                        dve(v.tensor_tensor(x2, p2, add[:, :, c], ALU.add))
                    wait("pe", g.latest["dve"])
                    for p in range(2):
                        for r in halves:
                            ins = mm(bank[1][r, p * HD:(p + 1) * HD], TT[r, p, c], xr[r, p, :])
                    t = pe(ins)
                    wait("dve", t)
                    dve(v.tensor_copy(ur[:, :, :], bank[1][:, 0:2 * HD].rearrange("p (a d) -> p a d", a=2)))
                    wait("pe", g.latest["dve"], g.latest["act"])
                    for p in range(2):
                        for r in halves:
                            mm(bank[2][r, p * CH:(p + 1) * CH], G[r, p, :], QT[r, p, c], True, False)
                            mm(bank[2][r, p * CH:(p + 1) * CH], ur[r, p, :], AQ[r, p, c], False, not keys)
                            if keys:
                                mm(bank[2][r, p * CH:(p + 1) * CH], keys[2][r, p, c], keys[1][r, p, c], False, True)
                            mm(bank[3][r, p * HD:(p + 1) * HD], KH[r, p, c], ur[r, p, :], True, not keys)
                            if keys:
                                mm(bank[3][r, p * HD:(p + 1) * HD], keys[3][r, p, c], keys[2][r, p, c], False, True)
                    t = pe(tn.matmul(bank[4][0:32, 0:32], ident[:, 0:32], ident[:, 0:32], start=True, stop=True))
                    wait("dve", t)
                    wait("act", t)
                    for p in range(2):
                        dve(v.scalar_tensor_tensor(out=G[:, p, :], in0=G[:, p, :], scalar=lam[:, p, n:n + 1],
                                                   in1=bank[3][:, p * HD:(p + 1) * HD], op0=ALU.mult, op1=ALU.add))
                        act(s.copy(out(p)[:, c], bank[2][:, p * CH:(p + 1) * CH]))
                g.fence()

        def deltanet():
            with ExitStack() as st:
                tiles = {n: g.sb(st, "gdn_" + n, [P, 2, T]) for n in ("at", "til", "qt", "aq", "kh", "bv")}
                lam = g.sb(st, "gdn_lam", [P, 2, NCH])
                B = g.sb(st, "gdn_gc", [P, T])
                BB = g.sb(st, "gdn_beta", [P, T])
                E = g.sb(st, "gdn_e", [P, T])
                DD = g.sb(st, "gdn_decay", [P, T])
                bc = g.sb(st, "gdn_col", [P, NCH])
                g.fence()
                for k in range(6):
                    dwconv(B, PJ[:, k, :], T, "gdn_conv_2", k, 6, 4, 3)
                    wait("act", g.latest["dve"])
                    act(s.activation(PJ[:, k, :], B[:, :], ACT.Silu))
                    wait("dve", g.latest["act"])
                for k in range(4):
                    dve(v.tensor_tensor(B[:, :], PJ[:, k, :], PJ[:, k, :], ALU.mult))
                    ps = head_sums(B[:, :], 0)
                    rsqrt(ps, 1.0, 1e-6, E[:, :])
                    dve(v.tensor_tensor(PJ[:, k, :], PJ[:, k, :], E[:, :], ALU.mult))
                    if k < 2:
                        dve(v.tensor_scalar(PJ[:, k, :], PJ[:, k, :], HD ** -0.5, None, ALU.mult))
                x, t1, t2, t3 = SL[0:4, :], B[0:4, :], BB[0:4, :], E[0:4, :]
                dve(v.tensor_scalar(x, x, vec("gdn_dt_bias_2", parts=4), None, ALU.add))
                softplus(x, t1, t2, t3)
                wait("act", g.latest["dve"])
                act(s.activation(SM[0:4, 0:1], vec("gdn_a_log_2", parts=4), ACT.Exp))
                act(s.activation(SL[32:36, :], SL[32:36, :], ACT.Sigmoid))
                wait("dve", g.latest["act"])
                dve(v.tensor_scalar(x, x, SM[0:4, 0:1], -1.0, ALU.mult, ALU.mult))
                dve(v.tensor_tensor_scan(t1, con("reset", p1=4), x, 0.0, ALU.mult, ALU.add))
                dve(v.tensor_copy(x, t1))
                for p in range(2):
                    q, k, val = PJ[:, p, :], PJ[:, 2 + p, :], PJ[:, 4 + p, :]
                    wait("pe", g.latest["dve"], g.latest["act"])
                    mm(bank[0][:, :], con("sela", p * P, P, 0, 4), SL[0:4, :])
                    t = pe(mm(bank[1][:, :], con("selb", p * P, P, 32, 36), SL[32:36, :]))
                    wait("dve", t)
                    dve(v.tensor_copy(B[:, :], bank[0][:, :]))
                    dve(v.tensor_copy(BB[:, :], bank[1][:, :]))
                    dve(v.tensor_tensor(fm3(E[:, :], NCH), fm3(B[:, :], NCH),
                                        con("i64").unsqueeze(1).broadcast_to([P, NCH, CH]), ALU.mult))
                    dve(v.tensor_reduce(bc[:, :], fm3(E[:, :], NCH), AXX, ALU.add))
                    dve(v.tensor_tensor(fm3(DD[:, :], NCH), fm3(B[:, :], NCH),
                                        bc[:, :].unsqueeze(2).broadcast_to([P, NCH, CH]), ALU.subtract))
                    dve(v.tensor_scalar(DD[:, :], DD[:, :], 0.0, None, ALU.min))
                    dve(v.tensor_tensor(fm3(E[:, :], NCH), last_of_chunk(B[:, :]), fm3(B[:, :], NCH), ALU.subtract))
                    wait("act", g.latest["dve"])
                    act(s.activation(DD[:, :], DD[:, :], ACT.Exp))
                    act(s.activation(E[:, :], E[:, :], ACT.Exp))
                    act(s.activation(B[:, :], B[:, :], ACT.Exp))
                    wait("dve", g.latest["act"])
                    dve(v.tensor_copy(lam[:, p, :], fm3(B[:, :], NCH)[:, :, CH - 1]))
                    dve(v.tensor_tensor(tiles["qt"][:, p, :], q, B[:, :], ALU.mult))
                    dve(v.scalar_tensor_tensor(out=tiles["til"][:, p, :], in0=k, scalar=-1.0, in1=B[:, :], op0=ALU.mult, op1=ALU.mult))
                    dve(v.tensor_tensor(tiles["til"][:, p, :], tiles["til"][:, p, :], BB[:, :], ALU.mult))
                    dve(v.tensor_tensor(E[:, :], E[:, :], k, ALU.mult))
                    to_rows(2, E[:, :], tiles["kh"][:, p, :])
                    dve(v.tensor_tensor(E[:, :], val, BB[:, :], ALU.mult))
                    to_rows(3, E[:, :], tiles["bv"][:, p, :])
                    ps = tile_products(4, k, k)
                    dve(v.tensor_tensor(E[:, :], ps, DD[:, :], ALU.mult))
                    dve(v.scalar_tensor_tensor(out=E[:, :], in0=E[:, :], scalar=-1.0, in1=BB[:, :], op0=ALU.mult, op1=ALU.mult))
                    masked(tiles["at"][:, p, :], E[:, :], con("strict"))
                    ps = tile_products(5, k, q)
                    dve(v.tensor_tensor(E[:, :], ps, DD[:, :], ALU.mult))
                    masked(tiles["aq"][:, p, :], E[:, :], con("incl"))
                delta("gdn", tiles["at"], tiles["til"], tiles["qt"], tiles["aq"], tiles["kh"], lam, tiles["bv"], None,
                      lambda p: YS[:, p, :])
                for p in range(2):
                    dve(v.tensor_tensor(B[:, :], YS[:, p, :], YS[:, p, :], ALU.mult))
                    ps = head_sums(B[:, :], 0)
                    rsqrt(ps, 1.0 / HD, EPS, E[:, :])
                    dve(v.scalar_tensor_tensor(out=YS[:, p, :], in0=YS[:, p, :], scalar=vec("gdn_norm_2"), in1=E[:, :],
                                               op0=ALU.mult, op1=ALU.mult))
                    silu_into(YS[:, p, :], PJ[:, GZ + p, :])
                g.fence()

        def head_norm(x, eps, tmp, r, b):
            ps = head_sums(x, b)
            dve(v.scalar_tensor_tensor(out=x, in0=ps, scalar=-1.0 / HD, in1=x, op0=ALU.mult, op1=ALU.add))
            dve(v.tensor_tensor(tmp, x, x, ALU.mult))
            ps = head_sums(tmp, b + 1)
            rsqrt(ps, 1.0 / HD, eps, r)
            dve(v.tensor_tensor(x, x, r, ALU.mult))

        def rwkv():
            with ExitStack() as st:
                tiles = {n: g.sb(st, "rw_" + n, [P, 2, T]) for n in ("at", "til", "qt", "aq", "kh", "aak", "ark", "v", "kv")}
                lam = g.sb(st, "rw_lam", [P, 2, NCH])
                up = g.sb(st, "rw_up", [P, 256])
                g.fence()
                t = g.load(up[:, :], a["rw_up"], "rwup")
                wait("pe", t)
                z = [PJ[:, k, :] for k in range(6)]
                for k in range(7):
                    x = PJ[:, RK + k, :]
                    dve(v.tensor_tensor(z[0][:, 1:T], x[:, 0:T - 1], x[:, 1:T], ALU.subtract))
                    dve(v.tensor_scalar(z[0][:, 0:1], x[:, 0:1], -1.0, None, ALU.mult))
                    dve(v.scalar_tensor_tensor(out=x, in0=z[0], scalar=vec("rw_mu_2", k), in1=x, op0=ALU.mult, op1=ALU.add))
                wa = PJ[:, RK + 6, :]
                wait("act", g.latest["dve"])
                act(s.activation(wa[0:64, :], wa[0:64, :], ACT.Tanh))
                for p in range(2):
                    r, k, val = PJ[:, RK + p, :], PJ[:, RK + 2 + p, :], PJ[:, RK + 4 + p, :]
                    wait("pe", g.latest["act"], g.latest["dve"])
                    mm(bank[0][:, :], up[0:64, p * P:(p + 1) * P], wa[0:64, :])
                    t = pe(mm(bank[1][:, :], up[64:128, p * P:(p + 1) * P], wa[64:128, :]))
                    wait("act", t)
                    lw, L, aa, kk, e = z[0], z[1], z[2], z[3], R[:, :]
                    act(s.activation(lw, bank[0][:, :], ACT.Sigmoid, bias=vec("rw_w0_2", p)))
                    act(s.activation(aa, bank[1][:, :], ACT.Sigmoid, bias=vec("rw_a0_2", p)))
                    wait("dve", g.latest["act"])
                    dve(v.tensor_scalar(lw, lw, -math.exp(-0.5), None, ALU.mult))
                    dve(v.tensor_tensor_scan(L, con("reset"), lw, 0.0, ALU.mult, ALU.add))
                    dve(v.tensor_scalar(kk, k, vec("rw_k_k_2", p), None, ALU.mult))
                    dve(v.tensor_tensor(e, kk, kk, ALU.mult))
                    ps = head_sums(e, 2)
                    rsqrt(ps, 1.0, 1e-6, e)
                    dve(v.tensor_tensor(kk, kk, e, ALU.mult))
                    dve(v.tensor_scalar(e, aa, 1.0, vec("rw_k_a_2", p), ALU.subtract, ALU.mult))
                    dve(v.scalar_tensor_tensor(out=k, in0=e, scalar=1.0, in1=k, op0=ALU.add, op1=ALU.mult))
                    dve(v.tensor_tensor(aa, aa, kk, ALU.mult))
                    dve(v.scalar_tensor_tensor(out=e, in0=r, scalar=vec("rw_r_k_2", p), in1=k, op0=ALU.mult, op1=ALU.mult))
                    ps = head_sums(e, 3)
                    dve(v.tensor_tensor(z[4 + p], ps, val, ALU.mult))
                    dve(v.tensor_tensor(lw, L, lw, ALU.subtract))
                    wait("act", g.latest["dve"])
                    act(s.activation(lw, lw, ACT.Exp))
                    act(s.activation(e, L, ACT.Exp))
                    wait("dve", g.latest["act"])
                    dve(v.scalar_tensor_tensor(out=tiles["til"][:, p, :], in0=kk, scalar=-1.0, in1=lw, op0=ALU.mult, op1=ALU.mult))
                    dve(v.tensor_tensor(tiles["qt"][:, p, :], r, e, ALU.mult))
                    dve(v.tensor_copy(lam[:, p, :], fm3(e, NCH)[:, :, CH - 1]))
                    dve(v.tensor_tensor(fm3(lw, NCH), last_of_chunk(L), fm3(L, NCH), ALU.subtract))
                    wait("act", g.latest["dve"])
                    act(s.activation(lw, lw, ACT.Exp))
                    act(s.activation(L, L, ACT.Exp, scale=-1.0))
                    wait("dve", g.latest["act"])
                    dve(v.tensor_tensor(e, aa, lw, ALU.mult))
                    to_rows(4, e, tiles["kh"][:, p, :])
                    dve(v.tensor_tensor(e, k, lw, ALU.mult))
                    to_rows(5, e, tiles["kv"][:, p, :])
                    to_rows(6, val, tiles["v"][:, p, :])
                    dve(v.tensor_tensor(aa, aa, L, ALU.mult))
                    dve(v.tensor_tensor(k, k, L, ALU.mult))
                    masked(tiles["at"][:, p, :], tile_products(7, aa, tiles["til"][:, p, :]), con("strict"))
                    masked(tiles["aak"][:, p, :], tile_products(0, k, tiles["til"][:, p, :]), con("strict"))
                    masked(tiles["aq"][:, p, :], tile_products(1, aa, tiles["qt"][:, p, :]), con("incl"))
                    masked(tiles["ark"][:, p, :], tile_products(2, k, tiles["qt"][:, p, :]), con("incl"))
                    g.fence()
                delta("rw", tiles["at"], tiles["til"], tiles["qt"], tiles["aq"], tiles["kh"], lam, None,
                      (tiles["aak"], tiles["ark"], tiles["v"], tiles["kv"]), lambda p: YS[:, 4 + p, :])
                for p in range(2):
                    y = YS[:, 4 + p, :]
                    head_norm(y, 64e-5, z[0], R[:, :], 0)
                    dve(v.tensor_scalar(y, y, vec("rw_gn_gain_2", p), vec("rw_gn_bias_2", p), ALU.mult, ALU.add))
                    dve(v.tensor_tensor(y, y, z[4 + p], ALU.add))
                    silu_into(y, PJ[:, RZ + p, :])
                g.fence()

        def spatial():
            with ExitStack() as st:
                ws = g.sb(st, "sg_w", [P, 4, P])
                bs = g.sb(st, "sg_b", [1, 4, P])
                vt = g.sb(st, "sg_v", [P, 4, 256])
                tmp = g.sb(st, "sg_tmp", [P, T])
                g.fence()
                t1 = g.load(ws[:, :, :], a["sg_w"].rearrange("p (g t) -> p g t", g=4), "sgw")
                t2 = g.load(bs[:, :, :], a["sg_b"].rearrange("o (g t) -> o g t", g=4), "sgb")
                wait("dve", t1)
                wait("pe", t2)
                dve(v.tensor_tensor(ws[:, :, :], ws[:, :, :], con("tril").unsqueeze(1).broadcast_to([P, 4, P]), ALU.mult))
                for k in range(2):
                    act(s.activation(PJ[:, SU + k, :], PJ[:, SU + k, :], ACT.Gelu_apprx_tanh))
                    act(s.activation(PJ[:, SV + k, :], PJ[:, SV + k, :], ACT.Gelu_apprx_tanh))
                wait("dve", g.latest["act"])
                for k in range(2):
                    x = PJ[:, SV + k, :]
                    head_norm(x, 1e-5, tmp[:, :], R[:, :], 0)
                    dve(v.tensor_scalar(x, x, vec("sg_ln_gain_2", k), vec("sg_ln_bias_2", k), ALU.mult, ALU.add))
                wait("pe", g.latest["dve"])
                for n in range(NT):
                    for k in range(2):
                        ins = tn.transpose(bank[2 + n % 2][:, k * P:(k + 1) * P], PJ[:, SV + k, n * P:(n + 1) * P], ident)
                    t = pe(ins)
                    wait("dve", t)
                    dve(v.tensor_copy(vt[:, n, :], bank[2 + n % 2][:, 0:256]))
                    wait("pe", g.latest["dve"])
                for k in range(2):
                    b = bank[4 + k]
                    for n in range(NT):
                        for j, r in enumerate(halves):
                            o = b[r, n * P:(n + 1) * P]
                            mm(o, vt[:, n, (2 * k + j) * 64:(2 * k + j + 1) * 64], ws[:, 2 * k + j, :], True, False)
                            ins = mm(o, con("ones", 0, 64, 0, 1), bs[:, 2 * k + j, :], False, True)
                    t = pe(tn.matmul(bank[6][0:32, 0:32], ident[:, 0:32], ident[:, 0:32], start=True, stop=True))
                    wait("dve", t)
                    y = YS[:, 2 + k, :]
                    dve(v.tensor_tensor(y, PJ[:, SU + k, :], b[:, :], ALU.mult))
                    silu_into(y, PJ[:, SZ + k, :])
                g.fence()

        def attention():
            NS = 512 + 384 + 32
            with ExitStack() as st:
                ks = g.sb(st, "ks", [P, T])
                kw = g.sb(st, "kw", [P, T])
                kc = g.sb(st, "kc", [P, 32])
                vs = g.sb(st, "vs", [P, NT, 2, HD])
                vc = g.sb(st, "vc", [32, HD])
                gt = g.sb(st, "gates", [P, NT, 12])
                cw = g.sb(st, "cmp_w1", [P, 32, HD])
                cw2 = g.sb(st, "cmp_w2", [P, HD])
                cp = g.sb(st, "cmp_pos", [P, 32])
                xc = g.sb(st, "cmp_x", [P, 32, NCMP])
                hc = g.sb(st, "cmp_h", [P, 32])
                nb = g.sb(st, "cmp_fill", [P, 4, 32])
                ps_ = g.sb(st, "scores", [P, 4, NS])
                pt = g.sb(st, "scores_t", [P, 2, 8 * P])
                ms = g.sb(st, "softmax", [P, 2, 12])
                g.fence()
                t = [g.load(cw[:, :, :], a["cmp_w1"].rearrange("p (j h) -> p j h", j=32), "cw1"),
                     g.load(cw2[:, :], a["cmp_w2"], "cw2"), g.load(cp[:, :], a["cmp_pos"], "cpos")]
                wait("pe", *t)
                wait("dve", *t)
                KC_, KS_, KW_ = (PJ[:, NKV + i, :] for i in range(3))
                for dst, src in ((ks, KS_), (kw, KW_)):
                    dve(v.tensor_copy(dst[0:64, :], src[0:64, :]))
                    dve(v.tensor_copy(dst[64:128, :], src[0:64, :]))
                for k in range(2):
                    dve(v.tensor_scalar(PJ[:, NQ + k, :], PJ[:, NQ + k, :], HD ** -0.5, None, ALU.mult))
                wait("act", g.latest["dve"])
                act(s.activation(SL[64:96, :], SL[64:96, :], ACT.Sigmoid))
                wait("pe", g.latest["dve"], g.latest["act"])
                for n in range(NT):
                    for q, src in enumerate((KS_, KW_)):
                        tn.transpose(bank[n][:, q * P:(q + 1) * P], src[:, n * P:(n + 1) * P], ident)
                    ins = tn.transpose(bank[n][:, 256:352], SL[:, n * P:(n + 1) * P], ident[0:96, 0:96])
                t = pe(ins)
                wait("dve", t)
                for n in range(NT):
                    dve(v.tensor_copy(vs[:, n, :, :], bank[n][:, 0:256].rearrange("p (q c) -> p q c", q=2)[:, :, 64:128]))
                    dve(v.tensor_copy(gt[:, n, :], bank[n][:, 320:332]))
                for h in range(2):
                    src = KC_[:, 16 * h:16 * h + 16 * NCMP].rearrange("p (n j) -> p j n", j=16)
                    dve(v.tensor_tensor(xc[:, 16 * h:16 * h + 16, :], src,
                                        cp[:, 16 * h:16 * h + 16].unsqueeze(2).broadcast_to([P, 16, NCMP]), ALU.add))
                wait("pe", g.latest["dve"])
                for r in halves:
                    for j in range(32):
                        mm(bank[4][r, 0:NCMP], cw[r, j, :], xc[r, j, :], j == 0, j == 31)
                t = pe(tn.matmul(bank[5][0:32, 0:32], ident[:, 0:32], ident[:, 0:32], start=True, stop=True))
                wait("act", t)
                act(s.activation(hc[:, 0:NCMP], bank[4][:, 0:NCMP], ACT.Gelu_apprx_tanh))
                wait("pe", g.latest["act"])
                for r in halves:
                    mm(bank[6][r, 0:NCMP], cw2[0:64, :], hc[0:64, 0:NCMP])
                mm(bank[7][0:NCMP, 0:HD], hc[64:128, 0:NCMP], cw2[64:128, :])
                t = pe(tn.matmul(bank[5][0:32, 0:32], ident[:, 0:32], ident[:, 0:32], start=True, stop=True))
                wait("dve", t)
                dve(v.tensor_copy(kc[:, 0:NCMP], bank[6][:, 0:NCMP]))
                dve(v.tensor_copy(vc[0:NCMP, :], bank[7][0:NCMP, 0:HD]))
                cm = con("cmask").rearrange("p (q n) -> p q n", q=4)
                cd = con("cdist").rearrange("p (q n) -> p q n", q=4)
                dve(v.tensor_scalar(nb[:, :, :], cm, BIG, -BIG, ALU.mult, ALU.add))
                g.fence()
                for c in range(NT):
                    n1, n2 = c + 1, min(c + 1, 3)
                    wait("pe", g.latest["dve"], g.latest["act"])
                    for h in range(4):
                        r = halves[h % 2]
                        q = PJ[r, NQ + h // 2, c * P:(c + 1) * P]
                        mm(bank[2 * h][:, 0:n1 * P], q, ks[r, 0:n1 * P])
                        mm(bank[2 * h + 1][:, 0:n2 * P], q, kw[r, (c + 1 - n2) * P:(c + 1) * P])
                        ins = mm(bank[2 * h + 1][:, 384:384 + NCMP], q, kc[r, 0:NCMP])
                    t = pe(tn.matmul(bank[7][0:32, 448:480], ident[:, 0:32], ident[:, 0:32], start=True, stop=True))
                    wait("dve", t)
                    spans = [(0, n1 * P), (512, 512 + n2 * P), (896, 896 + NCMP)]
                    for h in range(4):
                        dst = ps_[:, h, :]
                        dve(v.scalar_tensor_tensor(out=dst[:, 0:n1 * P], in0=con("dist", 384 - P * c), scalar=-SLOPES[h],
                                                   in1=bank[2 * h][:, 0:n1 * P], op0=ALU.mult, op1=ALU.add))
                        dve(v.scalar_tensor_tensor(out=dst[:, 512:512 + n2 * P], in0=con("distw", 384 - P * n2), scalar=-SLOPES[h],
                                                   in1=bank[2 * h + 1][:, 0:n2 * P], op0=ALU.mult, op1=ALU.add))
                        x = dst[:, 896:896 + NCMP]
                        dve(v.scalar_tensor_tensor(out=x, in0=cd[:, c, 0:NCMP], scalar=-SLOPES[h],
                                                   in1=bank[2 * h + 1][:, 384:384 + NCMP], op0=ALU.mult, op1=ALU.add))
                        dve(v.tensor_tensor(x, x, cm[:, c, 0:NCMP], ALU.mult))
                        dve(v.tensor_tensor(x, x, nb[:, c, 0:NCMP], ALU.add))
                        for b, (lo, hi) in enumerate(spans):
                            dve(v.tensor_reduce(ms[:, 0, 3 * h + b:3 * h + b + 1], dst[:, lo:hi], AXX, ALU.max, negate=True))
                        wait("act", g.latest["dve"])
                        for b, (lo, hi) in enumerate(spans):
                            i = 3 * h + b
                            act(s.activation(dst[:, lo:hi], dst[:, lo:hi], ACT.Exp, bias=ms[:, 0, i:i + 1], accum_out=ms[:, 1, i:i + 1]))
                    wait("dve", g.latest["act"])
                    dve(v.reciprocal(ms[:, 1, :], ms[:, 1, :]))
                    go = ms[:, 0, :]
                    order = (1, 2, 0)
                    for h in range(4):
                        for b in range(3):
                            i = 3 * h + b
                            dve(v.tensor_tensor(ms[:, 0, i:i + 1], ms[:, 1, i:i + 1],
                                                gt[:, c, 3 * h + order[b]:3 * h + order[b] + 1], ALU.mult))
                    for h in range(4):
                        dst = ps_[:, h, :]
                        for b, (lo, hi) in enumerate(spans):
                            i = 3 * h + b
                            dve(v.tensor_scalar(dst[:, lo:hi], dst[:, lo:hi], ms[:, 0, i:i + 1], None, ALU.mult))
                        dve(v.tensor_tensor(dst[:, 896:896 + NCMP], dst[:, 896:896 + NCMP], cm[:, c, 0:NCMP], ALU.mult))
                        wait("pe", g.latest["dve"])
                        blocks = [(j * P, P, vs[:, j, 0, :]) for j in range(n1)]
                        blocks += [(512 + j * P, P, vs[:, c + 1 - n2 + j, 1, :]) for j in range(n2)]
                        blocks += [(896, NCMP, vc[0:NCMP, :])]
                        bb = [bank[(2 * h) % 4], bank[(2 * h) % 4 + 1]]
                        for j, (o, w, _) in enumerate(blocks):
                            ins = tn.transpose(bb[j // 4][0:w, (j % 4) * P:(j % 4 + 1) * P], ps_[:, h, o:o + w], ident)
                        t = pe(ins)
                        wait("act", t)
                        nbk = len(blocks)
                        for j in range(0, nbk - 1, 4):
                            m = min(4, nbk - 1 - j)
                            act(s.copy(pt[:, h % 2, j * P:(j + m) * P], bb[j // 4][:, 0:m * P]))
                        j = nbk - 1
                        act(s.copy(pt[0:NCMP, h % 2, j * P:(j + 1) * P], bb[j // 4][0:NCMP, (j % 4) * P:(j % 4 + 1) * P]))
                        wait("pe", g.latest["act"])
                        ob = bank[4 + h // 2]
                        for j, (o, w, val) in enumerate(blocks):
                            ins = mm(ob[halves[h % 2], 0:P], val, pt[0:w, h % 2, j * P:(j + 1) * P], j == 0, j == nbk - 1)
                        t = pe(ins)
                        if h % 2:
                            wait("act", t)
                            act(s.copy(YS[:, 6 + h // 2, c * P:(c + 1) * P], ob[:, 0:P]))
                    g.fence()
                for k in range(2):
                    silu_into(YS[:, 6 + k, :], PJ[:, NZ + k, :])
                g.fence()

        spatial()
        deltanet()
        rwkv()
        attention()
        with ExitStack() as st:
            mix = g.sb(st, "mixed", [P, KD, T])
            wm = g.sb(st, "merge_w", [P, 5, KD, P])
            sg = g.sb(st, "merge_g", [P, 4, T])
            g.fence()
            with book.run(KD) as m:
                cpe, cdve, cact = g.cnt["pe"], g.cnt["dve"], g.cnt["act"]
                tw = []
                for q in range(5):
                    wait("sp", book.before(f"mw{q}", cpe))
                    src = wblock("w_in_2")(m + NPROJ + 8 * q) if q < 4 else wblock("w_branch")(m)
                    tw.append(g.load(wm[:, q, :, :], src, f"merge{q}"))
                for q in range(4):
                    wait("pe", tw[q], book.before(f"mg{q}", cact))
                    for k in range(KD):
                        ins = mm(bank[q][:, :], wm[:, q, k, :], H[:, k, :], k == 0, k == KD - 1)
                    t = book.name(f"mw{q}", pe(ins))
                    wait("act", t, book.before(f"ms{q}", cdve))
                    book.name(f"mg{q}", act(s.activation(sg[:, q, :], bank[q][:, :], ACT.Sigmoid)))
                wait("pe", tw[4])
                t_y = []
                for q in range(4):
                    wait("pe", book.before(f"ms{q}", cdve))
                    for k in range(2):
                        ins = mm(bank[4 + q][:, :], wm[:, 4, 2 * q + k, :], YS[:, 2 * q + k, :], k == 0, k == 1)
                    t_y.append(pe(ins))
                book.name("mw4", t_y[-1])
                wait("dve", g.latest["act"])
                row = mix[:, bass.ds(m, 1), :].rearrange("p o t -> p (o t)")
                for q in range(4):
                    wait("dve", t_y[q])
                    if q == 0:
                        t = dve(v.tensor_tensor(row, sg[:, 0, :], bank[4][:, :], ALU.mult))
                    else:
                        t = dve(v.tensor_tensor(sg[:, q, :], sg[:, q, :], bank[4 + q][:, :], ALU.mult))
                        t = dve(v.tensor_tensor(row, row, sg[:, q, :], ALU.add))
                    book.name(f"ms{q}", t)
            g.settle()
            g.fence()

            def ev_out(i, ps, e):
                xi = X[:, bass.ds(i, 1), :].rearrange("p o t -> p (o t)")
                return dve(v.tensor_tensor(xi, ps, xi, ALU.add))

            project(KD, wblock("w_out_2"), lambda k: mix[:, k, :], T, ev_out)


def columns(x):
    return np.ascontiguousarray(x).reshape(-1, P).T


def weight_blocks(w):
    k, n = w.shape
    return np.ascontiguousarray(w.reshape(k // P, P, n // P, P).transpose(2, 1, 0, 3).reshape(n // P, P, -1))


def feature_major(x):
    t, d = x.shape
    return np.ascontiguousarray(x.T.reshape(d // P, P, t).transpose(1, 0, 2).reshape(P, -1))


def arrange(inp):
    A = {k: np.asarray(x) for k, x in inp.items()}
    vecs = np.zeros((P, NVEC), np.float32)
    for name, w in VEC:
        o = VOFF[name]
        if name in ("filt_freq0", "filt_freq1"):
            vecs[:FHID, o] = A["filt_freq"][0, int(name[-1])]
        elif name in ("filt_b1", "filt_b2"):
            vecs[:FHID, o] = A[name][0]
        elif name in ("gdn_a_log_2", "gdn_dt_bias_2"):
            vecs[:4, o] = A[name][0]
        elif name == "gdn_norm_2":
            vecs[:64, o] = A[name][0]
            vecs[64:, o] = A[name][0]
        else:
            vecs[:, o:o + w] = columns(A[name])
    f = {"vecs": vecs, "consts": shape_constants()}
    f["dft"], f["idft"], f["filt_z"], f["window"] = dft_constants()
    f["x_fm"] = feature_major(A["x"][0])
    f["ctx_fm"] = feature_major(A["ctx"][0])
    f["w_mod"] = A["w_mod"]
    f["w_in"] = weight_blocks(A["w_in"][0])
    lw = np.stack([A["lru_wr"][0], A["lru_wi"][0]], 2).reshape(2, 4, 2, 2, 64, 64)
    f["lru_w"] = np.ascontiguousarray(lw.transpose(2, 4, 0, 1, 3, 5).reshape(2, 64, 16, 64))
    f["filt_w1"], f["filt_w2"], f["filt_w3"], f["filt_b3"] = (A["filt_w1"][0], A["filt_w2"][0], A["filt_w3"][0],
                                                             A["filt_b3"][0:1])
    for n in ("w_out", "cf_w1", "cf_w2", "w_out_2"):
        f[n] = weight_blocks(A[n][0])
    f["router"] = np.ascontiguousarray(A["router"].reshape(2, KD, P, NE).transpose(0, 2, 1, 3).reshape(2, P, -1))
    for n in ("exp_w1", "exp_w3", "exp_w2"):
        f[n] = A[n]
    w2 = A["w_in_2"][0]
    cols = np.r_[0:768, 776:3592, 3604:7956]
    f["w_in_2"] = weight_blocks(w2[:, cols])
    small = np.zeros((D, 96), np.float32)
    small[:, 0:4], small[:, 32:36], small[:, 64:76] = w2[:, 768:772], w2[:, 772:776], w2[:, 3592:3604]
    f["w_small"] = np.ascontiguousarray(small.reshape(KD, P, 96).transpose(1, 0, 2).reshape(P, -1))
    f["rw_up"] = np.concatenate([A["rw_w_up_2"][0], A["rw_a_up_2"][0]], 0)
    f["sg_w"] = np.ascontiguousarray(A["sg_w_s_2"][0].transpose(2, 0, 1).reshape(P, -1))
    f["sg_b"] = A["sg_b_s_2"][0].reshape(1, -1)
    f["cmp_w1"] = np.ascontiguousarray(A["nsa_cmp_w1_2"][0].reshape(2, 32, 64, 64).transpose(0, 2, 1, 3).reshape(P, -1))
    f["cmp_w2"] = A["nsa_cmp_w2_2"][0].reshape(P, 64)
    f["cmp_pos"] = np.ascontiguousarray(A["nsa_cmp_pos_2"][0].transpose(0, 2, 1).reshape(P, 32))
    f["w_branch"] = weight_blocks(A["w_branch_2"][0].reshape(D, D))
    return {k: np.ascontiguousarray(x) for k, x in f.items()}


def program(make, shapes):
    plan = {}
    for _ in range(2):
        nc = make()
        a = {n: nc.dram_tensor("in_" + n, shape, F32, kind="ExternalInput").ap() for n, shape in shapes.items()}
        a["out"] = nc.dram_tensor("out_0", (P, KD * T), F32, kind="ExternalOutput").ap()
        plan, before = build(nc, a, plan), plan
    assert plan == before
    return nc


def kernel(**inputs):
    import concourse.bacc as bacc
    from concourse.bass_utils import run_bass_kernel_spmd

    f = arrange(inputs)
    nc = program(lambda: bacc.Bacc("TRN2", target_bir_lowering=False, num_devices=1), {n: x.shape for n, x in f.items()})
    r = run_bass_kernel_spmd(nc, [{"in_" + n: x for n, x in f.items()}], core_ids=[0])
    out = r.results[0]["out_0"].reshape(P, KD, T)
    return np.ascontiguousarray(out.transpose(2, 1, 0).reshape(1, T, D))
```

```python
import math
from contextlib import ExitStack, contextmanager

import numpy as np

import concourse.bass as bass
from concourse import mybir

F32 = mybir.dt.float32
ALU = mybir.AluOpType
ACT = mybir.ActivationFunctionType
AXX = mybir.AxisListType.X

P = 128
T = 512
D = 1024
KD = D // P
NT = T // P
TC = 256
NE = 16
CAP = 2 * T // NE
FF = 1024
RW = 512
KR = RW // P
HD = 64
CH = 64
NCH = T // CH
LRU_C = 8.0
EPS = 1e-6
GRID_W = 64
CF_K = 31
NMOD = 6
FEMB, FHID = 33, 64
BIG = 1e30
NCMP = T // 16 - 1
SLOPES = [2.0 ** (-8.0 * (h + 1) / 4) for h in range(4)]
NRING = 12
LEVELS = 6

VEC = [("norm1_g", 16), ("norm2_g", 16), ("b_mod", 96), ("conv_a_w", 16), ("conv_a_b", 4),
       ("lru_br", 8), ("lru_bi", 8), ("lru_lam", 8), ("conv_b_w", 36), ("conv_b_b", 12),
       ("filt_bias", 8), ("cf_b1", 16), ("cf_dw_w", CF_K * 8), ("cf_dw_b", 8), ("cf_ln_g", 8),
       ("cf_ln_b", 8), ("cf_b2", 8), ("final_g", 8), ("norm_gain_2", 8), ("gdn_conv_2", 24),
       ("sg_ln_gain_2", 2), ("sg_ln_bias_2", 2), ("rw_mu_2", 7), ("rw_w0_2", 2), ("rw_a0_2", 2),
       ("rw_k_k_2", 2), ("rw_k_a_2", 2), ("rw_r_k_2", 2), ("rw_gn_gain_2", 2), ("rw_gn_bias_2", 2),
       ("final_gain_2", 8), ("c", 8), ("c_ctx", 8),
       ("gdn_norm_2", 1), ("filt_b1", 1), ("filt_b2", 1), ("filt_freq0", 1), ("filt_freq1", 1),
       ("gdn_a_log_2", 1), ("gdn_dt_bias_2", 1)]
VOFF, _n = {}, 0
for _name, _w in VEC:
    VOFF[_name] = _n
    _n += _w
NVEC = _n

CONST = [("ident", 128), ("ones", 128), ("blk1", 128), ("i64", 64), ("strict", 64), ("incl", 64),
         ("level", LEVELS * 64), ("reset", 512), ("sela", 256), ("selb", 256),
         ("iota", 128), ("dist", 512), ("distw", 384), ("cdist", 4 * 32), ("cmask", 4 * 32),
         ("tril", 128), ("pi", 1)]
COFF, _n = {}, 0
for _name, _w in CONST:
    COFF[_name] = _n
    _n += _w
NCONST = _n


def shape_constants():
    c = np.zeros((P, NCONST), np.float32)
    p = np.arange(P)[:, None]

    def put(name, a):
        c[:a.shape[0], COFF[name]:COFF[name] + a.shape[1]] = a

    t64 = np.arange(64)[None, :]
    put("ident", np.eye(P))
    put("ones", np.ones((P, P)))
    put("blk1", (p // 64 == np.arange(P)[None, :] // 64) * 1.0)
    put("i64", (p % 64 == t64) * 1.0)
    put("strict", (p % 64 < t64) * 1.0)
    put("incl", (p % 64 <= t64) * 1.0)
    put("level", np.concatenate([((t64 // b) % 2 == 1) * ((p % 64) // b == t64 // b - 1) * 1.0
                                 for b in (1 << i for i in range(LEVELS))], 1))
    put("reset", np.tile((np.arange(T) % CH != 0)[None, :] * 1.0, (P, 1)))
    sel = np.zeros((4, 2, P))
    for h in range(4):
        sel[h, h // 2, 64 * (h % 2):64 * (h % 2) + 64] = 1.0
    put("sela", sel.reshape(4, 256))
    c[32:36, COFF["selb"]:COFF["selb"] + 256] = sel.reshape(4, 256)
    put("iota", np.tile(np.arange(P)[None, :] % 64, (P, 1)))
    m = np.arange(512)[None, :]
    d = p + 384 - m
    put("dist", np.where(d >= 0, d, BIG))
    m = np.arange(384)[None, :]
    d = p + 256 - m
    put("distw", np.where((d >= 0) & (d < 256), d, BIG))
    cd, cm = np.zeros((P, 4, 32)), np.zeros((P, 4, 32))
    for q in range(4):
        d = (128 * q + p) - (16 * np.arange(32)[None, :] + 31)
        cm[:, q] = (d >= 0) & (np.arange(32)[None, :] < NCMP)
        cd[:, q] = d * cm[:, q]
    put("cdist", cd.reshape(P, -1))
    put("cmask", cm.reshape(P, -1))
    put("tril", (p <= np.arange(P)[None, :]) * 1.0)
    put("pi", np.full((P, 1), math.pi))
    return c


def dft_constants():
    k, t = np.arange(T), np.arange(T)
    ang = 2 * np.pi * np.outer(t, k) / (2 * T)
    fwd = np.concatenate([np.cos(ang), -np.sin(ang)], 1)
    fwd[:, T] = (-1.0) ** t
    inv = np.concatenate([2 * np.cos(ang.T), -2 * np.sin(ang.T)], 0) / (2 * T)
    inv[0] = 1.0 / (2 * T)
    inv[T] = (-1.0) ** t / (2 * T)
    fwd = fwd.reshape(NT, P, 2 * T).transpose(1, 0, 2).reshape(P, -1)
    inv = inv.reshape(2 * NT, P, T).transpose(1, 0, 2).reshape(P, -1)
    tt = np.linspace(0.0, 1.0, T)[:, None]
    bands = (FEMB - 1) // 2
    w = (2.0 * math.pi / T) * np.arange(T)[:, None]
    f = np.linspace(1e-4, bands - 1, bands)[None, :]
    z = np.concatenate([tt, np.cos(f * w), -np.sin(f * w)], -1)
    deltas = np.abs(np.linspace(math.log(1e-2) / 1.5, math.log(1e-2) / 0.3, RW))
    win = np.exp(-tt * deltas[None, :]) + 0.05
    win = win.reshape(NT, P, RW).transpose(1, 0, 2).reshape(P, -1)
    return [np.ascontiguousarray(a.astype(np.float32)) for a in (fwd, inv, z.T, win)]


class Token:

    def __init__(self, sem, value, loop=None, owner=None):
        self.sem, self.value, self.loop, self.owner = sem, value, loop, owner


class Counter:

    def __init__(self, book, name, step=1):
        self.book, self.name, self.step = book, name, step
        self.sem = book.nc.alloc_semaphore(name)
        self.count = 0

    def mark(self, ins):
        ins.then_inc(self.sem, self.step)
        self.count += self.step
        return Token(self, self.count, self.book.loop)


class Book:

    def __init__(self, nc, plan):
        self.nc, self.plan, self.loop = nc, plan, None
        self.counters = {}
        self.loops = 0
        self.names = {}
        self.fresh = {}

    def counter(self, name, step=1):
        if name not in self.counters:
            self.counters[name] = Counter(self, name, step)
        return self.counters[name]

    @contextmanager
    def run(self, n):
        lid = f"loop{self.loops}"
        self.loops += 1
        base = {k: c.count for k, c in self.counters.items()}
        per = self.plan.get(lid, {})
        with self.nc.Fori(0, n) as i:
            self.loop = (lid, i, base, per)
            self.names = {}
            yield i
            self.loop = None
        seen = {k: c.count - base.get(k, 0) for k, c in self.counters.items()}
        self.fresh[lid] = dict(seen, marks={k: t.value - base.get(t.sem.name, 0) for k, t in self.names.items()})
        for k, c in self.counters.items():
            c.count = base.get(k, 0) + n * seen[k]
        self.last = (lid, base, seen, n)

    def after(self, tok):
        lid, base, seen, n = self.last
        return Token(tok.sem, tok.value + (n - 1) * seen[tok.sem.name])

    def value(self, tok):
        if tok.loop is None:
            return tok.value
        lid, i, base, per = tok.loop
        assert self.loop is not None and self.loop[0] == lid
        return i * per.get(tok.sem.name, 0) + tok.value

    def name(self, key, tok):
        self.names[key] = tok
        return tok

    def later(self, key, counter):
        lid, i, base, per = self.loop
        return Token(counter, base.get(counter.name, 0) + per.get("marks", {}).get(key, 1), self.loop)

    def before(self, key, counter):
        lid, i, base, per = self.loop
        rise = per.get(counter.name, 0)
        off = per.get("marks", {}).get(key, 0)
        start = base.get(counter.name, 0)
        assert start - rise + off > 0 or not per, (key, start, rise)
        return Token(counter, start - rise + off, self.loop)


class Program:
    def __init__(self, nc, a, plan):
        self.nc, self.a = nc, a
        self.book = Book(nc, plan)
        b = self.book
        self.eng = {"pe": nc.tensor, "dve": nc.vector, "act": nc.scalar, "pool": nc.gpsimd, "sp": nc.sync}
        self.cnt = {k: b.counter(f"{k}_done") for k in self.eng}
        self.latest = {k: None for k in self.eng}
        self.resting = False
        self.background = None
        self.bank_free = {5: None}

    def wait(self, engine, *toks):
        for t in toks:
            if t is not None:
                self.eng[engine].wait_ge(t.sem.sem, self.book.value(t))

    def _step(self, engine, ins):
        t = self.cnt[engine].mark(ins)
        self.wait(engine, t)
        self.latest[engine] = t
        return t

    def dve(self, ins):
        return self._step("dve", ins)

    def act(self, ins):
        return self._step("act", ins)

    def pool(self, ins):
        return self._step("pool", ins)

    def pe(self, ins):
        t = self.cnt["pe"].mark(ins)
        self.latest["pe"] = t
        return t

    def load(self, dst, src, stream, engine="sync"):
        c = self.book.counter("dma_" + stream, 16)
        e = {"sync": self.nc.sync, "act": self.nc.scalar}[engine]
        return c.mark(e.dma_start(dst, src))

    def fence(self, *extra, skip=None):
        toks = [t for t in self.latest.values() if t is not None] + list(extra)
        for e in self.eng:
            if e == skip:
                continue
            for t in toks:
                if t.sem is not self.cnt[e]:
                    self.wait(e, t)

    def settle(self):
        for k, c in self.cnt.items():
            if c.count:
                self.latest[k] = Token(c, c.count)

    def mm(self, out, lhsT, rhs, start=True, stop=True):
        return self.nc.tensor.matmul(out, lhsT, rhs, start=start, stop=stop, skip_group_check=True)

    def spare(self):
        if self.background is not None:
            next(self.background, None)

    def rest(self):
        self.resting = True
        while self.background is not None and next(self.background, "idle") != "idle":
            pass
        self.resting = False

    def sb_top(self, name, shape):
        return self.sb(self.top_stack, name, shape)

    def take(self, bank):
        one = self.con("ident", 0, 32)
        self.mm(bank[0:32, 0:1], one, one[:, 0:1])

    def sb(self, stack, name, shape):
        return stack.enter_context(self.nc.sbuf_tensor(name, shape, F32))

    def vec(self, name, i=0, n=1, parts=P):
        o = VOFF[name] + i
        return self.V[0:parts, o:o + n]

    def con(self, name, i=0, n=None, p0=0, p1=P):
        o = COFF[name] + i
        return self.C[p0:p1, o:o + (n if n is not None else dict(CONST)[name] - i)]


def fm3(ap, n):
    return ap.rearrange("p (n t) -> p n t", n=n)


def build(nc, a, plan):
    g = Program(nc, a, plan)
    book, wait, dve, act, pe, mm = g.book, g.wait, g.dve, g.act, g.pe, g.mm
    v, s, tn = nc.vector, nc.scalar, nc.tensor
    top = ExitStack()
    with top:
        g.V = g.sb(top, "vecs", [P, NVEC])
        g.C = g.sb(top, "consts", [P, NCONST])
        X = g.sb(top, "residual", [P, KD, T])
        H = g.sb(top, "normed", [P, KD, T])
        R = g.sb(top, "rms", [P, T])
        SQ = g.sb(top, "squares", [P, 2, T])
        W = g.sb(top, "wring", [P, 2, KD, P])
        MOD = g.sb(top, "mods", [P, 2, 48, 2])
        SM = g.sb(top, "small", [P, 64])
        mrow = g.rowtile = g.sb(top, "mod_rows", [P, 512])
        bank = [top.enter_context(nc.psum_tensor(f"bank{i}", [P, 512], F32)) for i in range(8)]
        vec, con = g.vec, g.con
        ident = con("ident")

        t_v = g.load(g.V[:, :], a["vecs"], "vecs")
        t_c = g.load(g.C[:, :], a["consts"], "consts")
        for e in ("dve", "act", "pe", "pool"):
            wait(e, t_v, t_c)
        ring_used = book.counter("ring_used")
        for _ in range(24):
            t_ring = ring_used.mark(mm(bank[0][0:32, 0:1], ident[:, 0:32], ident[:, 0:1]))
        g.fence(t_ring)

        def rms_rows(src, kd, n, eps, out, width):
            b = bank[7]
            free = [None, None]
            wait("act", g.latest["dve"])
            for k in range(kd):
                wait("act", free[k % 2])
                t = act(s.activation(SQ[:, k % 2, 0:n], src(k), ACT.Square))
                wait("pe", t)
                free[k % 2] = pe(mm(b[:, 0:n], con("ones"), SQ[:, k % 2, 0:n], k == 0, k == kd - 1))
                g.spare()
            wait("dve", free[(kd - 1) % 2])
            rsqrt(b[:, 0:n], 1.0 / width, eps, out[:, 0:n])

        def rsqrt(psum, scale, eps, out):
            t = dve(v.tensor_scalar(out, psum, scale, eps, ALU.mult, ALU.add))
            wait("act", t)
            t = act(s.activation(out, out, ACT.Sqrt))
            wait("dve", t)
            dve(v.reciprocal(out, out))

        def project(n_chunks, wsrc, rhs, n, evac, kd=KD):
            project_pairs(n_chunks // 2, lambda i, j: wsrc(i * 2 + j), rhs, n, lambda i, j, ps: evac(i * 2 + j, ps, "dve"), kd)

        def project_pairs(n_pairs, wsrc, rhs, n, evac, kd=KD):
            with book.run(n_pairs) as i:
                for j in range(2):
                    wait("sp", book.before(f"mm{j}", g.cnt["pe"]))
                    t_w = g.load(W[:, j, 0:kd, :], wsrc(i, j), f"w{j}")
                    wait("pe", t_w, book.before(f"ev{j}", g.cnt["dve"]))
                    for k in range(kd):
                        ins = mm(bank[j][:, 0:n], W[:, j, k, :], rhs(k), k == 0, k == kd - 1)
                    t_m = book.name(f"mm{j}", pe(ins))
                    wait("dve", t_m)
                    book.name(f"ev{j}", evac(i, j, bank[j][:, 0:n]))
            g.settle()
            g.fence()

        def wblock(name):
            return lambda i: a[name][bass.ds(i, 1), :, :].rearrange("o p (k c) -> p (o k) c", c=P)

        def adaln_steps(layer, wm, cs):
            src = a["w_mod"][layer].rearrange("(k p) c -> k p c", p=P)
            used, loaded = {}, {}

            def fetch(n):
                if n < 24:
                    wait("sp", used.get(n - 4))
                    loaded[n] = g.load(wm[:, n % 4, :], src[n % KD][:, (n // KD) * 2048:(n // KD + 1) * 2048], f"wm{n % 4}")

            for n in range(4):
                fetch(n)
            t_row = None
            for n in range(24):
                i, k = n // KD, n % KD
                wait("pe", loaded[n], t_row if k == 0 else None)
                for q in range(4):
                    ins = mm(bank[4][32 * q:32 * q + 32, :], cs[:, k, :], wm[:, n % 4, 512 * q:512 * q + 512], k == 0, k == KD - 1)
                used[n] = pe(ins)
                fetch(n + 4)
                if k == KD - 1:
                    wait("dve", used[n], g.bank_free[5])
                    t_row = dve(v.tensor_copy(mrow[:, :], bank[4][:, :]))
                    wait("pe", t_row)
                    for j in range(4):
                        ins = tn.transpose(bank[5][:, j * P:(j + 1) * P], mrow[:, j * P:(j + 1) * P], ident)
                    wait("dve", pe(ins))
                    turned = bank[5][:, :].rearrange("p (j q r) -> p q j r", q=4, r=32)
                    bias = vec("b_mod", 48 * layer + 16 * i, 16).rearrange("p (q j) -> p q j", q=4)
                    for r in range(2):
                        o = MOD[:, layer, 16 * i:16 * i + 16, r].rearrange("p (q j) -> p q j", q=4)
                        g.bank_free[5] = dve(v.tensor_tensor(o, turned[:, :, :, r], bias, ALU.add))
                yield

        GA = g.sb(top, "gains", [P, 5, 8])

        def gain_of(slot, norm, off, layer, scale_chunk, r=0):
            dve(v.tensor_scalar(GA[:, slot, :], MOD[:, layer, scale_chunk:scale_chunk + 8, r], 1.0, None, ALU.add))
            dve(v.tensor_tensor(GA[:, slot, :], GA[:, slot, :], vec(norm, off, 8), ALU.mult))

        def modulate(src, n, slot, shift, dst):
            for k in range(KD):
                t = dve(v.scalar_tensor_tensor(out=dst(k), in0=src(k), scalar=GA[:, slot, k:k + 1], in1=R[:, 0:n],
                                               op0=ALU.mult, op1=ALU.mult))
                wait("act", t)
                act(s.activation(dst(k), dst(k), ACT.Identity, bias=shift(k)))

        def softplus(x, tmp, tmp2, tmp3):
            wait("act", g.latest["dve"])
            act(s.activation(tmp, x, ACT.Abs))
            act(s.activation(tmp, tmp, ACT.Exp, scale=-1.0))
            wait("dve", g.latest["act"])
            dve(v.tensor_scalar(tmp2, tmp, 2.0, None, ALU.add))
            dve(v.reciprocal(tmp2, tmp2))
            dve(v.tensor_tensor(tmp, tmp, tmp2, ALU.mult))
            dve(v.tensor_tensor(tmp2, tmp, tmp, ALU.mult))
            dve(v.tensor_scalar(tmp3, tmp2, 1.0 / 15, None, ALU.mult))
            for d in (13, 11, 9, 7, 5, 3):
                dve(v.scalar_tensor_tensor(out=tmp3, in0=tmp3, scalar=1.0 / d, in1=tmp2, op0=ALU.add, op1=ALU.mult))
            dve(v.scalar_tensor_tensor(out=tmp, in0=tmp3, scalar=1.0, in1=tmp, op0=ALU.add, op1=ALU.mult))
            dve(v.tensor_scalar(x, x, 0.0, None, ALU.max))
            dve(v.scalar_tensor_tensor(out=x, in0=tmp, scalar=2.0, in1=x, op0=ALU.mult, op1=ALU.add))

        def dwconv(dst, src, n, wname, w0, stride, ntap, lead, bname=None, b0=0):
            if bname is None:
                t = dve(v.tensor_scalar(dst[:, 0:n], src[:, 0:n], vec(wname, w0 + lead * stride), None, ALU.mult))
            else:
                t = dve(v.tensor_scalar(dst[:, 0:n], src[:, 0:n], vec(wname, w0 + lead * stride), vec(bname, b0),
                                    ALU.mult, ALU.add))
            for j in range(ntap):
                d = j - lead
                if d == 0:
                    continue
                lo, hi = max(0, -d), min(n, n - d)
                t = dve(v.scalar_tensor_tensor(out=dst[:, lo:hi], in0=src[:, lo + d:hi + d], scalar=vec(wname, w0 + j * stride),
                                           in1=dst[:, lo:hi], op0=ALU.mult, op1=ALU.add))
            return t

        LW = g.sb(top, "lru_state", [P, 2, 4])
        SPL = g.sb(top, "lru_rate", [P, 3, 8])

        def rglru(raw, n, gw, hh, ig, hs, context):
            t_e = {}
            xa = g.sb_top(f"xa{n}", [P, 2, n])
            for k in range(KR):
                x = xa[:, k % 2, :]
                dwconv(x, raw(k), n, "conv_a_w", k, KR, 4, 1, "conv_a_b", k)
                t = dve(v.tensor_copy(raw(k), x))
                wait("pe", t)
                for d in range(2):
                    j, b = d * KR + k, 2 * (k % 2) if d == 0 else 2 * (k % 2) + 1
                    b0, b1 = bank[0 + 2 * d], bank[1 + 2 * d]
                    wait("pe", t_e.get(d))
                    mm(b0[:, 0:n], gw[:, 2 * j, :], raw(k))
                    t = pe(mm(b1[:, 0:n], gw[:, 2 * j + 1, :], raw(k)))
                    wait("act", t)
                    act(s.activation(hh[:, j, :], b0[:, 0:n], ACT.Sigmoid, bias=vec("lru_br", j)))
                    t_e[d] = act(s.activation(ig[:, j, :], b1[:, 0:n], ACT.Sigmoid, bias=vec("lru_bi", j)))
                    act(s.activation(hh[:, j, :], hh[:, j, :], ACT.Tanh, scale=SPL[:, 1, j:j + 1]))
                    g.spare()
                    if not context:
                        g.spare()
            t_s = []
            for j in range(8):
                t_s.append(act(s.activation(hs[:, j, :], hh[:, j, :], ACT.Sqrt, scale=-1.0)))
            for j in range(8):
                d, k = j // KR, j % KR
                h_, i_, s_, q = hh[:, j, :], ig[:, j, :], hs[:, j, :], xa[:, 0, :]
                wait("dve", t_s[0 if j == 0 else j])
                dve(v.tensor_scalar(q, h_, -1.0, 1.0, ALU.mult, ALU.add))
                dve(v.reciprocal(q, q))
                dve(v.scalar_tensor_tensor(out=h_, in0=h_, scalar=1.0, in1=q, op0=ALU.add, op1=ALU.mult))
                dve(v.scalar_tensor_tensor(out=q, in0=q, scalar=2.0, in1=s_, op0=ALU.mult, op1=ALU.mult))
                dve(v.tensor_tensor(i_, i_, raw(k), ALU.mult))
                dve(v.tensor_tensor(i_, i_, q, ALU.mult))
                init = 0.0 if context else LW[:, d, k:k + 1]
                if d == 0:
                    dve(v.tensor_tensor_scan(s_, h_, i_, init, ALU.mult, ALU.add))
                else:
                    dve(v.tensor_tensor_scan(s_[:, ::-1], h_[:, ::-1], i_[:, ::-1], init, ALU.mult, ALU.add))
                if context:
                    e = n - 1 if d == 0 else 0
                    dve(v.tensor_copy(LW[:, d, k:k + 1], s_[:, e:e + 1]))
                g.spare()
                if not context:
                    g.spare()

        def sine(ps, layer, dst):
            f = vec(f"filt_freq{layer}", parts=FHID)
            dve(v.tensor_scalar(dst, ps, vec(f"filt_b{layer + 1}", parts=FHID), f, ALU.add, ALU.mult))
            q = R[0:FHID, :]
            dve(v.tensor_scalar(q, dst, 1.0 / (2 * math.pi), 12582912.0, ALU.mult, ALU.add))
            dve(v.tensor_scalar(q, q, -12582912.0, None, ALU.add))
            c1 = 6.28125
            dve(v.scalar_tensor_tensor(out=dst, in0=q, scalar=-c1, in1=dst, op0=ALU.mult, op1=ALU.add))
            dve(v.scalar_tensor_tensor(out=dst, in0=q, scalar=-(2 * math.pi - c1), in1=dst, op0=ALU.mult, op1=ALU.add))
            dve(v.tensor_scalar(dst, dst, 3.1415925, -3.1415925, ALU.min, ALU.max))
            wait("act", g.latest["dve"])
            act(s.activation(dst, dst, ACT.Sin))
            wait("pe", g.latest["act"])

        def spectrum_steps(st, fw, kf):
            sd = g.sb(st, "filt_sd", [P, 2, NT, RW])
            hid = g.sb(st, "hidden", [FHID + 1, 2, T])
            w3 = g.sb(st, "filt_w3", [FHID + 1, 4, RW])
            w12 = g.sb(st, "filt_w12", [FHID, 2, FHID])
            zf = g.sb(st, "filt_z", [FEMB, T])
            win = g.sb(st, "window", [P, NT, RW])
            t1 = [g.load(w12[0:FEMB, 0, :], a["filt_w1"], "fw1", "act"),
                  g.load(w12[:, 1, :], a["filt_w2"], "fw2", "act"),
                  g.load(zf[:, :], a["filt_z"], "fz", "act")]
            tt = [g.load(w3[0:FHID, :, :], a["filt_w3"].rearrange("p (q c) -> p q c", q=4), "fw3", "act"),
                  g.load(w3[FHID:FHID + 1, :, :], a["filt_b3"].rearrange("p (q c) -> p q c", q=4), "fb3", "act"),
                  g.load(win[:, :, :], a["window"].rearrange("p (k t) -> p k t", k=NT), "win", "act")]
            t_fw = g.load(fw[:, :, :], a["dft"].rearrange("p (k t) -> p k t", k=NT), "dft", "act")
            wait("pe", *t1)
            dve(v.memset(hid[FHID:FHID + 1, :, :], 1.0))
            t = pe(mm(bank[0][0:FHID, :], w12[0:FEMB, 0, :], zf[:, :]))
            yield
            wait("dve", t)
            sine(bank[0][0:FHID, :], 0, hid[0:FHID, 0, :])
            t = pe(mm(bank[1][0:FHID, :], w12[:, 1, :], hid[0:FHID, 0, :]))
            yield
            wait("dve", t)
            sine(bank[1][0:FHID, :], 1, hid[0:FHID, 1, :])
            wait("pe", t_fw, *tt)
            wait("dve", *tt)
            t_kf = None
            for o in range(2):
                t_f = {}
                for n in range(NT):
                    fb = [bank[2 * (n % 2)], bank[2 * (n % 2) + 1]]
                    wait("pe", t_f.get(n - 2), g.latest["dve"] if n == 0 else None)
                    for q in range(2):
                        ins = mm(fb[q][:, :], hid[:, 1, n * P:(n + 1) * P], w3[:, 2 * o + q, :])
                    wait("dve", pe(ins), t_kf)
                    f0, f1 = SQ[:, 0, :], SQ[:, 1, :]
                    dve(v.tensor_tensor(f0, fb[0][:, :], win[:, n, :], ALU.mult))
                    t_f[n] = dve(v.tensor_tensor(f1, fb[1][:, :], win[:, n, :], ALU.mult))
                    if n == 0:
                        dve(v.memset(SQ[0:1, 1, :], 0.0))
                    dve(v.tensor_tensor(sd[:, 0, n, :], f0, f1, ALU.add))
                    t_sd = dve(v.tensor_tensor(sd[:, 1, n, :], f0, f1, ALU.subtract))
                    yield
                done = []
                wait("pe", t_sd)
                for m in range(9):
                    b = bank[m % 4]
                    wait("pe", t_f[3 if m < 2 else 2] if m < 4 else done[m - 4])
                    col = m * P if m < 8 else T
                    for k in range(NT):
                        ins = mm(b[:, :], fw[:, k, col:col + P], sd[:, 1 if 4 <= m < 8 else 0, k, :], k == 0, k == NT - 1)
                    t_kf = pe(ins)
                    wait("act", t_kf)
                    done.append(act(s.copy(kf[:, o, m, :], b[:, :])))
                    yield
                wait("dve", done[-1])
                dve(v.tensor_copy(SQ[0:1, 0, :], kf[0:1, o, 8, :]))
                dve(v.tensor_copy(kf[:, o, 8, :], kf[:, o, 0, :]))
                dve(v.tensor_copy(kf[0:1, o, 8, :], SQ[0:1, 0, :]))
                dve(v.memset(kf[0:1, o, 4, :], 0.0))
            yield

        def layer0_mixer():
            with ExitStack() as st:
                kf = g.sb(st, "spectrum", [P, 2, 9, RW])
                fw = g.sb(st, "dft", [P, NT, 2 * T])
                gw = g.sb(st, "lru_w", [P, 16, P])
                with ExitStack() as early:
                    wm = g.sb(early, "wmod", [P, 4, 2048])
                    cs = g.sb(early, "cond", [P, KD, 32])
                    dve(v.memset(cs[:, :, :], 0.0))
                    wait("act", g.latest["dve"])
                    act(s.activation(cs[:, :, 0], vec("c", 0, 8), ACT.Silu))
                    act(s.activation(cs[:, :, 1], vec("c_ctx", 0, 8), ACT.Silu))
                    dve(v.memset(gw[:, :, :], 0.0))
                    g.fence()
                    with ExitStack() as gen:
                        spec = spectrum_steps(gen, fw, kf)
                        for _ in adaln_steps(0, wm, cs):
                            next(spec, None)
                        for _ in spec:
                            pass
                        g.fence()
                    t1 = g.load(gw[0:64, :, 0:64], a["lru_w"][0], "lru_w0")
                    t2 = g.load(gw[64:128, :, 64:128], a["lru_w"][1], "lru_w1")
                    wait("pe", t1, t2)
                    gain_of(0, "norm1_g", 0, 0, 8)
                    gain_of(1, "norm1_g", 0, 0, 8, 1)
                    dve(v.tensor_scalar(SPL[:, 0, :], vec("lru_lam", 0, 8), -1.0, None, ALU.mult))
                    softplus(SPL[:, 0, :], SPL[:, 1, :], SPL[:, 2, :], SM[:, 0:8])
                    t = dve(v.tensor_scalar(SPL[:, 1, :], SPL[:, 0, :], -0.5 * LRU_C, None, ALU.mult))
                    wait("act", t)
                    layer1_rows = adaln_steps(1, wm, cs)
                    with ExitStack() as cx:
                        xc = g.sb(cx, "ctx", [P, KD, TC])
                        ra = g.sb(cx, "ctx_raw", [P, KR, TC])
                        hc = g.sb(cx, "ctx_lru", [P, 3, 8, TC])
                        t = g.load(xc[:, :, :], a["ctx_fm"].rearrange("p (k t) -> p k t", k=KD), "ctx", "act")
                        t_x = g.load(X[:, :, :], a["x_fm"].rearrange("p (k t) -> p k t", k=KD), "x", "act")
                        wait("act", t)
                        wait("dve", t)
                        next(layer1_rows)
                        rms_rows(lambda k: xc[:, k, :], KD, TC, EPS, R, D)
                        modulate(lambda k: xc[:, k, :], TC, 1, lambda k: MOD[:, 0, k, 1:2], lambda k: xc[:, k, :])
                        g.fence()

                        def ev(i, ps, e):
                            return dve(v.tensor_copy(ra[:, bass.ds(i, 1), :].rearrange("p o t -> p (o t)"), ps))

                        src = wblock("w_in")
                        project(KR, lambda i: src(i + KR), lambda k: xc[:, k, :], TC, ev)
                        g.top_stack = cx
                        g.background = layer1_rows
                        rglru(lambda k: ra[:, k, :], TC, gw, hc[:, 0, :, :], hc[:, 1, :, :], hc[:, 2, :, :], True)
                        wait("act", t_x)
                        wait("dve", t_x)
                        rms_rows(lambda k: X[:, k, :], KD, T, EPS, R, D)
                        for _ in g.background:
                            pass
                        g.background = None
                        g.fence()
                modulate(lambda k: X[:, k, :], T, 0, lambda k: MOD[:, 0, k, 0:1], lambda k: H[:, k, :])
                pr = g.sb(st, "proj", [P, 20, T])
                g.fence()

                def ev(i, ps, e):
                    return dve(v.tensor_copy(pr[:, bass.ds(i, 1), :].rearrange("p o t -> p (o t)"), ps))

                src = wblock("w_in")
                project(KR, lambda i: src(i + KR), lambda k: H[:, k, :], T, lambda i, ps, e: ev(i + KR, ps, e))
                with ExitStack() as lru:
                    hl = g.sb(lru, "lru_g", [P, 8, T])
                    ht = g.sb(lru, "lru_h", [P, 8, T])
                    g.top_stack = lru
                    g.fence()

                    def rest_of_projection():
                        def empty(i, b, t):
                            if i < KR:
                                wait("act", t)
                                return act(s.activation(pr[:, i, :], b[:, :], ACT.Gelu_apprx_tanh))
                            wait("dve", t)
                            k = i - 2 * KR
                            return dwconv(pr[:, i, :], b[:, :], T, "conv_b_w", k, 12, 3, 1, "conv_b_b", k)

                        pending = None
                        order = [*range(KR), *range(2 * KR, 20)]
                        w, free = [None] * 2, [None] * 2
                        for u in range(2):
                            w[u] = g.load(W[:, u, :, :], src(order[u]), f"w{u}")
                        for j, i in enumerate(order):
                            b = bank[6 + j % 2]
                            wait("pe", w[j % 2], free[j % 2])
                            for k in range(KD):
                                ins = mm(b[:, :], W[:, j % 2, k, :], H[:, k, :], k == 0, k == KD - 1)
                                if k == 3:
                                    if pending:
                                        free[1 - j % 2] = empty(*pending)
                                    yield
                            t = pe(ins)
                            pending = (i, b, t)
                            if j + 2 < len(order):
                                wait("sp", t)
                                w[j % 2] = g.load(W[:, j % 2, :, :], src(order[j + 2]), f"w{j % 2}")
                            yield
                        empty(*pending)

                    g.background = rest_of_projection()
                    rglru(lambda k: pr[:, KR + k, :], T, gw, hl, pr[:, 12:20, :], ht, False)
                    for _ in g.background:
                        pass
                    g.background = None
                    wait("dve", g.latest["act"])
                    for k in range(KR):
                        dve(v.tensor_tensor(ht[:, k, :], ht[:, k, :], ht[:, KR + k, :], ALU.add))
                        dve(v.tensor_tensor(H[:, k, :], ht[:, k, :], pr[:, k, :], ALU.mult))
                    g.fence()
                hyena(lambda k: pr[:, 8 + k, :], lambda o, k: pr[:, 12 + 4 * o + k, :],
                      H[:, KR:2 * KR, :], lambda k: H[:, KR + k, :], fw, kf)

            def ev(i, ps, e):
                xi = X[:, bass.ds(i, 1), :].rearrange("p o t -> p (o t)")
                return dve(v.scalar_tensor_tensor(out=xi, in0=ps, scalar=MOD[:, 0, bass.ds(i + 16, 1), 0:1].rearrange("p a b -> p (a b)"),
                                                  in1=xi, op0=ALU.mult, op1=ALU.add))

            project(KD, wblock("w_out"), lambda k: H[:, k, :], T, ev)

        def hyena(zin, gate, ztm, zout, fw, kf):
            with ExitStack() as st:
                sd = g.sb(st, "z_spectrum", [P, 2, NT, RW])
                inv = g.sb(st, "idft", [P, 8, T])
                g.fence()
                t_inv = g.load(inv[:, :, :], a["idft"].rearrange("p (k t) -> p k t", k=8), "idft")
                for o in range(2):
                    wait("pe", g.latest["dve"])
                    t_z = []
                    for n in range(NT):
                        for k in range(KR):
                            ins = tn.transpose(bank[n][:, k * P:(k + 1) * P], zin(k)[:, n * P:(n + 1) * P], ident)
                        t = pe(ins)
                        wait("act", t)
                        t_z.append(act(s.copy(ztm[:, n, :], bank[n][:, :])))
                    wait("pe", *t_z)
                    t_free = {}
                    for m in range(NT):
                        br, bi = bank[(2 * m + 4) % 8], bank[(2 * m + 5) % 8]
                        for k in range(NT):
                            mm(br[:, :], fw[:, k, m * P:(m + 1) * P], ztm[:, k, :], k == 0, k == NT - 1)
                        for k in range(NT):
                            ins = mm(bi[:, :], fw[:, k, T + m * P:T + (m + 1) * P], ztm[:, k, :], k == 0, k == NT - 1)
                        t = pe(ins)
                        wait("dve", t)
                        kr, ki = kf[:, o, m, :], kf[:, o, 4 + m, :]
                        kr2 = kf[:, o, 8, :] if m == 0 else kr
                        q0, q1 = SQ[:, 0, :], SQ[:, 1, :]
                        dve(v.tensor_tensor(q0, br[:, :], kr, ALU.mult))
                        dve(v.tensor_tensor(q1, bi[:, :], ki, ALU.mult))
                        dve(v.tensor_tensor(sd[:, 0, m, :], q0, q1, ALU.subtract))
                        dve(v.tensor_tensor(q0, br[:, :], ki, ALU.mult))
                        dve(v.tensor_tensor(q1, bi[:, :], kr2, ALU.mult))
                        dve(v.tensor_tensor(sd[:, 1, m, :], q0, q1, ALU.add))
                    wait("pe", g.latest["dve"], t_inv)
                    for k in range(KR):
                        for m in range(8):
                            ins = mm(bank[k][:, :], sd[:, m // 4, m % 4, k * P:(k + 1) * P], inv[:, m, :], m == 0, m == 7)
                        t = pe(ins)
                        wait("dve", t)
                        dst = zin(k) if o == 0 else zout(k)
                        dve(v.scalar_tensor_tensor(out=zin(k), in0=zin(k), scalar=vec("filt_bias", 4 * o + k),
                                                   in1=bank[k][:, :], op0=ALU.mult, op1=ALU.add))
                        dve(v.tensor_tensor(dst, zin(k), gate(o, k), ALU.mult))
                g.fence()

        def moe(layer):
            sh, sc, gt = (24, 32, 40)
            L = f"_{layer}"
            with ExitStack() as st:
                ring = g.sb(st, "experts" + L, [P, NRING, 2, FF])
                HT = g.sb(st, "h_tm" + L, [P, NT, D])
                rt = g.sb(st, "router" + L, [P, KD, NE])
                pb = g.sb(st, "probs" + L, [P, NT, NE + 2])
                sl = g.sb(st, "slots" + L, [P, NT, NE + 2])
                pe_t = g.sb(st, "probs_e" + L, [NE, T])
                wk = g.sb(st, "topk" + L, [NE, 2, T])
                mx = g.sb(st, "max8" + L, [NE, 8])
                PM = g.sb(st, "pick" + L, [P, NT, 2, CAP])
                PG = g.sb(st, "give" + L, [P, NT, 2, CAP])
                PT = g.sb(st, "give_t" + L, [P, T])
                xr = W[:, 0, :, :].rearrange("p k c -> p (k c)")
                xs = W[:, 1, :, :]
                hs = SQ
                hT = g.sb(st, "hs_t" + L, [P, 2, 4, P])
                yy = g.sb(st, "y" + L, [P, D])
                g.fence()
                t = g.load(rt[:, :, :], a["router"][layer].rearrange("p (k e) -> p k e", k=KD), "router")
                wait("pe", t)
                gain_of(2, "norm2_g", 8 * layer, layer, sc)
                rms_rows(lambda k: X[:, k, :], KD, T, EPS, R, D)
                modulate(lambda k: X[:, k, :], T, 2, lambda k: MOD[:, layer, sh + k, 0:1], lambda k: H[:, k, :])
                wait("pe", g.latest["dve"], g.latest["act"])
                for k in range(KD):
                    ins = mm(bank[0][0:NE, :], rt[:, k, :], H[:, k, :], k == 0, k == KD - 1)
                t = pe(ins)
                wait("dve", t)
                t_l = dve(v.tensor_copy(pe_t[:, :], bank[0][0:NE, :]))
                wait("pe", t_l)
                for n in range(NT):
                    ins = tn.transpose(bank[1][:, n * NE:(n + 1) * NE], pe_t[:, n * P:(n + 1) * P], ident[0:NE, 0:NE])
                t_lt = pe(ins)
                for n in range(NT):
                    for h in range(2):
                        b = bank[4 + (2 * n + h) % 4]
                        if n >= 2:
                            wait("pe", t_h[2 * n + h - 4])
                        elif n + h == 0:
                            t_h = []
                        for k in range(4):
                            ins = tn.transpose(b[:, k * P:(k + 1) * P], H[:, 4 * h + k, n * P:(n + 1) * P], ident)
                        t = pe(ins)
                        wait("act", t)
                        t_h.append(act(s.copy(HT[:, n, 512 * h:512 * h + 512], b[:, :])))
                wait("dve", t_lt)
                lg = bank[1][:, 0:NT * NE].rearrange("p (n e) -> p n e", n=NT)
                pr = pb[:, :, 0:NE]
                dve(v.tensor_reduce(SM[:, 0:NT], lg, AXX, ALU.max))
                dve(v.tensor_tensor(pr, lg, SM[:, 0:NT].unsqueeze(2).broadcast_to([P, NT, NE]), ALU.subtract))
                wait("act", g.latest["dve"])
                act(s.activation(pr, pr, ACT.Exp))
                wait("dve", g.latest["act"])
                dve(v.tensor_reduce(SM[:, 8:8 + NT], pr, AXX, ALU.add))
                dve(v.reciprocal(SM[:, 8:8 + NT], SM[:, 8:8 + NT]))
                dve(v.tensor_tensor(pr, pr, SM[:, 8:8 + NT].unsqueeze(2).broadcast_to([P, NT, NE]), ALU.mult))
                wait("pe", g.latest["dve"])
                for n in range(NT):
                    ins = tn.transpose(bank[2][0:NE, n * P:(n + 1) * P], pb[:, n, 0:NE], ident)
                t = pe(ins)
                wait("dve", t)
                dve(v.tensor_copy(wk[:, 0, :], bank[2][0:NE, :]))
                for r in range(CAP // 8):
                    dve(v.max(mx[:, :], wk[:, r % 2, :]))
                    dve(v.match_replace(wk[:, (r + 1) % 2, :], mx[:, :], wk[:, r % 2, :], -1.0))
                dve(v.tensor_scalar(wk[:, 1, :], wk[:, 0, :], -1.0, None, ALU.is_equal))
                dve(v.memset(pe_t[:, :], 1.0))
                dve(v.tensor_tensor_scan(wk[:, 0, :], pe_t[:, :], wk[:, 1, :], 0.0, ALU.mult, ALU.add))
                dve(v.tensor_tensor(wk[:, 0, :], wk[:, 0, :], wk[:, 1, :], ALU.mult))
                dve(v.tensor_scalar(wk[:, 0, :], wk[:, 0, :], -1.0, None, ALU.add))
                wait("pe", g.latest["dve"])
                for n in range(NT):
                    ins = tn.transpose(bank[3][:, n * NE:(n + 1) * NE], wk[:, 0, n * P:(n + 1) * P], ident[0:NE, 0:NE])
                t = pe(ins)
                dve(v.memset(sl[:, :, :], -1.0))
                dve(v.memset(pb[:, :, NE:NE + 2], 0.0))
                dve(v.memset(yy[:, :], 0.0))
                dve(v.memset(PT[:, :], 0.0))
                wait("dve", t)
                dve(v.tensor_copy(sl[:, :, 0:NE], bank[3][:, 0:NT * NE].rearrange("p (n e) -> p n e", n=NT)))
                w = {q: a[f"exp_w{q}"][layer].rearrange("e (j k p) f -> e j p k f", j=4, p=P) for q in (1, 3, 2)}
                iota = con("iota", 0, CAP).unsqueeze(1).unsqueeze(1).broadcast_to([P, NT, 2, CAP])
                order = [(q, e, j) for e in range(2) for j in range(4) for q in (1, 3)]
                order += [(2, e, j) for j in range(4) for e in range(2)]
                place = {x: n % NRING for n, x in enumerate(order)}

                def pick(pair):
                    so = sl[:, :, bass.ds(pair * 2, 2)].unsqueeze(3).broadcast_to([P, NT, 2, CAP])
                    return dve(v.tensor_tensor(PM[:, :, :, :], iota, so, ALU.is_equal))

                def give(pair):
                    po = pb[:, :, bass.ds(pair * 2, 2)].unsqueeze(3).broadcast_to([P, NT, 2, CAP])
                    return dve(v.tensor_tensor(PG[:, :, :, :], PM[:, :, :, :], po, ALU.mult))

                def gather():
                    for h in range(2):
                        for n in range(NT):
                            ins = mm(bank[6 + h][:, :], PM[:, n, :, :], HT[:, n, 512 * h:512 * h + 512], n == 0, n == NT - 1)
                        t = pe(ins)
                        wait("act", t)
                        t_x = act(s.copy(xr[:, 512 * h:512 * h + 512], bank[6 + h][:, :]))
                    return t, t_x

                def turn(t_x):
                    wait("pe", t_x)
                    for h in range(2):
                        for k in range(4):
                            ins = tn.transpose(bank[6 + h][:, k * P:(k + 1) * P], xr[:, (4 * h + k) * P:(4 * h + k + 1) * P], ident)
                        t = pe(ins)
                        wait("act", t)
                        t_xs = act(s.copy(xs[:, 4 * h:4 * h + 4, :], bank[6 + h][:, :].rearrange("p (k c) -> p k c", k=4)))
                    return t, t_xs

                def scatter(last_adds):
                    adds = []
                    for k in range(KD):
                        b = bank[4 + k % 2]
                        wait("pe", last_adds[k] if k < 2 else adds[k - 2])
                        t = pe(mm(b[:, :], yy[:, k * P:(k + 1) * P], PT[:, :]))
                        wait("dve", t)
                        adds.append(dve(v.scalar_tensor_tensor(out=X[:, k, :], in0=b[:, :], scalar=MOD[:, layer, gt + k, 0:1],
                                                               in1=X[:, k, :], op0=ALU.mult, op1=ALU.add)))
                    return t, adds

                t = pick(0)
                wait("pe", t, g.latest["act"])
                t, t_x = gather()
                wait("dve", t)
                give(0)
                turn(t_x)
                g.fence(skip="sp")
                with book.run(NE // 2) as i:
                    cpe, cdve, cact = g.cnt["pe"], g.cnt["dve"], g.cnt["act"]
                    tw = {}
                    for n, (q, e, j) in enumerate(order):
                        if n < NRING:
                            wait("sp", book.before(f"use{n}", ring_used))
                        else:
                            wait("sp", book.later(f"use{n - NRING}x", ring_used))
                        tw[q, e, j] = g.load(ring[:, place[q, e, j], :, :],
                                             w[q][bass.ds(i * 2 + e, 1), j].rearrange("o p k f -> p (o k) f"),
                                             f"ring{place[q, e, j]}")

                    def used(x, t):
                        n = order.index(x)
                        if n < len(order) - NRING:
                            book.name(f"use{n}x", t)
                        if n >= len(order) - NRING:
                            book.name(f"use{n - (len(order) - NRING)}", t)

                    def up(e):
                        for j in range(4):
                            for q, m in ((0, 1), (1, 3)):
                                wait("pe", tw[m, e, j])
                                for k in range(2):
                                    for f in range(2):
                                        ins = mm(bank[2 * e + q][64 * f:64 * f + 64, :], xs[:, 2 * j + k, 64 * e:64 * e + 64],
                                                 ring[:, place[m, e, j], k, 512 * f:512 * f + 512], j + k == 0, j == 3 and k == 1)
                                t = ring_used.mark(ins)
                                used((m, e, j), t)
                        wait("act", t)
                        t_s = act(s.activation(hs[:, e, :], bank[2 * e][:, :], ACT.Silu))
                        wait("dve", t_s)
                        return dve(v.tensor_tensor(hs[:, e, :], hs[:, e, :], bank[2 * e + 1][:, :], ALU.mult))

                    def turn_hidden(e, t_hs):
                        wait("pe", t_hs)
                        for k in range(4):
                            ins = tn.transpose(bank[4 + e][:, k * P:(k + 1) * P], hs[:, e, k * P:(k + 1) * P], ident)
                        t = pe(ins)
                        wait("act", t)
                        return act(s.copy(hT[:, e, :, :], bank[4 + e][:, :].rearrange("p (k c) -> p k c", k=4)))

                    wait("dve", book.before("gather", cpe))
                    t_pm = pick(i + 1)
                    wait("pe", book.before("xs", cact), book.before("yy", cact))
                    t_h0 = up(0)
                    t_sc, adds = scatter([book.before("hT0", cact), book.before("hT1", cact)])
                    for n in range(NT):
                        ins = tn.transpose(bank[7][:, n * P:(n + 1) * P], PG[:, n, :, :].rearrange("p e c -> p (e c)"), ident)
                    t = pe(ins)
                    wait("act", t)
                    t_pt = act(s.copy(PT[:, :], bank[7][:, :]))
                    wait("dve", t)
                    give(i + 1)
                    t_h1 = up(1)
                    wait("pe", adds[6])
                    t_ht0 = book.name("hT0", turn_hidden(0, t_h0))
                    wait("pe", t_pm, t_pt)
                    t, t_x = gather()
                    book.name("gather", t)
                    wait("pe", adds[7])
                    t_ht1 = book.name("hT1", turn_hidden(1, t_h1))
                    _, t_xs = turn(t_x)
                    book.name("xs", t_xs)
                    wait("pe", t_ht0, t_ht1)
                    for j in range(4):
                        for e in range(2):
                            wait("pe", tw[2, e, j])
                        for k in range(2):
                            kk = 2 * j + k
                            for f in range(2):
                                for e in range(2):
                                    ins = mm(bank[f][64 * e:64 * e + 64, :], hT[:, e, kk % 4, 64 * (kk // 4):64 * (kk // 4) + 64],
                                             ring[:, place[2, e, j], k, 512 * f:512 * f + 512], kk == 0, kk == 7)
                        t = ring_used.mark(ins)
                        used((2, 0, j), t)
                        used((2, 1, j), t)
                    wait("act", t)
                    for f in range(2):
                        t_y = act(s.copy(yy[:, 512 * f:512 * f + 512], bank[f][:, :]))
                    book.name("yy", t_y)
                g.settle()
                g.fence()
                scatter([None, None])
                g.fence()

        def layer1_mixer():
            gain_of(0, "norm1_g", 8, 1, 8)
            rms_rows(lambda k: X[:, k, :], KD, T, EPS, R, D)
            modulate(lambda k: X[:, k, :], T, 0, lambda k: MOD[:, 1, k, 0:1], lambda k: H[:, k, :])
            with ExitStack() as st:
                Y = g.sb(st, "cf_y", [P, KD, T])
                gs = g.sb(st, "cf_sig", [P, T])
                w = g.sb(st, "cf_taps", [P, 2 * KD])
                u = g.sb(st, "cf_in", [P, T])
                y = g.sb(st, "cf_out", [P, T])
                g.fence()
                rows = T // GRID_W
                assert rows == KD
                half = (CF_K - 1) // 2

                def row(tile, i):
                    return tile[:, bass.ds(i, 1), :].rearrange("p o t -> p (o t)")

                def ev_u(i, j, ps):
                    if j == 0:
                        return dve(v.tensor_scalar(u[:, :], ps, g.V[:, bass.ds(i + VOFF["cf_b1"], 1)], None, ALU.add))
                    t = dve(v.tensor_scalar(gs[:, :], ps, g.V[:, bass.ds(i + VOFF["cf_b1"] + 8, 1)], None, ALU.add))
                    wait("act", t)
                    t_g = act(s.activation(gs[:, :], gs[:, :], ACT.Sigmoid))
                    taps = g.V[:, VOFF["cf_dw_w"]:VOFF["cf_dw_w"] + CF_K * 8].rearrange("p (j k) -> p j k", k=8)
                    dve(v.tensor_copy(w[:, 0:2 * rows - 1],
                                      taps[:, half - rows + 1:half + rows, bass.ds(i, 1)].rearrange("p j o -> p (j o)")))
                    dve(v.tensor_copy(w[:, 2 * rows - 1:2 * rows], g.V[:, bass.ds(i + VOFF["cf_dw_b"], 1)]))
                    wait("dve", t_g)
                    dve(v.tensor_tensor(u[:, :], u[:, :], gs[:, :], ALU.mult))
                    mid = rows - 1
                    dve(v.tensor_scalar(y[:, :], u[:, :], w[:, mid:mid + 1], w[:, 2 * rows - 1:2 * rows], ALU.mult, ALU.add))
                    for d in range(-(rows - 1), rows):
                        if d:
                            lo, hi = max(0, -d * GRID_W), min(T, T - d * GRID_W)
                            dve(v.scalar_tensor_tensor(out=y[:, lo:hi], in0=u[:, lo + d * GRID_W:hi + d * GRID_W],
                                                       scalar=w[:, mid + d:mid + d + 1], in1=y[:, lo:hi],
                                                       op0=ALU.mult, op1=ALU.add))
                    dve(v.tensor_copy(row(Y, i), y[:, :]))
                    return t

                src = wblock("cf_w1")
                project_pairs(KD, lambda i, j: src(i + KD * j), lambda k: H[:, k, :], T, ev_u)
                wait("pe", g.latest["dve"])
                for k in range(KD):
                    ins = mm(bank[0][:, :], con("ones"), Y[:, k, :], k == 0, k == KD - 1)
                t = pe(ins)
                wait("dve", t)
                dve(v.tensor_scalar(gs[:, :], bank[0][:, :], -1.0 / D, None, ALU.mult))
                for k in range(KD):
                    t = dve(v.tensor_tensor(Y[:, k, :], Y[:, k, :], gs[:, :], ALU.add))
                rms_rows(lambda k: Y[:, k, :], KD, T, EPS, R, D)
                for k in range(KD):
                    t = dve(v.tensor_tensor(Y[:, k, :], Y[:, k, :], R[:, :], ALU.mult))
                    wait("act", t)
                    act(s.activation(H[:, k, :], Y[:, k, :], ACT.Silu, bias=vec("cf_ln_b", k), scale=vec("cf_ln_g", k)))
                dve(v.tensor_tensor(SM[:, 0:8], MOD[:, 1, 16:24, 0], vec("cf_b2", 0, 8), ALU.mult))
                for k in range(KD):
                    dve(v.tensor_scalar(X[:, k, :], X[:, k, :], SM[:, k:k + 1], None, ALU.add))
                g.fence()

                def ev(i, ps, e):
                    return dve(v.scalar_tensor_tensor(out=row(X, i), in0=ps,
                                                      scalar=MOD[:, 1, bass.ds(i + 16, 1), 0:1].rearrange("p a b -> p (a b)"),
                                                      in1=row(X, i), op0=ALU.mult, op1=ALU.add))

                project(KD, wblock("cf_w2"), lambda k: H[:, k, :], T, ev)

        def plain_norm(name, dst, done=None):
            rms_rows(lambda k: X[:, k, :], KD, T, EPS, R, D)
            for k in range(KD):
                t = dve(v.scalar_tensor_tensor(out=dst[:, k, :], in0=X[:, k, :], scalar=vec(name, k), in1=R[:, :],
                                               op0=ALU.mult, op1=ALU.mult))
                if done:
                    done(k, t)

        layer0_mixer()
        moe(0)
        layer1_mixer()
        moe(1)
        plain_norm("final_g", X)
        second_block(g, a, X, H, R, SQ, W, SM, bank, project, wblock, softplus, rsqrt, plain_norm, dwconv)
        out = a["out"].rearrange("p (k t) -> p k t", k=KD)
        stored = []

        def store(k, t):
            wait("sp", t)
            stored.append(g.load(out[:, k, :], X[:, k, :], "out"))

        plain_norm("final_gain_2", X, store)
        wait("sp", stored[-1])
    return book.fresh


QKV, GZ, SU, SV, SZ, RK, RZ, NQ, NKV, NZ, NPROJ = 0, 6, 8, 10, 12, 14, 21, 23, 25, 28, 30


def second_block(g, a, X, H, R, SQ, W, SM, bank, project, wblock, softplus, rsqrt, plain_norm, dwconv):
    nc, book, wait, dve, act, pe, mm = g.nc, g.book, g.wait, g.dve, g.act, g.pe, g.mm
    v, s, tn = nc.vector, nc.scalar, nc.tensor
    vec, con = g.vec, g.con
    ident = con("ident")
    halves = [slice(0, 64), slice(64, 128)]
    outer = ExitStack()
    with outer:
        PJ = g.sb(outer, "proj2", [P, NPROJ, T])
        SL = g.sb(outer, "proj2_small", [96, T])
        YS = g.sb(outer, "mixer_out", [P, 8, T])
        g.fence()
        plain_norm("norm_gain_2", H)
        t = g.load(W[:, 0, :, 0:96], a["w_small"].rearrange("p (k c) -> p k c", c=96), "w0")
        wait("pe", t, g.latest["dve"])
        for k in range(KD):
            ins = mm(bank[0][0:96, :], W[:, 0, k, 0:96], H[:, k, :], k == 0, k == KD - 1)
        t = pe(ins)
        wait("dve", t)
        dve(v.tensor_copy(SL[:, :], bank[0][0:96, :]))
        g.fence()

        def ev(i, ps, e):
            return dve(v.tensor_copy(PJ[:, bass.ds(i, 1), :].rearrange("p o t -> p (o t)"), ps))

        project(NPROJ, wblock("w_in_2"), lambda k: H[:, k, :], T, ev)

        def weave(*gens):
            gens = list(gens)
            while gens:
                for x in list(gens):
                    if next(x, gens) is gens:
                        gens.remove(x)
                    g.spare()

        def head_sums(src, b):
            wait("pe", g.latest["dve"], g.latest["act"])
            t = pe(mm(bank[b][:, :], con("blk1"), src))
            yield
            wait("dve", t)
            return bank[b][:, :]

        def root(psum, scale, eps, out):
            t = dve(v.tensor_scalar(out, psum, scale, eps, ALU.mult, ALU.add))
            wait("act", t)
            t = act(s.activation(out, out, ACT.Sqrt))
            yield
            wait("dve", t)
            dve(v.reciprocal(out, out))

        def tile_products(b, left, right):
            wait("pe", g.latest["dve"], g.latest["act"])
            for n in range(NCH):
                for r in halves:
                    ins = mm(bank[b][r, n * CH:(n + 1) * CH], left[r, n * CH:(n + 1) * CH], right[r, n * CH:(n + 1) * CH])
            t = pe(ins)
            yield
            wait("dve", t)
            return bank[b][:, :]

        def to_rows(b, src, dst):
            wait("pe", g.latest["dve"], g.latest["act"])
            for n in range(NCH):
                for r in halves:
                    ins = mm(bank[b][r, n * CH:(n + 1) * CH], src[r, n * CH:(n + 1) * CH], con("i64")[r, :])
            t = pe(ins)
            yield
            wait("act", t)
            act(s.copy(dst, bank[b][:, :]))
            wait("dve", t)

        def masked(dst, ps, mask):
            dve(v.tensor_tensor(fm3(dst, NCH), fm3(ps, NCH), mask.unsqueeze(1).broadcast_to([P, NCH, CH]), ALU.mult))

        def last_of_chunk(x):
            return fm3(x, NCH)[:, :, CH - 1:CH].broadcast_to([P, NCH, CH])

        def head_norm(x, eps, tmp, r, b):
            ps = yield from head_sums(x, b)
            dve(v.scalar_tensor_tensor(out=x, in0=ps, scalar=-1.0 / HD, in1=x, op0=ALU.mult, op1=ALU.add))
            dve(v.tensor_tensor(tmp, x, x, ALU.mult))
            ps = yield from head_sums(tmp, b)
            yield from root(ps, 1.0 / HD, eps, r)
            dve(v.tensor_tensor(x, x, r, ALU.mult))

        def deltas():
            with ExitStack() as st:
                AT, TIL, QT, AQ, KH = (g.sb(st, "delta_" + n, [P, 4, T]) for n in ("at", "til", "qt", "aq", "kh"))
                BV, AAK, ARK, VV, KV = (g.sb(st, "delta_" + n, [P, 2, T]) for n in ("bv", "aak", "ark", "v", "kv"))
                lam = g.sb(st, "delta_lam", [P, 4, NCH])
                up = g.sb(st, "rw_up", [P, 256])
                z3 = g.sb(st, "rw_scratch", [P, T])
                t_up = g.load(up[:, :], a["rw_up"], "rwup")
                g.fence()
                weave(gdn_prepare(AT, TIL, QT, AQ, KH, BV, lam),
                      rwkv_prepare(AT, TIL, QT, AQ, KH, AAK, ARK, VV, KV, lam, up, t_up, z3))
                g.rest()
                TM_, TT, MM_, LT = (PJ[:, n:n + 4, :] for n in (8, 12, 16, 0))
                G = PJ[:, RK + 6, 0:256].rearrange("p (a d) -> p a d", a=4)
                xr = PJ[:, RK + 6, 256:512].rearrange("p (a d) -> p a d", a=4)
                ur = g.rowtile[:, 0:256].rearrange("p (a d) -> p a d", a=4)
                g.fence()
                eye = con("i64").unsqueeze(1).broadcast_to([P, NCH, CH])

                def level_below(p, mask):
                    return dve(v.tensor_tensor(fm3(LT[:, p, :], NCH), fm3(AT[:, p, :], NCH),
                                               mask.unsqueeze(1).broadcast_to([P, NCH, CH]), ALU.mult))

                def products(b, left, right):
                    for n in range(NCH):
                        c = slice(n * CH, (n + 1) * CH)
                        for r in halves:
                            ins = mm(bank[b][r, c], left[r, c], right(r, c))
                    return pe(ins)

                for p in range(4):
                    level_below(p, con("level", 0, CH))
                    dve(v.tensor_tensor(fm3(TT[:, p, :], NCH), fm3(LT[:, p, :], NCH), eye, ALU.add))
                wait("pe", g.latest["dve"])
                t_l = [products(p, LT[:, p, :], lambda r, c: con("i64")[r, :]) for p in range(4)]
                for p in range(4):
                    wait("dve", t_l[p])
                    dve(v.tensor_tensor(fm3(TM_[:, p, :], NCH), fm3(bank[p][:, :], NCH), eye, ALU.add))
                    level_below(p, con("level", CH, CH))

                def first(p):
                    t = book.name(f"m{p}", products(p, LT[:, p, :], lambda r, c: TM_[r, p, c]))
                    wait("act", t)
                    return act(s.copy(MM_[:, p, :], bank[p][:, :]))

                g.fence()
                with book.run(LEVELS - 2) as lv:
                    def second(p, t_m):
                        wait("pe", t_m)
                        g.take(bank[4 + p])
                        t1 = products(4 + p, TT[:, p, :], lambda r, c: MM_[r, p, c])
                        t = book.name(f"t{p}", products(p, MM_[:, p, :], lambda r, c: TT[r, p, c]))
                        wait("dve", t1)
                        dve(v.tensor_tensor(TM_[:, p, :], TM_[:, p, :], bank[4 + p][:, :], ALU.add))
                        wait("dve", t)
                        dve(v.tensor_tensor(TT[:, p, :], TT[:, p, :], bank[p][:, :], ALU.add))
                        book.name(f"l{p}", level_below(p, g.C[:, bass.ds(lv * CH + (COFF["level"] + 2 * CH), CH)]))

                    t_m = []
                    for p in range(4):
                        wait("pe", book.before(f"l{p}", g.cnt["dve"]))
                        g.take(bank[p])
                        wait("act", book.before(f"t{p}", g.cnt["pe"]))
                        t_m.append(first(p))
                        if p:
                            second(p - 1, t_m[p - 1])
                    second(3, t_m[3])
                g.settle()
                g.fence()
                t_m = [first(p) for p in range(4)]
                for p in range(4):
                    wait("pe", t_m[p])
                    t = products(p, MM_[:, p, :], lambda r, c: TT[r, p, c])
                    wait("dve", t)
                    dve(v.tensor_tensor(TT[:, p, :], TT[:, p, :], bank[p][:, :], ALU.add))
                g.fence()
                dve(v.memset(G, 0.0))
                o_free = [None, None]
                for n in range(NCH):
                    c = slice(n * CH, (n + 1) * CH)
                    wait("pe", g.latest["dve"])
                    for p in range(4):
                        o = slice(p * HD, (p + 1) * HD)
                        for r in halves:
                            if p >= 2:
                                mm(bank[0][r, o], AAK[r, p - 2, c], VV[r, p - 2, c], True, False)
                            ins = mm(bank[0][r, o], TIL[r, p, c], G[r, p, :], p < 2, True)
                    t = pe(ins)
                    g.spare()
                    wait("dve", t)
                    x4 = bank[0][:, 0:4 * HD].rearrange("p (a d) -> p a d", a=4)
                    dve(v.tensor_tensor(xr[:, 0:2, :], x4[:, 0:2, :], BV[:, :, c], ALU.add))
                    t_x = dve(v.tensor_copy(xr[:, 2:4, :], x4[:, 2:4, :]))
                    ob, sb_ = bank[(2, 4)[n % 2]], bank[(5, 6)[n % 2]]
                    wait("pe", o_free[n % 2])
                    for p in range(4):
                        o = slice(p * CH, (p + 1) * CH)
                        for r in halves:
                            mm(ob[r, o], G[r, p, :], QT[r, p, c], p == 0, False)
                            if p >= 2:
                                mm(ob[r, o], VV[r, p - 2, c], ARK[r, p - 2, c], False, False)
                                mm(sb_[r, o], KV[r, p - 2, c], VV[r, p - 2, c], p == 2, False)
                    wait("pe", t_x)
                    for p in range(4):
                        for r in halves:
                            ins = mm(bank[1][r, p * HD:(p + 1) * HD], TT[r, p, c], xr[r, p, :])
                    t = pe(ins)
                    g.spare()
                    wait("dve", t)
                    dve(v.tensor_copy(ur, bank[1][:, 0:4 * HD].rearrange("p (a d) -> p a d", a=4)))
                    wait("pe", g.latest["dve"])
                    for p in range(4):
                        o = slice(p * CH, (p + 1) * CH)
                        for r in halves:
                            ins = mm(sb_[r, o], KH[r, p, c], ur[r, p, :], False, True)
                    t = pe(ins)
                    g.spare()
                    wait("dve", t)
                    for p in range(4):
                        dve(v.scalar_tensor_tensor(out=G[:, p, :], in0=G[:, p, :], scalar=lam[:, p, n:n + 1],
                                                   in1=sb_[:, p * HD:(p + 1) * HD], op0=ALU.mult, op1=ALU.add))
                    for p in range(4):
                        o = slice(p * CH, (p + 1) * CH)
                        for r in halves:
                            ins = mm(ob[r, o], ur[r, p, :], AQ[r, p, c], False, True)
                    t = pe(ins)
                    wait("act", t)
                    for p, y in enumerate((0, 1, 4, 5)):
                        o_free[n % 2] = act(s.copy(YS[:, y, c], ob[:, p * CH:(p + 1) * CH]))
                    g.spare()
                g.fence()

        def gdn_prepare(AT, TIL, QT, AQ, KH, BV, lam):
            B, BB, E, DD = (PJ[:, 8 + i, :] for i in range(4))
            bc = SM[:, 8:8 + NCH]
            taken = [None, None]
            for k in range(6):
                x = (B, BB)[k % 2]
                wait("dve", taken[k % 2])
                t = dwconv(x, PJ[:, k, :], T, "gdn_conv_2", k, 6, 4, 3)
                wait("act", t)
                taken[k % 2] = act(s.activation(PJ[:, k, :], x, ACT.Silu))
                yield
            wait("dve", g.latest["act"])
            for k in range(4):
                dve(v.tensor_tensor(B, PJ[:, k, :], PJ[:, k, :], ALU.mult))
                ps = yield from head_sums(B, 0)
                yield from root(ps, 1.0, 1e-6, E)
                if k < 2:
                    dve(v.scalar_tensor_tensor(out=PJ[:, k, :], in0=PJ[:, k, :], scalar=HD ** -0.5, in1=E, op0=ALU.mult, op1=ALU.mult))
                else:
                    dve(v.tensor_tensor(PJ[:, k, :], PJ[:, k, :], E, ALU.mult))
            x, t1, t2, t3 = SL[0:4, :], B[0:4, :], BB[0:4, :], E[0:4, :]
            dve(v.tensor_scalar(x, x, vec("gdn_dt_bias_2", parts=4), None, ALU.add))
            softplus(x, t1, t2, t3)
            wait("act", g.latest["dve"])
            act(s.activation(SM[0:4, 0:1], vec("gdn_a_log_2", parts=4), ACT.Exp))
            t = act(s.activation(SL[32:36, :], SL[32:36, :], ACT.Sigmoid))
            yield
            wait("dve", t)
            dve(v.tensor_scalar(x, x, SM[0:4, 0:1], -1.0, ALU.mult, ALU.mult))
            dve(v.tensor_tensor_scan(t1, con("reset", p1=4), x, 0.0, ALU.mult, ALU.add))
            dve(v.tensor_copy(x, t1))
            for p in range(2):
                q, k, val = PJ[:, p, :], PJ[:, 2 + p, :], PJ[:, 4 + p, :]
                wait("pe", g.latest["dve"], g.latest["act"])
                mm(bank[0][:, :], con("sela", p * P, P, 0, 4), SL[0:4, :])
                t = pe(mm(bank[1][:, :], con("selb", p * P, P, 32, 36), SL[32:36, :]))
                yield
                wait("dve", t)
                dve(v.tensor_copy(B, bank[0][:, :]))
                dve(v.tensor_copy(BB, bank[1][:, :]))
                dve(v.tensor_tensor(fm3(E, NCH), fm3(B, NCH), con("i64").unsqueeze(1).broadcast_to([P, NCH, CH]), ALU.mult))
                dve(v.tensor_reduce(bc, fm3(E, NCH), AXX, ALU.add))
                dve(v.tensor_tensor(fm3(DD, NCH), fm3(B, NCH), bc.unsqueeze(2).broadcast_to([P, NCH, CH]), ALU.subtract))
                dve(v.tensor_scalar(DD, DD, 0.0, None, ALU.min))
                dve(v.tensor_tensor(fm3(E, NCH), last_of_chunk(B), fm3(B, NCH), ALU.subtract))
                wait("act", g.latest["dve"])
                act(s.activation(DD, DD, ACT.Exp))
                act(s.activation(E, E, ACT.Exp))
                t = act(s.activation(B, B, ACT.Exp))
                yield
                wait("dve", t)
                dve(v.tensor_copy(lam[:, p, :], fm3(B, NCH)[:, :, CH - 1]))
                dve(v.tensor_tensor(QT[:, p, :], q, B, ALU.mult))
                dve(v.scalar_tensor_tensor(out=TIL[:, p, :], in0=k, scalar=-1.0, in1=B, op0=ALU.mult, op1=ALU.mult))
                dve(v.tensor_tensor(TIL[:, p, :], TIL[:, p, :], BB, ALU.mult))
                dve(v.tensor_tensor(E, E, k, ALU.mult))
                yield from to_rows(2, E, KH[:, p, :])
                dve(v.tensor_tensor(val, val, BB, ALU.mult))
                yield from to_rows(1, val, BV[:, p, :])
                ps = yield from tile_products(0, k, k)
                dve(v.tensor_tensor(E, ps, DD, ALU.mult))
                dve(v.scalar_tensor_tensor(out=E, in0=E, scalar=-1.0, in1=BB, op0=ALU.mult, op1=ALU.mult))
                masked(AT[:, p, :], E, con("strict"))
                ps = yield from tile_products(1, k, q)
                dve(v.tensor_tensor(E, ps, DD, ALU.mult))
                masked(AQ[:, p, :], E, con("incl"))

        def gdn_finish():
            B, E = PJ[:, 8, :], PJ[:, 9, :]
            for p in range(2):
                dve(v.tensor_tensor(B, YS[:, p, :], YS[:, p, :], ALU.mult))
                ps = yield from head_sums(B, 0)
                yield from root(ps, 1.0 / HD, EPS, E)
                dve(v.scalar_tensor_tensor(out=YS[:, p, :], in0=YS[:, p, :], scalar=vec("gdn_norm_2"), in1=E,
                                           op0=ALU.mult, op1=ALU.mult))
                dve(v.tensor_tensor(YS[:, p, :], YS[:, p, :], PJ[:, GZ + p, :], ALU.mult))

        def rwkv_prepare(AT, TIL, QT, AQ, KH, AAK, ARK, VV, KV, lam, up, t_up, z3):
            lw, L, aa, kk, e = PJ[:, 12, :], PJ[:, 13, :], g.rowtile[:, :], z3[:, :], R[:, :]
            for k in range(7):
                x = PJ[:, RK + k, :]
                dve(v.tensor_tensor(lw[:, 1:T], x[:, 0:T - 1], x[:, 1:T], ALU.subtract))
                dve(v.tensor_scalar(lw[:, 0:1], x[:, 0:1], -1.0, None, ALU.mult))
                dve(v.scalar_tensor_tensor(out=x, in0=lw, scalar=vec("rw_mu_2", k), in1=x, op0=ALU.mult, op1=ALU.add))
                yield
            wa = PJ[:, RK + 6, :]
            wait("act", g.latest["dve"])
            act(s.activation(wa[0:64, :], wa[0:64, :], ACT.Tanh))
            for p in range(2):
                r, k, val = PJ[:, RK + p, :], PJ[:, RK + 2 + p, :], PJ[:, RK + 4 + p, :]
                wait("pe", g.latest["act"], g.latest["dve"], t_up)
                mm(bank[4][:, :], up[0:64, p * P:(p + 1) * P], wa[0:64, :])
                t = pe(mm(bank[5][:, :], up[64:128, p * P:(p + 1) * P], wa[64:128, :]))
                yield
                wait("act", t)
                act(s.activation(lw, bank[4][:, :], ACT.Sigmoid, bias=vec("rw_w0_2", p)))
                t = act(s.activation(aa, bank[5][:, :], ACT.Sigmoid, bias=vec("rw_a0_2", p)))
                yield
                wait("dve", t)
                dve(v.tensor_scalar(lw, lw, -math.exp(-0.5), None, ALU.mult))
                dve(v.tensor_tensor_scan(L, con("reset"), lw, 0.0, ALU.mult, ALU.add))
                dve(v.tensor_scalar(kk, k, vec("rw_k_k_2", p), None, ALU.mult))
                dve(v.tensor_tensor(e, kk, kk, ALU.mult))
                ps = yield from head_sums(e, 6)
                yield from root(ps, 1.0, 1e-6, e)
                dve(v.tensor_tensor(kk, kk, e, ALU.mult))
                dve(v.tensor_scalar(e, aa, 1.0, vec("rw_k_a_2", p), ALU.subtract, ALU.mult))
                dve(v.scalar_tensor_tensor(out=k, in0=e, scalar=1.0, in1=k, op0=ALU.add, op1=ALU.mult))
                dve(v.tensor_tensor(aa, aa, kk, ALU.mult))
                dve(v.scalar_tensor_tensor(out=e, in0=r, scalar=vec("rw_r_k_2", p), in1=k, op0=ALU.mult, op1=ALU.mult))
                ps = yield from head_sums(e, 4)
                dve(v.tensor_tensor(YS[:, 6 + p, :], ps, val, ALU.mult))
                dve(v.tensor_tensor(lw, L, lw, ALU.subtract))
                wait("act", g.latest["dve"])
                act(s.activation(lw, lw, ACT.Exp))
                t = act(s.activation(e, L, ACT.Exp))
                yield
                wait("dve", t)
                dve(v.scalar_tensor_tensor(out=TIL[:, 2 + p, :], in0=kk, scalar=-1.0, in1=lw, op0=ALU.mult, op1=ALU.mult))
                dve(v.tensor_tensor(QT[:, 2 + p, :], r, e, ALU.mult))
                dve(v.tensor_copy(lam[:, 2 + p, :], fm3(e, NCH)[:, :, CH - 1]))
                dve(v.tensor_tensor(fm3(lw, NCH), last_of_chunk(L), fm3(L, NCH), ALU.subtract))
                wait("act", g.latest["dve"])
                act(s.activation(lw, lw, ACT.Exp))
                t = act(s.activation(L, L, ACT.Exp, scale=-1.0))
                yield
                wait("dve", t)
                dve(v.tensor_tensor(e, aa, lw, ALU.mult))
                t_e = yield from to_rows(4, e, KH[:, 2 + p, :])
                dve(v.tensor_tensor(kk, k, lw, ALU.mult))
                yield from to_rows(5, kk, KV[:, p, :])
                yield from to_rows(6, val, VV[:, p, :])
                dve(v.tensor_tensor(aa, aa, L, ALU.mult))
                dve(v.tensor_tensor(k, k, L, ALU.mult))
                masked(AT[:, 2 + p, :], (yield from tile_products(5, aa, TIL[:, 2 + p, :])), con("strict"))
                masked(AAK[:, p, :], (yield from tile_products(6, k, TIL[:, 2 + p, :])), con("strict"))
                masked(AQ[:, 2 + p, :], (yield from tile_products(4, aa, QT[:, 2 + p, :])), con("incl"))
                masked(ARK[:, p, :], (yield from tile_products(5, k, QT[:, 2 + p, :])), con("incl"))

        def rwkv_finish():
            for p in range(2):
                y = YS[:, 4 + p, :]
                yield from head_norm(y, 64e-5, PJ[:, 12, :], R[:, :], 4)
                dve(v.tensor_scalar(y, y, vec("rw_gn_gain_2", p), vec("rw_gn_bias_2", p), ALU.mult, ALU.add))
                dve(v.tensor_tensor(y, y, YS[:, 6 + p, :], ALU.add))
                dve(v.tensor_tensor(y, y, PJ[:, RZ + p, :], ALU.mult))

        def spatial():
            with ExitStack() as st:
                ws = g.sb(st, "sg_w", [P, 4, P])
                bs = g.sb(st, "sg_b", [1, 4, P])
                vt = g.sb(st, "sg_v", [P, 4, 256])
                tmp = g.sb(st, "sg_tmp", [P, T])
                g.fence()
                t1 = g.load(ws[:, :, :], a["sg_w"].rearrange("p (g t) -> p g t", g=4), "sgw")
                t2 = g.load(bs[:, :, :], a["sg_b"].rearrange("o (g t) -> o g t", g=4), "sgb")
                wait("dve", t1)
                wait("pe", t2)
                dve(v.tensor_tensor(ws[:, :, :], ws[:, :, :], con("tril").unsqueeze(1).broadcast_to([P, 4, P]), ALU.mult))
                for k in range(2):
                    act(s.activation(PJ[:, SU + k, :], PJ[:, SU + k, :], ACT.Gelu_apprx_tanh))
                    act(s.activation(PJ[:, SV + k, :], PJ[:, SV + k, :], ACT.Gelu_apprx_tanh))
                wait("dve", g.latest["act"])
                for z in (SZ, GZ, RZ, NZ):
                    act(s.activation(PJ[:, z:z + 2, :], PJ[:, z:z + 2, :], ACT.Silu))
                t_z = g.latest["act"]
                for k in range(2):
                    x = PJ[:, SV + k, :]
                    weave(head_norm(x, 1e-5, tmp[:, :], R[:, :], 0))
                    dve(v.tensor_scalar(x, x, vec("sg_ln_gain_2", k), vec("sg_ln_bias_2", k), ALU.mult, ALU.add))
                wait("pe", g.latest["dve"])
                for n in range(NT):
                    for k in range(2):
                        ins = tn.transpose(bank[1 + n % 2][:, k * P:(k + 1) * P], PJ[:, SV + k, n * P:(n + 1) * P], ident)
                    t = pe(ins)
                    wait("dve", t)
                    dve(v.tensor_copy(vt[:, n, :], bank[1 + n % 2][:, 0:256]))
                    g.spare()
                    wait("pe", g.latest["dve"])
                for k in range(2):
                    b = bank[4 + k]
                    for n in range(NT):
                        for j, r in enumerate(halves):
                            o = b[r, n * P:(n + 1) * P]
                            mm(o, vt[:, n, (2 * k + j) * 64:(2 * k + j + 1) * 64], ws[:, 2 * k + j, :], True, False)
                            ins = mm(o, con("ones", 0, 64, 0, 1), bs[:, 2 * k + j, :], False, True)
                    t = pe(tn.matmul(bank[6][0:32, 0:32], ident[:, 0:32], ident[:, 0:32], start=True, stop=True))
                    wait("dve", t)
                    wait("dve", t_z)
                    y = YS[:, 2 + k, :]
                    dve(v.tensor_tensor(y, PJ[:, SU + k, :], b[:, :], ALU.mult))
                    dve(v.tensor_tensor(y, y, PJ[:, SZ + k, :], ALU.mult))
                g.fence()

        def attention():
            NS, NSTREAM = 512 + 384 + 32, 4
            with ExitStack() as st:
                ks = g.sb(st, "ks", [P, T])
                kw = g.sb(st, "kw", [P, T])
                kc = g.sb(st, "kc", [P, 32])
                vs = g.sb(st, "vs", [P, NT, 2, HD])
                vc = g.sb(st, "vc", [32, HD])
                gt = g.sb(st, "gates", [P, NT, 12])
                cw = g.sb(st, "cmp_w1", [P, 32, HD])
                cw2 = g.sb(st, "cmp_w2", [P, HD])
                cp = g.sb(st, "cmp_pos", [P, 32])
                xc = g.sb(st, "cmp_x", [P, 32, NCMP])
                hc = g.sb(st, "cmp_h", [P, 32])
                nb = g.sb(st, "cmp_fill", [P, 4, 32])
                ps_ = g.sb(st, "scores", [P, NSTREAM, NS])
                pt = g.sb(st, "scores_t", [P, NSTREAM, 8 * P])
                ms = g.sb(st, "softmax", [P, NSTREAM, 6])
                g.fence()
                t_load = [g.load(cw[:, :, :], a["cmp_w1"].rearrange("p (j h) -> p j h", j=32), "cw1"),
                     g.load(cw2[:, :], a["cmp_w2"], "cw2"), g.load(cp[:, :], a["cmp_pos"], "cpos")]
                cm = con("cmask").rearrange("p (q n) -> p q n", q=4)
                cd = con("cdist").rearrange("p (q n) -> p q n", q=4)

                def keys_and_values():
                    KC_, KS_, KW_ = (PJ[:, NKV + i, :] for i in range(3))
                    for dst, src in ((ks, KS_), (kw, KW_)):
                        dve(v.tensor_copy(dst[0:64, :], src[0:64, :]))
                        dve(v.tensor_copy(dst[64:128, :], src[0:64, :]))
                    for k in range(2):
                        dve(v.tensor_scalar(PJ[:, NQ + k, :], PJ[:, NQ + k, :], HD ** -0.5, None, ALU.mult))
                    t_s = act(s.activation(SL[64:96, :], SL[64:96, :], ACT.Sigmoid))
                    yield
                    wait("pe", t_s, g.latest["dve"])
                    bb = [bank[b] for b in (1, 2, 5, 6)]
                    for n in range(NT):
                        for q, src in enumerate((KS_, KW_)):
                            tn.transpose(bb[n][:, q * P:(q + 1) * P], src[:, n * P:(n + 1) * P], ident)
                        ins = tn.transpose(bb[n][:, 256:352], SL[:, n * P:(n + 1) * P], ident[0:96, 0:96])
                    t = pe(ins)
                    yield
                    wait("dve", t)
                    for n in range(NT):
                        dve(v.tensor_copy(vs[:, n, :, :], bb[n][:, 0:256].rearrange("p (q c) -> p q c", q=2)[:, :, 64:128]))
                        src = bb[n][:, 320:332].rearrange("p (h b) -> p h b", b=3)
                        dst = gt[:, n, :].rearrange("p (h b) -> p h b", b=3)
                        dve(v.tensor_copy(dst[:, :, 0:2], src[:, :, 1:3]))
                        dve(v.tensor_copy(dst[:, :, 2:3], src[:, :, 0:1]))
                        yield
                    wait("dve", *t_load)
                    for h in range(2):
                        src = KC_[:, 16 * h:16 * h + 16 * NCMP].rearrange("p (n j) -> p j n", j=16)
                        t = dve(v.tensor_tensor(xc[:, 16 * h:16 * h + 16, :], src,
                                                cp[:, 16 * h:16 * h + 16].unsqueeze(2).broadcast_to([P, 16, NCMP]), ALU.add))
                    yield
                    wait("pe", t, *t_load)
                    for j in range(32):
                        for r in halves:
                            ins = mm(bank[1][r, 0:NCMP], cw[r, j, :], xc[r, j, :], j == 0, j == 31)
                    t = pe(ins)
                    yield
                    wait("act", t)
                    t = act(s.activation(hc[:, 0:NCMP], bank[1][:, 0:NCMP], ACT.Gelu_apprx_tanh))
                    yield
                    wait("pe", t)
                    for r in halves:
                        mm(bank[2][r, 0:NCMP], cw2[0:64, :], hc[0:64, 0:NCMP])
                    t = pe(mm(bank[5][0:NCMP, 0:HD], hc[64:128, 0:NCMP], cw2[64:128, :]))
                    yield
                    wait("dve", t)
                    dve(v.tensor_copy(kc[:, 0:NCMP], bank[2][:, 0:NCMP]))
                    dve(v.tensor_copy(vc[0:NCMP, :], bank[5][0:NCMP, 0:HD]))
                    dve(v.tensor_scalar(nb[:, :, :], cm, BIG, -BIG, ALU.mult, ALU.add))

                weave(keys_and_values(), gdn_finish(), rwkv_finish())
                for _ in g.background:
                    pass
                g.background = None
                g.fence()
                free = [None] * NSTREAM

                def head(u, c, h):
                    n1, n2 = c + 1, min(c + 1, 3)
                    b0, b1 = bank[u], bank[4 + u]
                    sc, nmax, tot = ps_[:, u, :], ms[:, u, 0:3], ms[:, u, 3:6]
                    r, cols = halves[h % 2], slice(c * P, (c + 1) * P)
                    q = PJ[r, NQ + h // 2, cols]
                    wait("pe", free[u])
                    mm(b0[:, 0:n1 * P], q, ks[r, 0:n1 * P])
                    mm(b1[:, 0:n2 * P], q, kw[r, (c + 1 - n2) * P:(c + 1) * P])
                    t = pe(mm(b1[:, 384:384 + NCMP], q, kc[r, 0:NCMP]))
                    yield
                    wait("dve", t)
                    spans = [(0, n1 * P), (512, 512 + n2 * P), (896, 896 + NCMP)]
                    dve(v.scalar_tensor_tensor(out=sc[:, 0:n1 * P], in0=con("dist", 384 - P * c), scalar=-SLOPES[h],
                                               in1=b0[:, 0:n1 * P], op0=ALU.mult, op1=ALU.add))
                    dve(v.scalar_tensor_tensor(out=sc[:, 512:512 + n2 * P], in0=con("distw", 384 - P * n2), scalar=-SLOPES[h],
                                               in1=b1[:, 0:n2 * P], op0=ALU.mult, op1=ALU.add))
                    x = sc[:, 896:896 + NCMP]
                    dve(v.scalar_tensor_tensor(out=x, in0=cd[:, c, 0:NCMP], scalar=-SLOPES[h],
                                               in1=b1[:, 384:384 + NCMP], op0=ALU.mult, op1=ALU.add))
                    dve(v.tensor_tensor(x, x, cm[:, c, 0:NCMP], ALU.mult))
                    dve(v.tensor_tensor(x, x, nb[:, c, 0:NCMP], ALU.add))
                    for b, (lo, hi) in enumerate(spans):
                        t = dve(v.tensor_reduce(nmax[:, b:b + 1], sc[:, lo:hi], AXX, ALU.max, negate=True))
                    wait("act", t)
                    for b, (lo, hi) in enumerate(spans):
                        t = act(s.activation(sc[:, lo:hi], sc[:, lo:hi], ACT.Exp, bias=nmax[:, b:b + 1], accum_out=tot[:, b:b + 1]))
                    yield
                    wait("dve", t)
                    dve(v.reciprocal(tot, tot))
                    dve(v.tensor_tensor(tot, tot, gt[:, c, 3 * h:3 * h + 3], ALU.mult))
                    for b, (lo, hi) in enumerate(spans):
                        dve(v.tensor_scalar(sc[:, lo:hi], sc[:, lo:hi], tot[:, b:b + 1], None, ALU.mult))
                    t = dve(v.tensor_tensor(x, x, cm[:, c, 0:NCMP], ALU.mult))
                    yield
                    wait("pe", t)
                    blocks = [(j * P, P, vs[:, j, 0, :]) for j in range(n1)]
                    blocks += [(512 + j * P, P, vs[:, c + 1 - n2 + j, 1, :]) for j in range(n2)]
                    blocks += [(896, NCMP, vc[0:NCMP, :])]
                    bb = [b0, b1]
                    for j, (o, w, _) in enumerate(blocks):
                        ins = tn.transpose(bb[j // 4][0:w, (j % 4) * P:(j % 4 + 1) * P], sc[:, o:o + w], ident)
                    t = pe(ins)
                    yield
                    wait("act", t)
                    nbk = len(blocks)
                    for j in range(0, nbk - 1, 4):
                        m = min(4, nbk - 1 - j)
                        act(s.copy(pt[:, u, j * P:(j + m) * P], bb[j // 4][:, 0:m * P]))
                    j = nbk - 1
                    t = act(s.copy(pt[0:NCMP, u, j * P:(j + 1) * P], bb[j // 4][0:NCMP, (j % 4) * P:(j % 4 + 1) * P]))
                    yield
                    wait("pe", t)
                    for j, (o, w, val) in enumerate(blocks):
                        ins = mm(b0[r, 0:P], val, pt[0:w, u, j * P:(j + 1) * P], j == 0, j == nbk - 1)
                    t = pe(ins)
                    yield
                    wait("dve", t)
                    free[u] = dve(v.tensor_tensor(YS[r, 6 + h // 2, cols], b0[r, 0:P], PJ[r, NZ + h // 2, cols], ALU.mult))

                def stream(u):
                    for i in range(u, 4 * NT, NSTREAM):
                        yield from head(u, i // 4, i % 4)

                weave(*(stream(u) for u in range(NSTREAM)))
                g.fence()

        def merge_gates():
            order = [NPROJ + 8 * q + m for m in range(KD) for q in range(4)]
            w, free, left = [None] * 2, [None] * 2, [None] * 2
            src = wblock("w_in_2")
            for u in range(2):
                wait("sp", g.latest["pe"])
                w[u] = g.load(W[:, u, :, :], src(order[u]), f"w{u}")

            def empty(j, t):
                u = j % 2
                wait("act", t, left[u])
                free[u] = act(s.activation(SQ[:, u, :], bank[(3, 7)[u]][:, :], ACT.Sigmoid))
                left[u] = g.load(a["gates"][j], SQ[:, u, :], f"gate{u}", "act")
                stores[u] = left[u]

            pending = None
            for j, i in enumerate(order):
                u = j % 2
                wait("pe", w[u], free[u])
                for k in range(KD):
                    ins = mm(bank[(3, 7)[u]][:, :], W[:, u, k, :], H[:, k, :], k == 0, k == KD - 1)
                    if k == 1 and pending:
                        empty(*pending)
                    if k % 2 and k < KD - 1:
                        yield
                t = pe(ins)
                pending = (j, t)
                if j + 2 < len(order):
                    wait("sp", t)
                    w[u] = g.load(W[:, u, :, :], src(order[j + 2]), f"w{u}")
                if g.resting:
                    empty(*pending)
                    pending = None
                    yield "idle"
                else:
                    yield
            if pending:
                empty(*pending)

        stores = [None, None]
        g.background = merge_gates()
        spatial()
        deltas()
        attention()
        with ExitStack() as st:
            mix = PJ[:, 0:KD, :]
            wm = g.sb(st, "merge_w", [P, 2, KD, P])
            sg = g.sb(st, "merge_g", [P, 2, 4, T])
            g.fence()
            wait("sp", *stores)
            with book.run(KD // 2) as i:
                cpe, cdve = g.cnt["pe"], g.cnt["dve"]
                for u in range(2):
                    m = i * 2 + u
                    wait("sp", book.before(f"mw{u}", cpe))
                    t_w = g.load(wm[:, u, :, :], wblock("w_branch")(m), f"merge_w{u}")
                    wait("sp", book.before(f"ms{u}", cdve))
                    t_g = g.load(sg[:, u, :, :], a["gates"][bass.ds(m * 4, 4), :, :].rearrange("q p t -> p q t"), f"merge_g{u}")
                    wait("pe", t_w, book.before(f"ms{u}", cdve))
                    t_y = []
                    for q in range(4):
                        for k in range(2):
                            ins = mm(bank[4 * u + q][:, :], wm[:, u, 2 * q + k, :], YS[:, 2 * q + k, :], k == 0, k == 1)
                        t_y.append(pe(ins))
                    book.name(f"mw{u}", t_y[-1])
                    wait("dve", t_g)
                    row = mix[:, bass.ds(m, 1), :].rearrange("p o t -> p (o t)")
                    for q in range(4):
                        wait("dve", t_y[q])
                        if q == 0:
                            t = dve(v.tensor_tensor(row, sg[:, u, 0, :], bank[4 * u][:, :], ALU.mult))
                        else:
                            dve(v.tensor_tensor(sg[:, u, q, :], sg[:, u, q, :], bank[4 * u + q][:, :], ALU.mult))
                            t = dve(v.tensor_tensor(row, row, sg[:, u, q, :], ALU.add))
                    book.name(f"ms{u}", t)
            g.settle()
            g.fence()

            def ev_out(i, ps, e):
                xi = X[:, bass.ds(i, 1), :].rearrange("p o t -> p (o t)")
                return dve(v.tensor_tensor(xi, ps, xi, ALU.add))

            project(KD, wblock("w_out_2"), lambda k: mix[:, k, :], T, ev_out)


def columns(x):
    return np.ascontiguousarray(x).reshape(-1, P).T


def weight_blocks(w):
    k, n = w.shape
    return np.ascontiguousarray(w.reshape(k // P, P, n // P, P).transpose(2, 1, 0, 3).reshape(n // P, P, -1))


def feature_major(x):
    t, d = x.shape
    return np.ascontiguousarray(x.T.reshape(d // P, P, t).transpose(1, 0, 2).reshape(P, -1))


def arrange(inp):
    A = {k: np.asarray(x) for k, x in inp.items()}
    vecs = np.zeros((P, NVEC), np.float32)
    for name, w in VEC:
        o = VOFF[name]
        if name in ("filt_freq0", "filt_freq1"):
            vecs[:FHID, o] = A["filt_freq"][0, int(name[-1])]
        elif name in ("filt_b1", "filt_b2"):
            vecs[:FHID, o] = A[name][0]
        elif name in ("gdn_a_log_2", "gdn_dt_bias_2"):
            vecs[:4, o] = A[name][0]
        elif name == "gdn_norm_2":
            vecs[:64, o] = A[name][0]
            vecs[64:, o] = A[name][0]
        else:
            vecs[:, o:o + w] = columns(A[name])
    f = {"vecs": vecs, "consts": shape_constants()}
    f["dft"], f["idft"], f["filt_z"], f["window"] = dft_constants()
    f["x_fm"] = feature_major(A["x"][0])
    f["ctx_fm"] = feature_major(A["ctx"][0])
    f["w_mod"] = A["w_mod"]
    f["w_in"] = weight_blocks(A["w_in"][0])
    lw = np.stack([A["lru_wr"][0], A["lru_wi"][0]], 2).reshape(2, 4, 2, 2, 64, 64)
    f["lru_w"] = np.ascontiguousarray(lw.transpose(2, 4, 0, 1, 3, 5).reshape(2, 64, 16, 64))
    f["filt_w1"], f["filt_w2"], f["filt_w3"], f["filt_b3"] = (A["filt_w1"][0], A["filt_w2"][0], A["filt_w3"][0],
                                                             A["filt_b3"][0:1])
    for n in ("w_out", "cf_w1", "cf_w2", "w_out_2"):
        f[n] = weight_blocks(A[n][0])
    f["router"] = np.ascontiguousarray(A["router"].reshape(2, KD, P, NE).transpose(0, 2, 1, 3).reshape(2, P, -1))
    for n in ("exp_w1", "exp_w3", "exp_w2"):
        f[n] = A[n]
    w2 = A["w_in_2"][0]
    cols = np.r_[0:768, 776:3592, 3604:7956]
    f["w_in_2"] = weight_blocks(w2[:, cols])
    small = np.zeros((D, 96), np.float32)
    small[:, 0:4], small[:, 32:36], small[:, 64:76] = w2[:, 768:772], w2[:, 772:776], w2[:, 3592:3604]
    f["w_small"] = np.ascontiguousarray(small.reshape(KD, P, 96).transpose(1, 0, 2).reshape(P, -1))
    f["rw_up"] = np.concatenate([A["rw_w_up_2"][0], A["rw_a_up_2"][0]], 0)
    f["sg_w"] = np.ascontiguousarray(A["sg_w_s_2"][0].transpose(2, 0, 1).reshape(P, -1))
    f["sg_b"] = A["sg_b_s_2"][0].reshape(1, -1)
    f["cmp_w1"] = np.ascontiguousarray(A["nsa_cmp_w1_2"][0].reshape(2, 32, 64, 64).transpose(0, 2, 1, 3).reshape(P, -1))
    f["cmp_w2"] = A["nsa_cmp_w2_2"][0].reshape(P, 64)
    f["cmp_pos"] = np.ascontiguousarray(A["nsa_cmp_pos_2"][0].transpose(0, 2, 1).reshape(P, 32))
    f["w_branch"] = weight_blocks(A["w_branch_2"][0].reshape(D, D))
    return {k: np.ascontiguousarray(x) for k, x in f.items()}


def program(make, shapes):
    plan = {}
    for _ in range(2):
        nc = make()
        a = {n: nc.dram_tensor("in_" + n, shape, F32, kind="ExternalInput").ap() for n, shape in shapes.items()}
        a["gates"] = nc.dram_tensor("merge_gates", (4 * KD, P, T), F32, kind="Internal").ap()
        a["out"] = nc.dram_tensor("out_0", (P, KD * T), F32, kind="ExternalOutput").ap()
        plan, before = build(nc, a, plan), plan
    assert plan == before
    return nc


def kernel(**inputs):
    import concourse.bacc as bacc
    from concourse.bass_utils import run_bass_kernel_spmd

    f = arrange(inputs)
    nc = program(lambda: bacc.Bacc("TRN2", target_bir_lowering=False, num_devices=1), {n: x.shape for n, x in f.items()})
    r = run_bass_kernel_spmd(nc, [{"in_" + n: x for n, x in f.items()}], core_ids=[0])
    out = r.results[0]["out_0"].reshape(P, KD, T)
    return np.ascontiguousarray(out.transpose(2, 1, 0).reshape(1, T, D))
```
